# Optimizing a Trainium2 kernel written in Bass

```python
import math
import jax, jax.numpy as jnp
from jax import lax
import numpy as np

D_MODEL = 1024
BATCH = 1
SEQ = 512
DEPTH = 2

HEAD_DIM = 64
N_HEADS = 16
D_MIX = N_HEADS * HEAD_DIM
N_HEADS_A = 8
N_KV_A = 2
WINDOW = 128
N_HEADS_B = 4
MOBA_BLOCK = 256
MOBA_TOPK = 3
N_HEADS_C = 4
C_KV_LATENT = 128
N_IDX_HEADS = 4
IDX_DIM = 64
DSA_TOPK = 256
D_FF = 2816
N_BUCKETS = 32
MAX_DISTANCE = 128
RMS_EPS = 1e-6
Q_BLOCK = 128

A_Q = N_HEADS_A * HEAD_DIM
A_KV = N_KV_A * HEAD_DIM
B_QKV = N_HEADS_B * HEAD_DIM
C_Q = N_HEADS_C * HEAD_DIM
C_QIDX = N_IDX_HEADS * IDX_DIM
COL_SIZES = (A_Q, A_KV, A_KV, B_QKV, B_QKV, B_QKV, C_Q, C_KV_LATENT, C_QIDX, IDX_DIM, N_IDX_HEADS)
D_IN = A_Q + 2 * A_KV + 3 * B_QKV + C_Q + C_KV_LATENT + C_QIDX + IDX_DIM + N_IDX_HEADS


def _rmsnorm(x, g):
    x32 = x.astype(jnp.float32)
    y = x32 * lax.rsqrt(jnp.mean(x32 * x32, axis=-1, keepdims=True) + RMS_EPS)
    return (y * g.astype(jnp.float32)).astype(x.dtype)

def _swiglu(x, w_gate, w_up, w_down):
    return (jax.nn.silu(x @ w_gate) * (x @ w_up)) @ w_down

def _t5_bucket(dist):
    n = jnp.maximum(dist, 0)
    max_exact = N_BUCKETS // 2
    nf = jnp.maximum(n, 1).astype(jnp.float32)
    large = max_exact + (jnp.log(nf / max_exact) / math.log(MAX_DISTANCE / max_exact)
                         * (N_BUCKETS - max_exact)).astype(jnp.int32)
    large = jnp.minimum(large, N_BUCKETS - 1)
    return jnp.where(n < max_exact, n, large)

def _split_cols(p):
    cuts = []
    acc = 0
    for sz in COL_SIZES[:-1]:
        acc += sz
        cuts.append(acc)
    return jnp.split(p, cuts, axis=-1)

def _sliding_window_attn(q, k, v, sinks, bias_tab):
    B, T = q.shape[0], q.shape[1]
    nq = T // Q_BLOCK
    G = N_HEADS_A // N_KV_A
    pad = ((0, 0), (WINDOW, 0), (0, 0), (0, 0))
    kp = jnp.pad(k, pad).reshape(B, nq + 1, Q_BLOCK, N_KV_A, HEAD_DIM)
    vp = jnp.pad(v, pad).reshape(B, nq + 1, Q_BLOCK, N_KV_A, HEAD_DIM)
    kb = jnp.concatenate([kp[:, :-1], kp[:, 1:]], axis=2)
    vb = jnp.concatenate([vp[:, :-1], vp[:, 1:]], axis=2)
    qb = q.reshape(B, nq, Q_BLOCK, N_KV_A, G, HEAD_DIM)
    s = jnp.einsum('bnqkgd,bnskd->bnkgqs', qb, kb).astype(jnp.float32) * (HEAD_DIM ** -0.5)
    qi = jnp.arange(Q_BLOCK)[:, None]
    si = jnp.arange(2 * Q_BLOCK)[None, :]
    dist = WINDOW + qi - si
    bias = bias_tab[:, _t5_bucket(dist)].astype(jnp.float32)
    bias = bias.reshape(N_KV_A, G, Q_BLOCK, 2 * Q_BLOCK)
    key_pos = jnp.arange(nq)[:, None] * Q_BLOCK - WINDOW + si
    valid = ((dist >= 0) & (dist < WINDOW))[None] & (key_pos >= 0)[:, None, :]
    s = jnp.where(valid[None, :, None, None], s + bias, -jnp.inf)
    sink = sinks.astype(jnp.float32).reshape(N_KV_A, G)[None, None, :, :, None, None]
    m = jnp.maximum(jnp.max(s, axis=-1, keepdims=True), sink)
    p = jnp.exp(s - m)
    denom = jnp.sum(p, axis=-1, keepdims=True) + jnp.exp(sink - m)
    o = jnp.einsum('bnkgqs,bnskd->bnqkgd', (p / denom).astype(v.dtype), vb)
    return o.reshape(B, T, N_HEADS_A * HEAD_DIM)

def _moba_attn(q, k, v, bias_tab):
    B, T = q.shape[0], q.shape[1]
    nb = -(-T // MOBA_BLOCK)
    Tp = nb * MOBA_BLOCK
    pad = ((0, 0), (0, Tp - T), (0, 0), (0, 0))
    kbh = jnp.pad(k, pad).reshape(B, nb, MOBA_BLOCK, N_HEADS_B, HEAD_DIM).transpose(0, 3, 1, 2, 4)
    vbh = jnp.pad(v, pad).reshape(B, nb, MOBA_BLOCK, N_HEADS_B, HEAD_DIM).transpose(0, 3, 1, 2, 4)
    n_sel = min(MOBA_TOPK, nb - 1)
    scale = HEAD_DIM ** -0.5
    h_idx = jnp.arange(N_HEADS_B)[None, :, None, None]
    b_idx = jnp.arange(B)[:, None, None, None]
    if n_sel > 0:
        k_mean = jnp.mean(kbh.astype(jnp.float32), axis=3)
        gate = jnp.einsum('bthd,bhnd->bhtn', q.astype(jnp.float32), k_mean)
        own_all = jnp.arange(T) // MOBA_BLOCK
        past = jnp.arange(nb)[None, :] < own_all[:, None]
        gate = jnp.where(past[None, None], gate, -jnp.inf)
        _, sel_idx = lax.top_k(gate, n_sel)

    def chunk(i):
        t0 = i * Q_BLOCK
        tq = t0 + jnp.arange(Q_BLOCK)
        qc = lax.dynamic_slice_in_dim(q, t0, Q_BLOCK, axis=1).transpose(0, 2, 1, 3)
        ob = t0 // MOBA_BLOCK
        k_own = lax.dynamic_index_in_dim(kbh, ob, axis=2, keepdims=False)
        v_own = lax.dynamic_index_in_dim(vbh, ob, axis=2, keepdims=False)
        d_own = tq[:, None] - (ob * MOBA_BLOCK + jnp.arange(MOBA_BLOCK))[None, :]
        s_own = (jnp.einsum('bhqd,bhsd->bhqs', qc, k_own).astype(jnp.float32) * scale
                 + bias_tab[:, _t5_bucket(d_own)].astype(jnp.float32)[None])
        s_own = jnp.where((d_own >= 0)[None, None], s_own, -jnp.inf)
        if n_sel == 0:
            p_own = jax.nn.softmax(s_own, axis=-1)
            o = jnp.einsum('bhqs,bhsd->bhqd', p_own.astype(v.dtype), v_own)
            return o.transpose(0, 2, 1, 3)
        idx_c = lax.dynamic_slice_in_dim(sel_idx, t0, Q_BLOCK, axis=2)
        k_sel = kbh[b_idx, h_idx, idx_c]
        v_sel = vbh[b_idx, h_idx, idx_c]
        sel_pos = idx_c[..., None] * MOBA_BLOCK + jnp.arange(MOBA_BLOCK)
        d_sel = tq[None, None, :, None, None] - sel_pos
        b_sel = bias_tab[h_idx[..., None], _t5_bucket(d_sel)].astype(jnp.float32)
        s_sel = jnp.einsum('bhqd,bhqjsd->bhqjs', qc, k_sel).astype(jnp.float32) * scale + b_sel
        ok = (idx_c < (tq // MOBA_BLOCK)[None, None, :, None])[..., None]
        s_sel = jnp.where(ok, s_sel, -jnp.inf).reshape(B, N_HEADS_B, Q_BLOCK, n_sel * MOBA_BLOCK)
        p = jax.nn.softmax(jnp.concatenate([s_sel, s_own], axis=-1), axis=-1).astype(v.dtype)
        p_sel = p[..., :n_sel * MOBA_BLOCK].reshape(B, N_HEADS_B, Q_BLOCK, n_sel, MOBA_BLOCK)
        p_own = p[..., n_sel * MOBA_BLOCK:]
        o = (jnp.einsum('bhqjs,bhqjsd->bhqd', p_sel, v_sel)
             + jnp.einsum('bhqs,bhsd->bhqd', p_own, v_own))
        return o.transpose(0, 2, 1, 3)

    out = lax.map(chunk, jnp.arange(T // Q_BLOCK))
    return out.transpose(1, 0, 2, 3, 4).reshape(B, T, N_HEADS_B * HEAD_DIM)

def _dsa_attn(q, k, v, q_idx, k_idx, w_idx, bias_tab):
    B, T = q.shape[0], q.shape[1]
    n_keep = min(DSA_TOPK, T // 4)
    key_pos = jnp.arange(T)
    b_idx = jnp.arange(B)[:, None, None]
    scale = HEAD_DIM ** -0.5

    def chunk(i):
        t0 = i * Q_BLOCK
        tq = t0 + jnp.arange(Q_BLOCK)
        qi = lax.dynamic_slice_in_dim(q_idx, t0, Q_BLOCK, axis=1)
        wi = lax.dynamic_slice_in_dim(w_idx, t0, Q_BLOCK, axis=1).astype(jnp.float32)
        dots = jnp.einsum('bqhd,bsd->bqhs', qi, k_idx).astype(jnp.float32) * (IDX_DIM ** -0.5)
        score = jnp.einsum('bqhs,bqh->bqs', jax.nn.relu(dots), wi)
        score = jnp.where((key_pos[None, :] <= tq[:, None])[None], score, -jnp.inf)
        _, idx = lax.top_k(score, n_keep)
        k_sel = k[b_idx, idx]
        v_sel = v[b_idx, idx]
        qc = lax.dynamic_slice_in_dim(q, t0, Q_BLOCK, axis=1)
        d = tq[None, :, None] - idx
        bias = bias_tab[:, _t5_bucket(d)].astype(jnp.float32).transpose(1, 0, 2, 3)
        s = jnp.einsum('bqhd,bqkd->bhqk', qc, k_sel).astype(jnp.float32) * scale + bias
        s = jnp.where((d >= 0)[:, None], s, -jnp.inf)
        p = jax.nn.softmax(s, axis=-1).astype(v.dtype)
        return jnp.einsum('bhqk,bqkd->bqhd', p, v_sel)

    out = lax.map(chunk, jnp.arange(T // Q_BLOCK))
    return out.transpose(1, 0, 2, 3, 4).reshape(B, T, N_HEADS_C * HEAD_DIM)

def first_inputs(seed: int = 0) -> dict:
    key = jax.random.key(seed)
    ks = jax.random.split(key, 18)

    def nrm(k, shape, fan_in):
        return jax.random.normal(k, shape, jnp.float32) * (fan_in ** -0.5)

    def gain(k, shape):
        return 1.0 + 0.05 * jax.random.normal(k, shape, jnp.float32)

    return {
        "x": jax.random.normal(ks[0], (BATCH, SEQ, D_MODEL), jnp.float32),
        "rel_bias_table": 0.5 * jax.random.normal(ks[1], (N_BUCKETS, N_HEADS), jnp.float32),
        "ffn1_norm": gain(ks[2], (DEPTH, D_MODEL)),
        "ffn1_w_gate": nrm(ks[3], (DEPTH, D_MODEL, D_FF), D_MODEL),
        "ffn1_w_up": nrm(ks[4], (DEPTH, D_MODEL, D_FF), D_MODEL),
        "ffn1_w_down": nrm(ks[5], (DEPTH, D_FF, D_MODEL), D_FF),
        "mix_norm": gain(ks[6], (DEPTH, D_MODEL)),
        "w_in": nrm(ks[7], (DEPTH, D_MODEL, D_IN), D_MODEL),
        "attn_sinks": 0.5 * jax.random.normal(ks[8], (DEPTH, N_HEADS_A), jnp.float32),
        "kv_norm_c": gain(ks[9], (DEPTH, C_KV_LATENT)),
        "w_kv_up_c": nrm(ks[10], (DEPTH, C_KV_LATENT, 2 * HEAD_DIM), C_KV_LATENT),
        "w_out": nrm(ks[11], (DEPTH, D_MIX, D_MODEL), D_MIX),
        "ffn2_norm": gain(ks[12], (DEPTH, D_MODEL)),
        "ffn2_w_gate": nrm(ks[13], (DEPTH, D_MODEL, D_FF), D_MODEL),
        "ffn2_w_up": nrm(ks[14], (DEPTH, D_MODEL, D_FF), D_MODEL),
        "ffn2_w_down": nrm(ks[15], (DEPTH, D_FF, D_MODEL), D_FF),
        "final_norm": gain(ks[16], (D_MODEL,)),
    }

def first_block(x, rel_bias_table, ffn1_norm, ffn1_w_gate, ffn1_w_up, ffn1_w_down, mix_norm, w_in,
              attn_sinks, kv_norm_c, w_kv_up_c, w_out, ffn2_norm, ffn2_w_gate, ffn2_w_up,
              ffn2_w_down, final_norm):
    B, T = x.shape[0], x.shape[1]
    tab = rel_bias_table.T
    tab_a = tab[:N_HEADS_A]
    tab_b = tab[N_HEADS_A:N_HEADS_A + N_HEADS_B]
    tab_c = tab[N_HEADS_A + N_HEADS_B:]
    for l in range(DEPTH):
        x = x + 0.5 * _swiglu(_rmsnorm(x, ffn1_norm[l]), ffn1_w_gate[l], ffn1_w_up[l], ffn1_w_down[l])
        h = _rmsnorm(x, mix_norm[l])
        (qa, ka, va, qb, kb, vb, qc, ckv, qidx, kidx, widx) = _split_cols(h @ w_in[l])
        out_a = _sliding_window_attn(qa.reshape(B, T, N_HEADS_A, HEAD_DIM),
                                     ka.reshape(B, T, N_KV_A, HEAD_DIM),
                                     va.reshape(B, T, N_KV_A, HEAD_DIM),
                                     attn_sinks[l], tab_a)
        out_b = _moba_attn(qb.reshape(B, T, N_HEADS_B, HEAD_DIM),
                           kb.reshape(B, T, N_HEADS_B, HEAD_DIM),
                           vb.reshape(B, T, N_HEADS_B, HEAD_DIM), tab_b)
        kv_c = _rmsnorm(ckv, kv_norm_c[l]) @ w_kv_up_c[l]
        out_c = _dsa_attn(qc.reshape(B, T, N_HEADS_C, HEAD_DIM),
                          kv_c[..., :HEAD_DIM], kv_c[..., HEAD_DIM:],
                          qidx.reshape(B, T, N_IDX_HEADS, IDX_DIM), kidx,
                          widx * (N_IDX_HEADS ** -0.5), tab_c)
        x = x + jnp.concatenate([out_a, out_b, out_c], axis=-1) @ w_out[l]
        x = x + 0.5 * _swiglu(_rmsnorm(x, ffn2_norm[l]), ffn2_w_gate[l], ffn2_w_up[l], ffn2_w_down[l])
    return _rmsnorm(x, final_norm)


N_A_LAYERS = DEPTH // 2
N_B_LAYERS = DEPTH - N_A_LAYERS
A_HEADS = 8
A_HEAD_DIM = D_MODEL // A_HEADS // 2
B_HEADS = 16
B_HEAD_DIM = D_MODEL // B_HEADS
CONV_WIDTH = 3
SUBLN_EPS = 1e-5
NEG_INF = -1e30


def rms_norm(x, gain, eps=RMS_EPS):
    xf = x.astype(jnp.float32)
    y = xf * lax.rsqrt(jnp.mean(xf * xf, axis=-1, keepdims=True) + eps)
    return (y * gain.astype(jnp.float32)).astype(x.dtype)

def t5_bucket(dist):
    max_exact = N_BUCKETS // 2
    d = jnp.maximum(dist, 0)
    log_ratio = jnp.log(jnp.maximum(d, 1).astype(jnp.float32) / max_exact) / math.log(MAX_DISTANCE / max_exact)
    large = jnp.minimum(max_exact + (log_ratio * (N_BUCKETS - max_exact)).astype(jnp.int32), N_BUCKETS - 1)
    return jnp.where(d < max_exact, d, large)

def lambda_init_fn(layer_idx):
    return 0.8 - 0.6 * math.exp(-0.3 * layer_idx)

def diff_attention(x, w_qkv, w_o, lam_q1, lam_k1, lam_q2, lam_k2, subln_g, rel_bias, lambda_init):
    B, S, _ = x.shape
    qkv = x @ w_qkv
    nq = 2 * A_HEADS * A_HEAD_DIM
    q, k, v = jnp.split(qkv, [nq, 2 * nq], axis=-1)
    q = q.reshape(B, S, A_HEADS, 2, A_HEAD_DIM).astype(jnp.float32) * (A_HEAD_DIM ** -0.5)
    k = k.reshape(B, S, A_HEADS, 2, A_HEAD_DIM).astype(jnp.float32)
    v = v.reshape(B, S, A_HEADS, 2 * A_HEAD_DIM).astype(jnp.float32)
    lam = (jnp.exp(jnp.sum(lam_q1.astype(jnp.float32) * lam_k1.astype(jnp.float32)))
           - jnp.exp(jnp.sum(lam_q2.astype(jnp.float32) * lam_k2.astype(jnp.float32)))
           + lambda_init)
    outs = []
    for i in range(S // Q_BLOCK):
        q0 = i * Q_BLOCK
        k_end = q0 + Q_BLOCK
        dist = jnp.arange(q0, k_end)[:, None] - jnp.arange(k_end)[None, :]
        bias = jnp.moveaxis(rel_bias[t5_bucket(dist)].astype(jnp.float32), -1, 0)
        logits = jnp.einsum('bqhcd,bkhcd->bchqk', q[:, q0:k_end], k[:, :k_end]) + bias[None, None]
        logits = jnp.where(dist >= 0, logits, NEG_INF)
        p = jax.nn.softmax(logits, axis=-1)
        attn = p[:, 0] - lam * p[:, 1]
        outs.append(jnp.einsum('bhqk,bkhe->bqhe', attn, v[:, :k_end]))
    o = jnp.concatenate(outs, axis=1)
    o = rms_norm(o, subln_g, SUBLN_EPS) * (1.0 - lambda_init)
    return o.reshape(B, S, A_HEADS * 2 * A_HEAD_DIM).astype(x.dtype) @ w_o

def shared_kv(h, kv_norm, w_kvf, b_f):
    B, S, _ = h.shape
    kvf = rms_norm(h, kv_norm) @ w_kvf
    k, v, f_logit = jnp.split(kvf, [B_HEADS * B_HEAD_DIM, 2 * B_HEADS * B_HEAD_DIM], axis=-1)
    k = k.reshape(B, S, B_HEADS, B_HEAD_DIM).astype(jnp.float32)
    v = v.reshape(B, S, B_HEADS, B_HEAD_DIM).astype(jnp.float32)
    log_f = jax.nn.log_sigmoid(f_logit.astype(jnp.float32) + b_f.astype(jnp.float32))
    c = jnp.cumsum(log_f, axis=1)
    return k, v, jnp.transpose(c, (0, 2, 1))

def forgetting_attention(x, w_q, w_o, k, v, c):
    B, S, _ = x.shape
    q = (x @ w_q).reshape(B, S, B_HEADS, B_HEAD_DIM).astype(jnp.float32) * (B_HEAD_DIM ** -0.5)
    outs = []
    for i in range(S // Q_BLOCK):
        q0 = i * Q_BLOCK
        k_end = q0 + Q_BLOCK
        dist = jnp.arange(q0, k_end)[:, None] - jnp.arange(k_end)[None, :]
        decay = c[:, :, q0:k_end, None] - c[:, :, None, :k_end]
        logits = jnp.einsum('bqhd,bkhd->bhqk', q[:, q0:k_end], k[:, :k_end]) + decay
        logits = jnp.where(dist >= 0, logits, NEG_INF)
        p = jax.nn.softmax(logits, axis=-1)
        outs.append(jnp.einsum('bhqk,bkhd->bqhd', p, v[:, :k_end]))
    o = jnp.concatenate(outs, axis=1)
    return o.reshape(B, S, B_HEADS * B_HEAD_DIM).astype(x.dtype) @ w_o

def conv_ffn(x, w_in, conv_w, conv_b, w_out):
    u = x @ w_in
    u = lax.conv_general_dilated(u, conv_w[:, None, :].astype(u.dtype), window_strides=(1,),
                                 padding=[(CONV_WIDTH - 1, 0)],
                                 dimension_numbers=('NWC', 'WIO', 'NWC'),
                                 feature_group_count=2 * D_FF) + conv_b
    gate, val = jnp.split(u, 2, axis=-1)
    return (jax.nn.gelu(gate) * val) @ w_out

def second_inputs(seed: int = 0) -> dict:
    key = jax.random.key(seed)
    ks = iter(jax.random.split(key, 32))
    nrm = lambda shape, s: jax.random.normal(next(ks), shape, jnp.float32) * s
    gain = lambda shape: 1.0 + nrm(shape, 0.05)
    D, F = D_MODEL, D_FF
    return {
        "x": nrm((BATCH, SEQ, D), 1.0),
        "rel_bias": nrm((N_BUCKETS, A_HEADS), 0.2),
        "a_norm_pre": gain((N_A_LAYERS, D)),
        "a_norm_post": gain((N_A_LAYERS, D)),
        "a_w_qkv": nrm((N_A_LAYERS, D, 3 * 2 * A_HEADS * A_HEAD_DIM), D ** -0.5),
        "a_lam_q1": nrm((N_A_LAYERS, A_HEAD_DIM), 0.1),
        "a_lam_k1": nrm((N_A_LAYERS, A_HEAD_DIM), 0.1),
        "a_lam_q2": nrm((N_A_LAYERS, A_HEAD_DIM), 0.1),
        "a_lam_k2": nrm((N_A_LAYERS, A_HEAD_DIM), 0.1),
        "a_subln": gain((N_A_LAYERS, 2 * A_HEAD_DIM)),
        "a_w_o": nrm((N_A_LAYERS, 2 * A_HEADS * A_HEAD_DIM, D), D ** -0.5),
        "kv_norm": gain((D,)),
        "w_kvf": jnp.concatenate([nrm((D, 2 * B_HEADS * B_HEAD_DIM), D ** -0.5),
                                  nrm((D, B_HEADS), 0.1 * D ** -0.5)], axis=-1),
        "b_f": 3.0 + nrm((B_HEADS,), 0.1),
        "b_norm_pre": gain((N_B_LAYERS, D)),
        "b_norm_post": gain((N_B_LAYERS, D)),
        "b_w_q": nrm((N_B_LAYERS, D, B_HEADS * B_HEAD_DIM), D ** -0.5),
        "b_w_o": nrm((N_B_LAYERS, B_HEADS * B_HEAD_DIM, D), D ** -0.5),
        "ffn_norm_pre": gain((DEPTH, D)),
        "ffn_norm_post": gain((DEPTH, D)),
        "ffn_w_in": nrm((DEPTH, D, 2 * F), D ** -0.5),
        "ffn_conv_w": nrm((DEPTH, CONV_WIDTH, 2 * F), CONV_WIDTH ** -0.5),
        "ffn_conv_b": nrm((DEPTH, 2 * F), 0.02),
        "ffn_w_out": nrm((DEPTH, F, D), F ** -0.5),
    }

def second_block(x, rel_bias, a_norm_pre, a_norm_post, a_w_qkv, a_lam_q1, a_lam_k1, a_lam_q2, a_lam_k2,
              a_subln, a_w_o, kv_norm, w_kvf, b_f, b_norm_pre, b_norm_post, b_w_q, b_w_o,
              ffn_norm_pre, ffn_norm_post, ffn_w_in, ffn_conv_w, ffn_conv_b, ffn_w_out):
    h = x
    for l in range(DEPTH):
        if l < N_A_LAYERS:
            a = diff_attention(rms_norm(h, a_norm_pre[l]), a_w_qkv[l], a_w_o[l],
                               a_lam_q1[l], a_lam_k1[l], a_lam_q2[l], a_lam_k2[l],
                               a_subln[l], rel_bias, lambda_init_fn(l))
            h = h + rms_norm(a, a_norm_post[l])
        else:
            if l == N_A_LAYERS:
                k_sh, v_sh, c_sh = shared_kv(h, kv_norm, w_kvf, b_f)
            j = l - N_A_LAYERS
            a = forgetting_attention(rms_norm(h, b_norm_pre[j]), b_w_q[j], b_w_o[j], k_sh, v_sh, c_sh)
            h = h + rms_norm(a, b_norm_post[j])
        f = conv_ffn(rms_norm(h, ffn_norm_pre[l]), ffn_w_in[l], ffn_conv_w[l], ffn_conv_b[l], ffn_w_out[l])
        h = h + rms_norm(f, ffn_norm_post[l])
    return h


def setup_inputs(seed=0):
    out = dict(first_inputs(seed))
    for name, value in second_inputs(seed + 1).items():
        if name != "x":
            out[name + "_2"] = value
    return out


def reference(
    x, rel_bias_table, ffn1_norm, ffn1_w_gate, ffn1_w_up, ffn1_w_down, mix_norm, w_in,
    attn_sinks, kv_norm_c, w_kv_up_c, w_out, ffn2_norm, ffn2_w_gate, ffn2_w_up, ffn2_w_down,
    final_norm, rel_bias_2, a_norm_pre_2, a_norm_post_2, a_w_qkv_2, a_lam_q1_2, a_lam_k1_2,
    a_lam_q2_2, a_lam_k2_2, a_subln_2, a_w_o_2, kv_norm_2, w_kvf_2, b_f_2, b_norm_pre_2,
    b_norm_post_2, b_w_q_2, b_w_o_2, ffn_norm_pre_2, ffn_norm_post_2, ffn_w_in_2, ffn_conv_w_2,
    ffn_conv_b_2, ffn_w_out_2,
):
    x = first_block(
        x, rel_bias_table, ffn1_norm, ffn1_w_gate, ffn1_w_up, ffn1_w_down, mix_norm, w_in,
        attn_sinks, kv_norm_c, w_kv_up_c, w_out, ffn2_norm, ffn2_w_gate, ffn2_w_up, ffn2_w_down,
        final_norm,
    )
    return second_block(
        x, rel_bias_2, a_norm_pre_2, a_norm_post_2, a_w_qkv_2, a_lam_q1_2, a_lam_k1_2,
        a_lam_q2_2, a_lam_k2_2, a_subln_2, a_w_o_2, kv_norm_2, w_kvf_2, b_f_2, b_norm_pre_2,
        b_norm_post_2, b_w_q_2, b_w_o_2, ffn_norm_pre_2, ffn_norm_post_2, ffn_w_in_2,
        ffn_conv_w_2, ffn_conv_b_2, ffn_w_out_2,
    )


_drawn_inputs = setup_inputs


def setup_inputs(seed=0):
    import zlib

    import numpy as np

    out = dict(_drawn_inputs(seed))
    spreads = {}
    factors = {'a_lam_q1_2': 3.794, 'a_lam_k1_2': 3.22, 'b_f_2': 25.896, 'b_norm_pre_2': 6.304}
    for name, (base, spread) in spreads.items():
        noise = np.random.default_rng([zlib.crc32(name.encode()), seed]).standard_normal(out[name].shape)
        drawn = base * np.exp(spread * noise) if base else spread * noise
        out[name] = __import__('jax').numpy.asarray(drawn.astype(out[name].dtype))
    for name, factor in factors.items():
        out[name] = (out[name] * factor).astype(out[name].dtype)
    return out
```

```python
import math
from contextlib import ExitStack

import numpy as np
import concourse.bass as bass
from concourse import mybir

T, D, F, P = 512, 1024, 2816, 128
DEPTH, HD = 2, 64
KT, NT = D // P, T // P
FB = F // P
HALVES = 2
FH = FB // HALVES
BUCKETS, MAX_DIST, WINDOW = 32, 128, 128
D_IN, D_KVF = 2244, 2064
HA, HB, HC, HI = 8, 4, 4, 4
TOPK = T // 4
SCALE = HD ** -0.5
RMS_EPS, SUBLN_EPS = 1e-6, 1e-5
MASKED = -1e30
TAKEN = -3e38
NEAR = 2 * P
SPAN = T + P
PACK = P * NT * (NT + 1) // 2
LAMBDA_INIT = 0.8 - 0.6 * math.exp(0.0)

QA, KA, VA, QB, KB, VB, QC, CKV, QI, KI = 0, 4, 5, 6, 8, 10, 12, 14, 15, 17
W_IN_ORDER = [KI, QI, QI + 1, CKV] + list(range(CKV))
KI_COLS = D_IN - KI * P
FG_ROW, FG_COLS = 96, 112

GAINS = ["ffn1_norm", "mix_norm", "ffn2_norm", "final_norm", "a_norm_pre_2", "a_norm_post_2", "kv_norm_2",
         "b_norm_pre_2", "b_norm_post_2", "ffn_norm_pre_2", "ffn_norm_post_2"]
GAIN_ROWS = {"ffn1_norm": 2, "mix_norm": 2, "ffn2_norm": 2, "ffn_norm_pre_2": 2, "ffn_norm_post_2": 2}

ALL_STAGES = ["ffn1_0", "mix_0", "ffn2_0", "ffn1_1", "mix_1", "ffn2_1", "final", "diff", "conv_0", "fox", "conv_1"]


def kind(name):
    return "ffn" if name[:3] == "ffn" else name.split("_")[0]


def off(i):
    return P * i * (i + 1) // 2


TURN_GROUPS = [(0,), (1, 3), (2,)]
TURN_AT = {0: 0, 1: 0, 3: T - P, 2: 0}
SLOT_AT = {0: 0, 1: T, 3: 2 * T - P, 2: 2 * T}


def t5_onehot(window):
    dist = T - 1 - np.arange(SPAN)
    n = np.maximum(dist, 0)
    exact = BUCKETS // 2
    large = exact + (np.log(np.maximum(n, 1) / exact) / math.log(MAX_DIST / exact) * (BUCKETS - exact)).astype(np.int64)
    bucket = np.where(n < exact, n, np.minimum(large, BUCKETS - 1))
    hot = np.zeros((BUCKETS + 1, SPAN), np.float32)
    hot[bucket, np.arange(SPAN)] = 1.0 / SCALE
    hot[BUCKETS] = np.where((dist < 0) | (dist >= window), MASKED / SCALE, 0.0)
    return hot


def program(nc, A, out, stages):
    f32, f32r = mybir.dt.float32, mybir.dt.float32r
    ALU, ACT, AX = mybir.AluOpType, mybir.ActivationFunctionType, mybir.AxisListType
    DS = bass.ds

    UNIT, BASE = [], {}
    UNITS = {
        "ffn": ([(KT, P)] * (2 * FH) + [(FH, P)] * KT) * HALVES,
        "mix": [(KT, KI_COLS)] + [(KT, P)] * 17 + [(KT, P)] * KT,
        "diff": [(KT, P)] * (3 * KT) + [(KT, P)] * KT,
        "conv": ([(KT, P)] * (2 * FH) + [(FH, P)] * KT) * HALVES,
        "fox": [(KT, FG_COLS)] + [(KT, P)] * (3 * KT) + [(KT, P)] * KT,
        "final": [],
    }
    for name in stages:
        BASE[name] = len(UNIT)
        UNIT.extend(UNITS[kind(name)])
    MIX = {n: i for i, n in enumerate(n for n in stages if n[:3] == "mix")}
    N_HEADS = {"mix_0": 16, "mix_1": 16, "diff": 8, "fox": 16}
    XT_USES = KT // 2

    pre_norms = [n for n in stages if n != "final"]
    PRE = {}
    for n in pre_norms:
        PRE[n] = len(PRE)
        if n == "fox":
            PRE["fox_q"] = len(PRE)
    STAT, ROOT, POOL_SUM, SQ_FIRST, X_FIRST, NEXT = {}, {}, {}, {}, {}, {}
    squares = 0
    for a, b in zip(stages, stages[1:]):
        NEXT[a] = b
    CHAINED = ("diff", "conv_0", "fox", "conv_1")
    SQUARED = ("ffn1_0",) + CHAINED
    for n in stages:
        STAT[n], ROOT[n] = len(STAT), len(ROOT)
        if n in SQUARED:
            SQ_FIRST[n] = squares
            squares += KT
        else:
            POOL_SUM[n] = len(POOL_SUM)
        if n == "final":
            X_FIRST[n] = KT * len(X_FIRST)
        if n in MIX:
            STAT["ckv_" + n], ROOT["ckv_" + n] = len(STAT), len(ROOT)
            SQ_FIRST["ckv_" + n] = squares
            squares += 1
        if n in CHAINED:
            STAT["post_" + n], ROOT["post_" + n] = len(STAT), len(ROOT)
            POOL_SUM["post_" + n] = len(POOL_SUM)
            SQ_FIRST["post_" + n] = squares
            squares += 1
            X_FIRST[n] = KT * len(X_FIRST)
    T_FIRST = {n: KT * i for i, n in enumerate(n for n in stages if n in CHAINED)}
    USED = {n: (KT - 1) * i for i, n in enumerate(n for n in [m for m in stages if m[:4] == "ffn2"] + ["fox_q"])}
    JOB, HEAD, OUTB, VT_FIRST = {}, {}, {}, {}
    jobs = heads = turned = 0
    for n in stages:
        if n in N_HEADS:
            JOB[n], HEAD[n], OUTB[n], VT_FIRST[n] = jobs, heads, KT * len(OUTB), turned
            jobs, heads, turned = jobs + 16, heads + N_HEADS[n], turned + (4 if n in MIX else KT)
    PL_FIRST = {n: 16 * i for i, n in enumerate(n for n in stages if n[:3] in ("mix", "fox"))}
    FF = {n: FB * i for i, n in enumerate(n for n in stages if n[:3] in ("ffn", "con"))}
    CV = {n: FB * i for i, n in enumerate(n for n in stages if n[:4] == "conv")}

    ctx = ExitStack()
    with ctx:
        where = [nc.sbuf_base + (-nc.sbuf_base) % 32]

        def room(size):
            at = where[0]
            where[0] += size + (-size) % 32
            assert where[0] <= nc.sbuf_usable_end, where[0]
            return at

        def put(name, shape, at=None, dt=f32):
            size = 4 * int(np.prod(shape[1:]))
            return nc.alloc_sbuf_tensor_at(name, shape, dt, offset=room(size) if at is None else at)

        def sem(name):
            return ctx.enter_context(nc.semaphore(name))

        xres = put("xres", [P, KT, T])
        h_hi, h_lo = (put(n, [P, KT, T], dt=f32r) for n in ("h_hi", "h_lo"))
        raw = [put(f"w_raw{i}", [P, FH, P]) for i in range(2)]
        w_hi = [put(f"w_hi{i}", [P, FH, P], dt=f32r) for i in range(2)]
        w_lo = [put(f"w_lo{i}", [P, FH, P], dt=f32r) for i in range(2)]

        bias_at = room(4 * (HA * NEAR + (HB + HC) * T))
        bias_win = put("bias_win", [P, HA, NEAR], bias_at)
        bias_far = put("bias_far", [P, HB + HC, T], bias_at + 4 * HA * NEAR)
        bias_diff = put("bias_diff", [P, 8, T], bias_at + 4 * HA * NEAR)
        causal = put("causal", [P, T], bias_at)
        decay_q = put("decay_q", [P, 4, T], bias_at + 4 * T, f32r)
        decay_k = put("decay_k", [P, 4, T], bias_at + 4 * 5 * T, f32r)

        big_at = room(4 * 24 * T)
        act_hi = put("act_hi", [P, FH, T], big_at, f32r)
        act_lo = put("act_lo", [P, FH, T], big_at + 4 * FH * T, f32r)
        proj = put("proj", [P, 24, T], big_at)
        pen_bias = [put(f"pen_bias{i}", [P, PACK], big_at + 4 * (18 * T + i * PACK)) for i in range(2)]

        val_at = room(4 * 8 * T)
        v_win = put("v_win", [P, NT, P], val_at)
        v_blk = put("v_blk", [P, NT, 2 * P], val_at + 4 * T)
        v_sp = put("v_sp", [P, NT, HD], val_at + 4 * 3 * T)
        k_swap = put("k_swap", [P, T], val_at + 4 * 4 * T)
        k_idx = put("k_idx", [P, T], val_at + 4 * 6 * T)
        k_sp = put("k_sp", [P, T], val_at + 4 * 7 * T)
        v_all = put("v_all", [P, NT, D], val_at)
        acc = put("acc", [P, KT, T], val_at)
        xtok = put("xtok", [P, NT, D], val_at)

        prob_at = room(2 * 4 * PACK)
        score_at = room(4 * PACK)
        pair = [put("probs0", [P, PACK], prob_at), put("probs1", [P, PACK], prob_at + 4 * PACK)]
        third = put("probs2", [P, PACK], score_at)
        in_proj = put("probs2_mix", [P, PACK], big_at + 4 * CKV * T)
        PROBS = {"mix": pair + [in_proj], "fox": pair + [third],
                 "diff": pair + [third, put("probs3", [P, PACK], bias_at)]}
        rel = put("rel", [P, HI, T], prob_at)
        score = put("score", [P, PACK], score_at)
        ckv_n = put("ckv_n", [P, T], prob_at + 4 * HI * T)
        gated = put("gated", [P, T], prob_at)
        gate_r = put("gate_r", [P, T], prob_at + 8 * T)
        tap_g = put("tap_g", [P, T], prob_at + 4 * T)
        tap_v = put("tap_v", [P, T], prob_at + 8 * T)
        prod = put("prod", [P, T], prob_at + 12 * T)
        scaled_g, scaled_v = put("scaled_g", [P, T], prob_at + 16 * T), put("scaled_v", [P, T], score_at)
        norm_t = [put(f"norm_t{i}", [P, T], prob_at + 4 * i * T) for i in range(4)]
        biased_at = room(4 * PACK)
        biased = put("biased", [P, PACK], biased_at)
        sq = [put(f"sq{i}", [P, T], biased_at + 4 * i * T) for i in range(2)]
        psq = put("psq", [P, T], biased_at + 0)
        fgate = [put(f"fgate{i}", [P, T], prob_at + 4 * i * T) for i in range(5)]
        fparts = [put(f"fparts{i}", [P, T], prob_at + 4 * at * T, f32r) for i, at in enumerate((0, 1, 2, 4))]
        turned_at = room(4 * PACK)
        probs_t = put("probs_t", [P, PACK], turned_at)
        rstd2 = put("rstd2", [P, T], turned_at)
        v_sp_t = put("v_sp_t", [P, T], big_at + 4 * 23 * T)
        ssq, rms, rstd = put("ssq", [P, T]), put("rms", [P, T]), put("rstd", [P, T])

        ident, ones = put("ident", [P, P]), put("ones", [P, P])
        gain_rows, gains = put("gain_rows", [P, P], turned_at), put("gains", [P, P])
        conv_rows = [put(f"conv_rows{i}", [4 * FB, P], turned_at + 4 * P * (1 + i)) for i in range(4)]
        conv = put("conv", [P, DEPTH, 4, 2 * FB])
        onehot = [put(f"onehot{i}", [BUCKETS + 1, SPAN], bias_at + 4 * SPAN * i) for i in range(2)]
        table, table2 = put("table", [BUCKETS + 1, 16]), put("table2", [BUCKETS + 1, 8])
        brow = [put(f"brow{i}", [16, SPAN], bias_at + 4 * SPAN * (2 + i)) for i in range(3)]
        w_kvup = put("w_kvup", [P, DEPTH, P])
        few_rows = put("few_rows", [DEPTH + 1, P], turned_at + 4 * P * 8)
        g_few = put("g_few", [P, DEPTH + 1])
        g_ckv, g_sub = g_few[:, 0:DEPTH], g_few[:, DEPTH:DEPTH + 1]
        sinks, nsinks = put("sinks", [P, DEPTH, HA]), put("nsinks", [P, DEPTH, HA])
        lam_in, lam_t = put("lam_in", [P, 4, HD], turned_at + 4 * P * 5), put("lam_t", [P, 2, HD], turned_at + 4 * P * 7)
        lam_e = put("lam_e", [P, 2])
        nlam = put("nlam", [P, 1])
        spare = put("spare", [P, 1])
        eps_c, sub_eps, mean_p = put("eps_c", [P, 1]), put("sub_eps", [P, 1]), put("mean_p", [P, P])
        nmax, psum_r, recip = (put(n, [P, 4, NT]) for n in ("nmax", "psum_r", "recip"))
        sink_e = put("sink_e", [P, 4, NT])
        top8 = put("top8", [P, 8])
        w_idx = put("w_idx", [P, NT, HI])
        bf_col = put("bf_col", [P, 1])
        brow_d = [nc.dram_tensor(f"bias_rows{i}", [8, P, SPAN], f32, kind="Internal") for i in range(3)]

        bank = [ctx.enter_context(nc.psum_tensor(f"bank{i}", [P, T], f32)) for i in range(8)]
        FIRST = {BASE[n] + i: bank[3 + (BASE[n] + i) % 2] for n in stages if n != "final" for i in range(2)}

        def result(c):
            return FIRST.get(c, bank[c % 2])

        STATB, OUT = bank[2], bank[7]
        SCORES = [bank[0], bank[1], bank[3], bank[4]]
        DOTS = [bank[3], bank[4], bank[5], bank[6]]
        TURN = [bank[5], bank[6], bank[2]]

        raw_full = [sem("raw_full0"), sem("raw_full1")]
        hi_ready, lo_ready = sem("hi_ready"), sem("lo_ready")
        mm_done = sem("mm_done")
        bank_free = [sem("bank_free0"), sem("bank_free1")]
        consts, x_in, x_turned = sem("consts"), sem("x_in"), sem("x_turned")
        gains_in, rows_in, gains_turned, rows_turned, rows_out = (
            sem("gains_in"), sem("rows_in"), sem("gains_turned"), sem("rows_turned"), sem("rows_out"))
        small_in = sem("small_in")
        tab_mm, tab_row, tab_dram, tab_back = sem("tab_mm"), sem("tab_row"), sem("tab_dram"), sem("tab_back")
        ssq_ready, pool_step = sem("ssq_ready"), sem("pool_step")
        sq_ready, h_used = sem("sq_ready"), sem("h_used")
        sum_ready, rms_ready, rstd_ready = sem("sum_ready"), sem("rms_ready"), sem("rstd_ready")
        t_ready, hhi_ready, h_ready = sem("t_ready"), sem("hhi_ready"), sem("h_ready")
        x_done = sem("x_done")
        silu_ready, gate_ready, prod_ready, acthi_ready, act_ready = sem("silu_ready"), sem("gate_ready"), sem("prod_ready"), sem("acthi_ready"), sem("act_ready")
        gelu_ready, tap_ready, conv_step, conv_done = sem("gelu_ready"), sem("tap_ready"), sem("conv_step"), sem("conv_done")
        shifted = sem("shifted")
        idxw_turned, dots_ready, rel_ready, score_ready = (sem("idxw_turned"), sem("dots_ready"), sem("rel_ready"),
                                                           sem("score_ready"))
        score_masked, pen_ready, penb_ready = sem("score_masked"), sem("pen_ready"), sem("penb_ready")
        ckvn_ready, kvup_done, kv_ready = sem("ckvn_ready"), sem("kvup_done"), sem("kv_ready")
        vt_turned, vt_ready = sem("vt_turned"), sem("vt_ready")
        s_ready, s_biased, p_ready, sink_ready = sem("s_ready"), sem("s_biased"), sem("p_ready"), sem("sink_ready")
        sinkin_ready = sem("sinkin_ready")
        pn_ready, pt_turned = sem("pn_ready"), sem("pt_turned")
        pt_act, pt_dve, pv_done = sem("pt_act"), sem("pt_dve"), sem("pv_done")
        ohi_ready, o_ready, o_sq = sem("ohi_ready"), sem("o_ready"), sem("o_sq")
        recip_ready, first_ready, pl_ready = sem("recip_ready"), sem("first_ready"), sem("pl_ready")
        sub_sum, sub_out, sub_inv = sem("sub_sum"), sem("sub_out"), sem("sub_inv")
        sub_root, sub_norm = sem("sub_root"), sem("sub_norm")
        lam_ready, fg_one, fg_ready, decay_in = sem("lam_ready"), sem("fg_one"), sem("fg_ready"), sem("decay_in")
        fg_act = sem("fg_act")
        y_turned, y_out, stored = sem("y_turned"), sem("y_out"), sem("stored")
        dve_step = sem("dve_step")

        def wait_evacuated(eng, c, j=0):
            eng.wait_ge(bank_free[c % 2], XT_USES + c // 2 + 1 + j)

        assert T // 256 == 2

        def softmax_job(stage, n):
            if stage.startswith("mix"):
                if n < HA:
                    h, lo = n, HD * (n % 2)
                    return dict(q=proj[lo:lo + HD, QA + h // 2, :], k=proj[lo:lo + HD, KA, :] if h // (HA // 2) == h % 2 else k_swap[lo:lo + HD, :], window=True,
                                bias=lambda i, h=h: bias_win[:, h, NEAR - (P if i == 0 else NEAR):NEAR])
                if n < HA + HB:
                    h = n - HA
                    lo = HD * (h % 2)
                    return dict(q=proj[lo:lo + HD, QB + h // 2, :], k=proj[lo:lo + HD, KB + h // 2, :], window=False,
                                bias=lambda i, h=h: bias_far[:, h, T - P * (i + 1):T])
                h = n - HA - HB
                lo = HD * (h % 2)
                return dict(q=proj[lo:lo + HD, QC + h // 2, :], k=k_sp[lo:lo + HD, :], window=False, sparse=h,
                            bias=lambda i, h=h: (bias_far[:, HB + h, T - P:T] if i == 0 else
                                                 pen_bias[h % 2][:, off(i):off(i + 1)]))
            if stage == "diff":
                h, lo = n // 2, HD * (n % 2)
                return dict(q=proj[lo:lo + HD, h, :], k=proj[lo:lo + HD, KT + h, :], window=False,
                            bias=lambda i, h=h: bias_diff[:, h, T - P * (i + 1):T])
            lo = HD * (n % 2)
            return dict(q=proj[lo:lo + HD, 2 * KT + n // 2, :], k=proj[lo:lo + HD, n // 2, :], window=False, decay=n,
                        bias=lambda i: causal[:, T - P * (i + 1):T])

        def keys(job, i):
            first = P * max(0, i - 1) if job["window"] else 0
            return first, P * (i + 1) - first

        def head_values(stage, v, b):
            if stage.startswith("mix"):
                if v < HA:
                    g = v // (HA // 2)
                    return v_win[:, b, HD * g:HD * (g + 1)]
                if v < HA + HB:
                    return v_blk[:, b, HD * (v - HA):HD * (v - HA + 1)]
                return v_sp[:, b, :]
            w = P if stage == "diff" else HD
            return v_all[:, b, w * v:w * (v + 1)]

        def turned_width(stage, v, b):
            if stage in MIX and v < HA:
                return min(NEAR, T - P * b)
            return T - P * b

        gain_at, at = {}, 0
        for g in GAINS:
            for l in range(GAIN_ROWS.get(g, 1)):
                gain_at[g, l] = at
                at += KT

        def gain(name, l, k):
            return gains[:, gain_at[name, l] + k:gain_at[name, l] + k + 1]

        PRE_GAIN = {"ffn1_0": ("ffn1_norm", 0), "mix_0": ("mix_norm", 0), "ffn2_0": ("ffn2_norm", 0),
                    "ffn1_1": ("ffn1_norm", 1), "mix_1": ("mix_norm", 1), "ffn2_1": ("ffn2_norm", 1),
                    "final": ("final_norm", 0), "diff": ("a_norm_pre_2", 0), "conv_0": ("ffn_norm_pre_2", 0),
                    "fox": ("kv_norm_2", 0), "fox_q": ("b_norm_pre_2", 0), "conv_1": ("ffn_norm_pre_2", 1)}
        POST_GAIN = {"diff": ("a_norm_post_2", 0), "conv_0": ("ffn_norm_post_2", 0), "fox": ("b_norm_post_2", 0),
                     "conv_1": ("ffn_norm_post_2", 1)}
        N_ROWS = 2 + 3 * DEPTH
        N_SMALL = 11
        TABLES = [(table, onehot[1], HA), (table, onehot[0], 16), (table2, onehot[0], 8)]
        out_units = {n: BASE[n] + len(UNITS[kind(n)]) - KT for n in stages}

        BEFORE = {b: a for a, b in NEXT.items()} | {stages[0]: None}
        FOLLOW = {a: b for a, b in NEXT.items() if b not in CHAINED and b != "final"}
        LAST_USE = {n: (BASE["fox"] + 2 * KT if n == "fox_q" else out_units[BEFORE[n]] + KT - 1) for n in USED if n != "fox_q" or "fox" in BASE}
        SQUARES = {n: (proj if n == "ffn1_0" else acc) for n in SQUARED}
        CONV_FF = {n: sum(FB for m in stages[:i] if kind(m) == "conv") for i, n in enumerate(stages)}

        def wait_x(eng, stage, k):
            if stage is None:
                eng.wait_ge(bank_free[k % 2], k // 2 + 1)
            elif stage in X_FIRST:
                eng.wait_ge(x_done, X_FIRST[stage] + k + 1)
            else:
                wait_evacuated(eng, out_units[stage] + k)

        block = ctx.enter_context(nc.Block())

        @block.sync
        def _(sp):
            def load(c, src, j=None):
                nk, cols = UNIT[c]
                if c >= 2:
                    sp.wait_ge(lo_ready, c - 1 if j is None else c - 1 + 2 * j)
                elif j is not None:
                    sp.wait_ge(lo_ready, c + 1 + 2 * (j - 1))
                sp.dma_start(raw[c % 2][:, 0:nk, 0:cols], src).then_inc(raw_full[c % 2], 16)

            def kview(w, l):
                return w[l].rearrange("(k p) n -> p k n", p=P)

            def ff(name, up_a, up_b, down):
                for hf in range(HALVES):
                    c = BASE[name] + 30 * hf
                    first = hf * FH * P
                    with sp.Fori(1 if c == 0 else 0, FH) as j:
                        for s, w in enumerate((up_a, up_b)):
                            load(c + s, w[:, :, DS(first + P * j, P)], j)
                    c += 2 * FH
                    with sp.Fori(0, KT // 2) as j:
                        for s in range(2):
                            load(c + s, down[:, hf * FH:(hf + 1) * FH, DS(2 * P * j + P * s, P)], j)

            def columns(c, w, n):
                with sp.Fori(0, n // 2) as j:
                    for s in range(2):
                        load(c + s, w[:, :, DS(P * s + 2 * P * j, P)], j)

            sp.dma_start(xtok[:, :, :], A["x"][0].rearrange("(t p) d -> p t d", p=P)).then_inc(x_in, 16)
            load(0, kview(A["ffn1_w_gate"], 0)[:, :, 0:P])
            load(1, kview(A["ffn1_w_up"], 0)[:, :, 0:P])
            for n, g in enumerate(GAINS):
                rows = GAIN_ROWS.get(g, 1) * KT
                src = A[g].rearrange("l (k p) -> (l k) p", p=P) if len(A[g].shape) == 2 else \
                    A[g].rearrange("(k p) -> k p", p=P)
                sp.dma_start(gain_rows[gain_at[g, 0]:gain_at[g, 0] + rows, :], src).then_inc(gains_in, 16)
            sp.dma_start(few_rows[0:DEPTH, :], A["kv_norm_c"]).then_inc(rows_in, 16)
            sp.dma_start(few_rows[DEPTH:DEPTH + 1, :], A["a_subln_2"]).then_inc(rows_in, 16)
            for l in range(DEPTH):
                taps = A["ffn_conv_w_2"][l].rearrange("c (j p) -> (c j) p", p=P)
                sp.dma_start(conv_rows[2 * l][0:4 * FB, :], taps[0:4 * FB, :]).then_inc(rows_in, 16)
                sp.dma_start(conv_rows[2 * l + 1][0:2 * FB, :], taps[4 * FB:6 * FB, :]).then_inc(rows_in, 16)
                sp.dma_start(conv_rows[2 * l + 1][2 * FB:4 * FB, :],
                              A["ffn_conv_b_2"][l].rearrange("(j p) -> j p", p=P)).then_inc(rows_in, 16)
            sp.dma_start(table[0:BUCKETS, :], A["rel_bias_table"]).then_inc(small_in, 16)
            sp.dma_start(table2[0:BUCKETS, :], A["rel_bias_2"]).then_inc(small_in, 16)
            sp.dma_start(onehot[0][:, :], A["onehot_causal"]).then_inc(small_in, 16)
            sp.dma_start(onehot[1][:, :], A["onehot_window"]).then_inc(small_in, 16)
            sp.dma_start(w_kvup[:, :, :], A["w_kv_up_c"].rearrange("l p n -> p l n")).then_inc(small_in, 16)
            sp.dma_start(sinks[:, :, :].rearrange("p l h -> p (l h)"),
                          A["attn_sinks"].rearrange("l h -> (l h)").partition_broadcast(P)).then_inc(small_in, 16)
            sp.dma_start(bf_col[FG_ROW:FG_ROW + 16, :],
                          A["b_f_2"].rearrange("(h a) -> h a", a=1)).then_inc(small_in, 16)
            for n, w in enumerate(("a_lam_q1_2", "a_lam_k1_2", "a_lam_q2_2", "a_lam_k2_2")):
                sp.dma_start(lam_in[:, n, :],
                              A[w].rearrange("l d -> (l d)").partition_broadcast(P)).then_inc(small_in, 16)

            for name in stages:
                l = int(name[-1]) if name[-1] in "01" else 0
                c = BASE[name]
                if kind(name) == "ffn":
                    w = name[:4]
                    ff(name, kview(A[w + "_w_gate"], l), kview(A[w + "_w_up"], l), kview(A[w + "_w_down"], l))
                elif kind(name) == "mix":
                    w = kview(A["w_in"], l)
                    for i, cb in enumerate(W_IN_ORDER[:4]):
                        load(c + i, w[:, :, P * cb:P * cb + UNIT[c + i][1]])
                    columns(c + 4, w, 14)
                    columns(c + 18, kview(A["w_out"], l), KT)
                elif kind(name) == "diff":
                    columns(c, kview(A["a_w_qkv_2"], 0), 3 * KT)
                    columns(c + 3 * KT, kview(A["a_w_o_2"], 0), KT)
                elif kind(name) == "fox":
                    w = A["w_kvf_2"].rearrange("(k p) n -> p k n", p=P)
                    load(c, w[:, :, D_KVF - FG_COLS:D_KVF])
                    columns(c + 1, w, 2 * KT)
                    columns(c + 1 + 2 * KT, kview(A["b_w_q_2"], 0), KT)
                    columns(c + 1 + 3 * KT, kview(A["b_w_o_2"], 0), KT)
                elif kind(name) == "conv":
                    w = kview(A["ffn_w_in_2"], l)
                    ff(name, w[:, :, 0:F], w[:, :, F:2 * F], kview(A["ffn_w_out_2"], l))
            for t in range(NT):
                sp.wait_ge(y_out, 2 * t + 2)
                sp.dma_start(out[0, P * t:P * (t + 1), :], xtok[:, t, :]).then_inc(stored, 16)
            sp.wait_ge(stored, 16 * NT)

        @block.gpsimd
        def _(pool):
            steps = [0]

            def chain(ins):
                steps[0] += 1
                ins.then_inc(pool_step, 1)
                pool.wait_ge(pool_step, steps[0])

            chain(nc.gpsimd.memset(ident[:, :], 0.0))
            chain(nc.gpsimd.affine_select(out=ident[:, :], in_=ident[:, :], compare_op=ALU.not_equal, fill=1.0,
                                          base=0, pattern=[[-1, P]], channel_multiplier=1))
            chain(nc.gpsimd.memset(ones[:, :], 1.0))
            chain(nc.gpsimd.memset(table[BUCKETS:BUCKETS + 1, :], 1.0))
            chain(nc.gpsimd.memset(table2[BUCKETS:BUCKETS + 1, :], 1.0))
            chain(nc.gpsimd.memset(eps_c[:, :], RMS_EPS))
            chain(nc.gpsimd.memset(sub_eps[:, :], SUBLN_EPS))
            nc.gpsimd.memset(mean_p[:, :], 1.0 / P).then_inc(consts, 1)

            def sum_squares(wait_block, src, n=KT):
                for k in range(n):
                    wait_block(k)
                    if k == 0:
                        chain(nc.gpsimd.tensor_tensor(ssq[:, :], src[:, k, :], src[:, k, :], ALU.mult))
                        continue
                    chain(nc.gpsimd.tensor_tensor(psq[:, :], src[:, k, :], src[:, k, :], ALU.mult))
                    add = nc.gpsimd.tensor_tensor(ssq[:, :], ssq[:, :], psq[:, :], ALU.add)
                    if k < n - 1:
                        chain(add)
                    else:
                        add.then_inc(ssq_ready, 1)

            def store_bias_rows():
                for r, (_, _, heads) in enumerate(TABLES):
                    pool.wait_ge(tab_row, 2 * r + 2)
                    rows = brow[r][heads - 8:heads, :].unsqueeze(1).broadcast_to((8, P, SPAN))
                    pool.dma_start(brow_d[r].ap(), rows).then_inc(tab_dram, 16)

            def spread_bias(dst, r, width):
                src = bass.AP(brow_d[r].ap().tensor, T - 1 - (width - P), [[SPAN - 1, P], [P * SPAN, 8], [1, width]])
                pool.dma_start(dst, src).then_inc(tab_back, 16)

            def normalise(stage, v):
                n = 2 * v if stage == "diff" else v
                job, g = softmax_job(stage, n), JOB[stage] + n
                ring = PROBS[kind(stage)]
                buf = ring[n % len(ring)]
                pool.wait_ge(recip_ready, HEAD[stage] + v + 1)
                for i in range(NT // 2):
                    tile = buf[:, off(i):off(i) + keys(job, i)[1]]
                    ins = nc.gpsimd.tensor_scalar(tile, tile, recip[:, g % 4, i:i + 1], None, ALU.mult)
                ins.then_inc(first_ready if stage == "diff" else pn_ready, 1)

            def select(h):
                if h == 0:
                    pool.wait_ge(pen_ready, 3 * (MIX[name] + 1))
                    pool.wait_ge(tab_back, 32)
                if h >= 2:
                    pool.wait_ge(s_biased, NT * (JOB[name] + HA + HB + h - 1))
                for i in range(1, NT):
                    nc.gpsimd.tensor_tensor(pen_bias[h % 2][:, off(i):off(i + 1)], bias_far[:, HB + h, T - P * (i + 1):T],
                                            score[:, off(i):off(i + 1)], ALU.add).then_inc(penb_ready, 1)

            store_bias_rows()
            before = None
            for name in stages:
                if name in POOL_SUM:
                    sum_squares(lambda k: wait_x(pool, before, k), xres)
                if name in MIX:
                    if MIX[name] == 0:
                        pool.wait_ge(tab_dram, 16 * len(TABLES))
                        spread_bias(bias_win[:, :, :], 0, NEAR)
                        spread_bias(bias_far[:, :, :], 1, T)
                    for i in range(1, NT):
                        pool.wait_ge(score_ready, 3 * MIX[name] + i)
                        own = score[:, off(i) + P * i:off(i + 1)]
                        nc.gpsimd.affine_select(out=own, in_=own, compare_op=ALU.is_ge, fill=MASKED, base=0,
                                                pattern=[[-1, P]], channel_multiplier=1).then_inc(score_masked, 1)
                    for v in range(N_HEADS[name]):
                        normalise(name, v)
                        if v in (9, 10, 12, 13):
                            select((9, 10, 12, 13).index(v))
                if name == "diff":
                    pool.wait_ge(tab_dram, 16 * len(TABLES))
                    if MIX:
                        pool.wait_ge(s_biased, NT * JOB[name])
                    spread_bias(bias_diff[:, :, :], 2, T)
                    for v in range(KT):
                        normalise(name, v)
                if name == "fox":
                    pool.wait_ge(o_ready, OUTB["fox"])
                    chain(nc.gpsimd.memset(causal[:, :], 0.0))
                    chain(nc.gpsimd.affine_select(out=causal[:, :], in_=causal[:, :], compare_op=ALU.is_ge,
                                                  fill=MASKED / SCALE, base=T - P, pattern=[[-1, T]],
                                                  channel_multiplier=1))
                    chain(nc.gpsimd.memset(decay_q[:, :, :].bitcast(f32), 1.0))
                    chain(nc.gpsimd.memset(decay_k[:, :, :].bitcast(f32), 1.0))
                    pool.wait_ge(fg_ready, 1)
                    for h in range(16):
                        row, col = 32 * (h % 4), h // 4
                        for n, part in enumerate(fparts):
                            to, r = (decay_q, row + n) if n < 2 else (decay_k, row + n)
                            pool.dma_start(to[r:r + 1, col, :],
                                           part[FG_ROW + h:FG_ROW + h + 1, :]).then_inc(decay_in, 16)
                    for v in range(N_HEADS[name]):
                        normalise(name, v)
                if name in CHAINED:
                    sum_squares(lambda k: wait_evacuated(pool, out_units[name] + k), acc, KT - 1)
                    for k in range(KT):
                        pool.wait_ge(t_ready, T_FIRST[name] + k + 1)
                        nc.gpsimd.tensor_tensor(xres[:, k, :], xres[:, k, :], norm_t[k % 4][:, :], ALU.add).then_inc(x_done, 1)
                before = name

        @block.scalar
        def _(act):
            def hi(c, j=0, also=None):
                if c >= len(UNIT):
                    return
                nk, cols = UNIT[c]
                if also is not None:
                    act.wait_ge(*also)
                if c >= 2:
                    act.wait_ge(mm_done, c - 1 + 2 * j)
                act.wait_ge(raw_full[c % 2], 16 * (c // 2 + 1) + 16 * j)
                nc.scalar.activation(w_hi[c % 2][:, 0:nk, 0:cols], raw[c % 2][:, 0:nk, 0:cols],
                                     ACT.Copy).then_inc(hi_ready, 1)

            def root(name, n):
                nc.scalar.activation(spare[:, :], eps_c[:, :], ACT.Sqrt)
                if ROOT[name]:
                    act.wait_ge(rstd_ready, ROOT[name])
                act.wait_ge(sum_ready, STAT[name] + 1)
                nc.scalar.activation(rms[:, :], STATB[:, :], ACT.Sqrt, bias=eps_c[:, 0:1],
                                     scale=1.0 / n).then_inc(rms_ready, 1)

            def h_high(name, k):
                g, l = PRE_GAIN[name]
                if name != "fox_q":
                    wait_x(act, BEFORE[name], k)
                if name in USED:
                    if k < KT - 1:
                        act.wait_ge(h_used, USED[name] + k + 1)
                    else:
                        act.wait_ge(mm_done, LAST_USE[name] + 1)
                nc.scalar.activation(h_hi[:, k, :], xres[:, k, :], ACT.Copy, scale=gain(g, l, k)).then_inc(hhi_ready, 1)

            def squared_input(name):
                for k in range(KT):
                    h_high(name, k)
                    nc.scalar.activation(SQUARES[name][:, k, :], xres[:, k, :], ACT.Square).then_inc(sq_ready, 1)

            def act_high(jj):
                nc.scalar.activation(act_hi[:, DS(jj, 1), :], prod[:, :].rearrange("p (o n) -> p o n", o=1),
                                     ACT.Copy).then_inc(acthi_ready, 1)

            def down_parts(c, name):
                with act.Fori(0, KT // 2 - 1) as j:
                    hi(c + 2, j)
                    hi(c + 3, j)
                hi(c + KT)
                follow = FOLLOW.get(name)
                if follow:
                    for k in range(KT - 1):
                        h_high(follow, k)
                hi(c + KT + 1)
                if follow:
                    h_high(follow, KT - 1)

            def gated_ff(name):
                for hf in range(HALVES):
                    c = BASE[name] + 30 * hf


                    def pair(j):
                        at, jj = (c + 2 * j, 0) if isinstance(j, int) else (c + 2, j - 1)
                        product = (bank_free[(c + 1) % 2], XT_USES + (c + 1) // 2 + 1 + j)
                        act.wait_ge(bank_free[c % 2], XT_USES + c // 2 + 1 + j)
                        nc.scalar.activation(gated[:, :], scaled_g[:, :], ACT.Silu).then_inc(silu_ready, 1)
                        if at in FIRST:
                            act.wait_ge(*product)
                        else:
                            hi(at + 2, jj)
                            hi(at + 3, jj, also=product)
                        act_high(j)

                    if hf == 0:
                        pair(0)
                    with act.Fori(1 - hf, FH - 1) as j:
                        pair(j)
                    pair(FH - 1)
                    down_parts(c + 2 * FH, name if hf else None)

            def conv_ff(name):
                l = int(name[-1])

                def tap(dst, src, ch):
                    nc.scalar.activation(dst[:, :], src[:, :], ACT.Identity, bias=conv[:, l, 3, DS(ch, 1)],
                                         scale=conv[:, l, 2, DS(ch, 1)]).then_inc(tap_ready, 1)

                for hf in range(HALVES):
                    c = BASE[name] + 30 * hf
                    cv = CV[name] + FH * hf

                    def pair(j, first=False):
                        at, jj = (c + 2 * j, 0) if isinstance(j, int) else (c + 2, j - 1)
                        if not first:
                            act.wait_ge(prod_ready, cv + j)
                        made_g = (bank_free[c % 2], XT_USES + c // 2 + 1 + j)
                        made_v = (bank_free[(c + 1) % 2], XT_USES + (c + 1) // 2 + 1 + j)
                        early = first and hf == 0
                        if early:
                            act.wait_ge(*made_g)
                        else:
                            hi(at + 2, jj, also=made_g)
                        if not first:
                            act_high(j - 1)
                        tap(tap_g, scaled_g, hf * FH + j)
                        if early:
                            act.wait_ge(*made_v)
                        else:
                            hi(at + 3, jj, also=made_v)
                        tap(tap_v, scaled_v, FB + hf * FH + j)
                        act.wait_ge(conv_done, 2 * cv + 1 + 2 * j)
                        nc.scalar.activation(gated[:, :], tap_g[:, :], ACT.Gelu_apprx_tanh).then_inc(gelu_ready, 1)

                    pair(0, first=True)
                    with act.Fori(1, FH - 1) as j:
                        pair(j)
                    pair(FH - 1)
                    act.wait_ge(prod_ready, cv + FH)
                    act_high(FH - 1)
                    down_parts(c + 2 * FH, name if hf else None)

            def turn_values(stage, groups):
                for g, dst in enumerate(groups):
                    act.wait_ge(vt_turned, VT_FIRST[stage] + g + 1)
                    w = dst.shape[2]
                    nc.scalar.activation(dst, TURN[g % 2][:, 0:NT * w].rearrange("p (b w) -> p b w", w=w),
                                         ACT.Copy).then_inc(vt_ready, 1)

            def exps(stage, n):
                job, g = softmax_job(stage, n), JOB[stage] + n
                ring = PROBS[kind(stage)]
                if n >= len(ring):
                    used = (n - len(ring)) // (2 if stage == "diff" else 1)
                    act.wait_ge(pt_turned, len(TURN_GROUPS) * (HEAD[stage] + used + 1))
                for i in range(NT):
                    w = keys(job, i)[1]
                    act.wait_ge(s_biased, NT * g + i + 1)
                    nc.scalar.activation(ring[n % len(ring)][:, off(i):off(i) + w], biased[:, off(i):off(i) + w], ACT.Exp,
                                         bias=nmax[:, g % 4, i:i + 1], scale=-1.0,
                                         accum_out=psum_r[:, g % 4, i:i + 1]).then_inc(p_ready, 1)
                if job["window"]:
                    act.wait_ge(sinkin_ready, HA * MIX[stage] + n + 1)
                    nc.scalar.activation(sink_e[:, g % 4, :], sink_e[:, g % 4, :], ACT.Exp).then_inc(sink_ready, 1)

            def probs_out(stage, v):
                g = HEAD[stage] + v
                for n, group in enumerate(TURN_GROUPS):
                    if n == 1:
                        continue
                    b = group[0]
                    w = turned_width(stage, v, b)
                    act.wait_ge(pt_turned, len(TURN_GROUPS) * g + n + 1)
                    if g:
                        act.wait_ge(pv_done, g)
                    nc.scalar.activation(probs_t[:, SLOT_AT[b]:SLOT_AT[b] + w], TURN[n][:, 0:w],
                                         ACT.Copy).then_inc(pt_act, 1)

            def head_out(stage, v):
                g = HEAD[stage] + v
                if stage == "diff":
                    act.wait_ge(pv_done, g + 1)
                    nc.scalar.activation(proj[:, v, :], OUT[:, :], ACT.Copy)
                    nc.scalar.activation(proj[:, KT + v, :], OUT[:, :], ACT.Square).then_inc(o_sq, 1)
                elif v % 2:
                    act.wait_ge(pv_done, g + 1)
                    nc.scalar.activation(h_hi[:, v // 2, :], OUT[:, :], ACT.Copy).then_inc(ohi_ready, 1)

            def sub_mean(v):
                act.wait_ge(sub_sum, v + 1)
                nc.scalar.activation(proj[:, KT + v, :], OUT[:, :], ACT.Identity, bias=sub_eps[:, 0:1],
                                     scale=1.0).then_inc(sub_out, 1)

            def sub_high(v):
                act.wait_ge(sub_norm, v + 1)
                nc.scalar.activation(h_hi[:, v, :], proj[:, 2 * KT + v, :], ACT.Copy).then_inc(ohi_ready, 1)

            def attention(stage):
                n = N_HEADS[stage]
                for m in range(2 if stage == "diff" else 3):
                    exps(stage, m)
                if stage == "diff":
                    for v in range(n):
                        if v + 1 < n:
                            exps(stage, 2 * v + 2)
                            exps(stage, 2 * v + 3)
                        if v:
                            sub_mean(v - 1)
                        probs_out(stage, v)
                        head_out(stage, v)
                    sub_mean(n - 1)
                    for v in range(n):
                        act.wait_ge(sub_inv, v + 1)
                        nc.scalar.activation(proj[:, KT + v, :], proj[:, KT + v, :], ACT.Sqrt).then_inc(sub_root, 1)
                        if v:
                            sub_high(v - 1)
                    sub_high(n - 1)
                    return
                probs_out(stage, 0)
                for v in range(n):
                    if v + 3 < n:
                        exps(stage, v + 3)
                    if v + 1 < n:
                        probs_out(stage, v + 1)
                    head_out(stage, v)

            for k in range(0, KT, 2):
                act.wait_ge(x_turned, k + 1)
                nc.scalar.activation(xres[:, k, :], bank[0][:, :], ACT.Copy).then_inc(bank_free[0], 1)
            act.wait_ge(gains_turned, 1)
            nc.scalar.activation(gains[:, :], bank[5][:, 0:P], ACT.Copy).then_inc(rows_out, 1)
            act.wait_ge(rows_out, 1)
            hi(0)
            hi(1)
            squared_input(stages[0])

            def channel_rows():
                act.wait_ge(rows_turned, 1 + 2 * DEPTH)
                nc.scalar.activation(g_few[:, :], bank[7][:, 4 * T // 5:4 * T // 5 + DEPTH + 1], ACT.Copy).then_inc(rows_out, 1)
                for i in range(2 * DEPTH):
                    nc.scalar.activation(conv[:, i // 2, 2 * (i % 2):2 * (i % 2) + 2, :],
                                         bank[7][:, 4 * FB * i:4 * FB * (i + 1)].rearrange("p (c j) -> p c j", c=2),
                                         ACT.Copy).then_inc(rows_out, 1)
                for r, (_, _, heads) in enumerate(TABLES):
                    for a, w in ((0, T), (1, P)):
                        act.wait_ge(tab_mm, 2 * r + a + 1)
                        nc.scalar.activation(brow[r][0:heads, T * a:T * a + w], bank[5 + a][0:heads, 0:w],
                                             ACT.Copy).then_inc(tab_row, 1)
                act.wait_ge(lam_ready, 1)
                nc.scalar.activation(lam_e[:, :], lam_e[:, :], ACT.Exp).then_inc(lam_ready, 1)

            for name in stages:
                c = BASE[name]
                if name in CHAINED:
                    squared_input(name)
                if name == "final":
                    root(name, D)
                    continue
                hi(c + 2)
                if name in SQUARED:
                    hi(c + 3)
                root(name, D)
                if name not in SQUARED:
                    hi(c + 3)
                if name == stages[0]:
                    channel_rows()
                if kind(name) == "ffn":
                    gated_ff(name)
                elif kind(name) == "mix":
                    l = MIX[name]
                    for i, cb in enumerate(W_IN_ORDER):
                        if i >= 2:
                            hi(c + i + 2)
                        if cb in (KI, KA):
                            wait_evacuated(act, c + i)
                            if cb == KA:
                                nc.scalar.activation(k_swap[0:HD, :], proj[HD:P, KA, :], ACT.Copy)
                            nc.scalar.activation((k_idx if cb == KI else k_swap)[HD:P, :], proj[0:HD, cb, :],
                                                 ACT.Copy).then_inc(shifted, 1)
                        if cb == CKV:
                            wait_evacuated(act, c + i)
                            nc.scalar.activation(sq[0][:, :], proj[:, CKV, :], ACT.Square).then_inc(sq_ready, 1)
                        if i in (3, 4, 5):
                            t = i - 2
                            w = P * (t + 1)
                            act.wait_ge(dots_ready, 3 * l + t)
                            if t > 1:
                                act.wait_ge(score_ready, 3 * l + t - 1)
                            for h in range(HI):
                                ins = nc.scalar.activation(rel[:, h, 0:w], DOTS[h][:, 0:w], ACT.Relu, scale=SCALE)
                            ins.then_inc(rel_ready, 1)
                        if i == 8:
                            root("ckv_" + name, P)
                        if i == 14:
                            act.wait_ge(kvup_done, l + 1)
                            nc.scalar.activation(k_sp[0:HD, :], OUT[0:HD, :], ACT.Copy)
                            nc.scalar.activation(k_sp[HD:P, :], OUT[0:HD, :], ACT.Copy)
                            nc.scalar.activation(v_sp_t[HD:P, :], OUT[HD:P, :], ACT.Copy).then_inc(kv_ready, 1)
                    turn_values(name, [v_win[:, :, :], v_blk[:, :, 0:P], v_blk[:, :, P:2 * P], v_sp[:, :, :]])
                    attention(name)
                    down_parts(c + 18, name)
                elif kind(name) == "diff":
                    for i in range(2, 3 * KT):
                        hi(c + i + 2)
                    turn_values(name, [v_all[:, :, P * g:P * (g + 1)] for g in range(KT)])
                    attention(name)
                    down_parts(c + 3 * KT, None)
                elif kind(name) == "fox":
                    z, e, u, cq, ck = (t[FG_ROW:FG_ROW + 16, :] for t in fgate)
                    for i in range(1 + 3 * KT):
                        if i >= 2:
                            hi(c + i + 2)
                        if i == 4:
                            wait_evacuated(act, c)
                            nc.scalar.activation(z, z, ACT.Identity, bias=bf_col[FG_ROW:FG_ROW + 16, :],
                                                 scale=1.0).then_inc(fg_act, 1)
                            act.wait_ge(fg_act, 1)
                            nc.scalar.activation(e, z, ACT.Abs).then_inc(fg_act, 1)
                            act.wait_ge(fg_act, 2)
                            nc.scalar.activation(e, e, ACT.Exp, scale=-1.0).then_inc(fg_act, 1)
                        if i == 6:
                            act.wait_ge(fg_one, 1)
                            nc.scalar.activation(cq, u, ACT.Ln).then_inc(fg_act, 1)
                        if i == 2 * KT - 1:
                            for k in range(KT):
                                h_high("fox_q", k)
                    turn_values(name, [v_all[:, :, P * g:P * (g + 1)] for g in range(KT)])
                    attention(name)
                    down_parts(c + 1 + 3 * KT, None)
                elif kind(name) == "conv":
                    conv_ff(name)
                if name in CHAINED:
                    wait_evacuated(act, out_units[name] + KT - 1)
                    nc.scalar.activation(sq[1][:, :], acc[:, KT - 1, :], ACT.Square).then_inc(sq_ready, 1)
                    root("post_" + name, D)
            for t in range(NT):
                for a in range(2):
                    act.wait_ge(y_turned, 2 * t + a + 1)
                    nc.scalar.activation(xtok[:, t, T * a:T * (a + 1)], bank[3 + 2 * (t % 2) + a][:, :],
                                         ACT.Copy).then_inc(y_out, 1)

        @block.vector
        def _(dve):
            steps = [0]

            def mark(ins):
                steps[0] += 1
                ins.then_inc(dve_step, 1)
                return steps[0]

            def chain(ins):
                dve.wait_ge(dve_step, mark(ins))

            def lo(c, j=0):
                if c >= len(UNIT):
                    return
                nk, cols = UNIT[c]
                dve.wait_ge(hi_ready, c + 1 + 2 * j)
                nc.vector.tensor_tensor(w_lo[c % 2][:, 0:nk, 0:cols], raw[c % 2][:, 0:nk, 0:cols],
                                        w_hi[c % 2][:, 0:nk, 0:cols].bitcast(f32), ALU.subtract).then_inc(lo_ready, 1)

            def invert(name):
                dve.wait_ge(rms_ready, ROOT[name] + 1)
                dst = rstd if name in BASE else rstd2
                nc.vector.reciprocal(dst[:, :], rms[:, :]).then_inc(rstd_ready, 1)
                dve.wait_ge(rstd_ready, ROOT[name] + 1)

            def h_low(name, k):
                g, l = PRE_GAIN[name]
                dve.wait_ge(hhi_ready, KT * PRE[name] + k + 1)
                nc.vector.scalar_tensor_tensor(h_lo[:, k, :], xres[:, k, :], gain(g, l, k), h_hi[:, k, :].bitcast(f32),
                                               ALU.mult, ALU.subtract).then_inc(h_ready, 1)

            def post(name):
                g, l = POST_GAIN[name]
                invert("post_" + name)
                lag = 2
                for k in range(KT + lag):
                    if k < KT:
                        if k >= 4:
                            dve.wait_ge(x_done, X_FIRST[name] + k - 3)
                        nc.vector.scalar_tensor_tensor(norm_t[k % 4][:, :], acc[:, k, :], gain(g, l, k), rstd2[:, :],
                                                       ALU.mult, ALU.mult).then_inc(t_ready, 1)
                    if k >= lag and name in NEXT:
                        h_low(NEXT[name], k - lag)

            def divided(c, dst, j=0, rows=slice(0, P)):
                dve.wait_ge(mm_done, c + 1 + 2 * j)
                nc.vector.tensor_tensor(dst, result(c)[rows, :], rstd[rows, :], ALU.mult).then_inc(bank_free[c % 2], 1)

            def act_low(count, jj):
                dve.wait_ge(acthi_ready, count)
                nc.vector.tensor_tensor(act_lo[:, DS(jj, 1), :], prod[:, :].rearrange("p (o n) -> p o n", o=1),
                                        act_hi[:, DS(jj, 1), :].bitcast(f32), ALU.subtract).then_inc(act_ready, 1)

            def output_gemm(c, how, name):
                def take(c, n, j=0):
                    b = c % 2
                    got = bank[b][:, :].rearrange("p (o n) -> p o n", o=1)
                    dve.wait_ge(mm_done, c + 1 + 2 * j)
                    if how == "half":
                        ins = nc.vector.scalar_tensor_tensor(xres[:, DS(n, 1), :], got, 0.5, xres[:, DS(n, 1), :],
                                                             ALU.mult, ALU.add)
                    elif how == "add":
                        ins = nc.vector.tensor_tensor(xres[:, DS(n, 1), :], got, xres[:, DS(n, 1), :], ALU.add)
                    elif how == "set":
                        ins = nc.vector.tensor_scalar(acc[:, DS(n, 1), :], got, 1.0, None, ALU.mult)
                    else:
                        ins = nc.vector.tensor_tensor(acc[:, DS(n, 1), :], got, acc[:, DS(n, 1), :], ALU.add)
                    ins.then_inc(bank_free[b], 1)

                with dve.Fori(0, KT // 2 - 1) as j:
                    for s in range(2):
                        take(c + s, 2 * j + s, j)
                        lo(c + 2 + s, j)
                follow = FOLLOW.get(name)
                take(c + KT - 2, KT - 2)
                lo(c + KT)
                if follow:
                    for k in range(KT - 1):
                        h_low(follow, k)
                take(c + KT - 1, KT - 1)
                if follow:
                    h_low(follow, KT - 1)
                lo(c + KT + 1)

            def gated_ff(name):
                for hf in range(HALVES):
                    c = BASE[name] + 30 * hf
                    a0 = FF[name] + FH * hf


                    def pair(j):
                        at, jj = (c + 2 * j, 0) if isinstance(j, int) else (c + 2, j - 1)
                        divided(at, scaled_g[:, :], jj)
                        if at not in FIRST:
                            lo(at + 2, jj)
                        dve.wait_ge(silu_ready, a0 - CONV_FF[name] + 1 + j)
                        nc.vector.tensor_tensor(gate_r[:, :], gated[:, :], rstd[:, :], ALU.mult).then_inc(gate_ready, 1)
                        dve.wait_ge(gate_ready, a0 - CONV_FF[name] + 1 + j)
                        dve.wait_ge(mm_done, c + 2 + 2 * j)
                        nc.vector.tensor_tensor(prod[:, :], gate_r[:, :], result(at + 1)[:, :],
                                                ALU.mult).then_inc(bank_free[(c + 1) % 2], 1)
                        if at not in FIRST:
                            lo(at + 3, jj)
                        act_low(a0 + 1 + j, j)

                    if hf == 0:
                        pair(0)
                    with dve.Fori(1 - hf, FH - 1) as j:
                        pair(j)
                    pair(FH - 1)
                    output_gemm(c + 2 * FH, "half", name if hf else None)

            def conv_ff(name):
                l = int(name[-1])
                for hf in range(HALVES):
                    c = BASE[name] + 30 * hf
                    a0, cv = FF[name] + FH * hf, CV[name] + FH * hf

                    def taps(dst, src, ch, count):
                        dve.wait_ge(tap_ready, count)
                        nc.vector.scalar_tensor_tensor(dst[:, 1:T], src[:, 0:T - 1], conv[:, l, 1, DS(ch, 1)],
                                                       dst[:, 1:T], ALU.mult, ALU.add).then_inc(conv_step, 1)
                        dve.wait_ge(conv_step, count)
                        nc.vector.scalar_tensor_tensor(dst[:, 2:T], src[:, 0:T - 2], conv[:, l, 0, DS(ch, 1)],
                                                       dst[:, 2:T], ALU.mult, ALU.add).then_inc(conv_done, 1)

                    def pair(j, first=False):
                        at, jj = (c + 2 * j, 0) if isinstance(j, int) else (c + 2, j - 1)
                        if not first:
                            dve.wait_ge(prod_ready, cv + j)
                        divided(at, scaled_g[:, :], jj)
                        if at not in FIRST:
                            lo(at + 2, jj)
                        if not first:
                            act_low(a0 + j, j - 1)
                        taps(tap_g, scaled_g, hf * FH + j, 2 * cv + 1 + 2 * j)
                        divided(at + 1, scaled_v[:, :], jj)
                        if at not in FIRST:
                            lo(at + 3, jj)
                        taps(tap_v, scaled_v, FB + hf * FH + j, 2 * cv + 2 + 2 * j)
                        dve.wait_ge(conv_done, 2 * cv + 2 + 2 * j)
                        if not first:
                            dve.wait_ge(act_ready, a0 + j)
                        dve.wait_ge(gelu_ready, cv + 1 + j)
                        nc.vector.tensor_tensor(prod[:, :], gated[:, :], tap_v[:, :], ALU.mult).then_inc(prod_ready, 1)

                    pair(0, first=True)
                    with dve.Fori(1, FH - 1) as j:
                        pair(j)
                    pair(FH - 1)
                    act_low(a0 + FH, FH - 1)
                    output_gemm(c + 2 * FH, "set" if hf == 0 else "sum", None)

            def index_scores(name, t):
                l, w = MIX[name], P * (t + 1)
                dst = score[:, off(t):off(t + 1)]
                dve.wait_ge(rel_ready, 3 * l + t)
                chain(nc.vector.tensor_scalar(dst, rel[:, 0, 0:w], w_idx[:, t, 0:1], None, ALU.mult))
                for h in range(1, HI):
                    ins = nc.vector.scalar_tensor_tensor(dst, rel[:, h, 0:w], w_idx[:, t, h:h + 1], dst, ALU.mult, ALU.add)
                    if h < HI - 1:
                        chain(ins)
                ins.then_inc(score_ready, 1)

            EARLY_ROUNDS = 35
            LATE = 3 * (TOPK // 8) - EARLY_ROUNDS

            def topk_rounds(name, first, last):
                per = TOPK // 8
                for n in range(first, last):
                    t, r = 1 + n // per, n % per
                    tile = score[:, off(t):off(t + 1)]
                    if r == 0:
                        dve.wait_ge(score_masked, 3 * MIX[name] + t)
                    chain(nc.vector.max(top8[:, :], tile))
                    chain(nc.vector.match_replace(tile, top8[:, :], tile, TAKEN))
                    if r == per - 1:
                        nc.vector.tensor_scalar(tile, tile, TAKEN / 2, MASKED / SCALE, ALU.is_gt,
                                                ALU.mult).then_inc(pen_ready, 1)

            def bias_max(stage, n):
                job, g = softmax_job(stage, n), JOB[stage] + n
                if n == 0 and stage in MIX:
                    dve.wait_ge(tab_back, 32)
                if n == 0 and stage == "diff":
                    dve.wait_ge(tab_back, 16 * (3 if MIX else 1))
                for i in range(NT):
                    w = keys(job, i)[1]
                    if "sparse" in job and i:
                        dve.wait_ge(penb_ready, 12 * MIX[stage] + 3 * job["sparse"] + i)
                    if g:
                        dve.wait_ge(p_ready, NT * (g - 1) + i + 1)
                    dve.wait_ge(s_ready, NT * g + i + 1)
                    floor = nsinks[:, MIX[stage], n:n + 1] if job["window"] else -TAKEN
                    nc.vector.tensor_tensor_reduce(biased[:, off(i):off(i) + w], SCORES[i][:, 0:w], job["bias"](i), -SCALE,
                                                   floor, ALU.add, ALU.min, nmax[:, g % 4, i:i + 1]).then_inc(s_biased, 1)
                if job["window"]:
                    dve.wait_ge(s_biased, NT * (g + 1))
                    nc.vector.tensor_scalar(sink_e[:, g % 4, :], nmax[:, g % 4, :], sinks[:, MIX[stage], n:n + 1], None,
                                            ALU.add).then_inc(sinkin_ready, 1)

            def invert_sums(stage, v):
                if stage == "diff":
                    dve.wait_ge(p_ready, NT * (JOB[stage] + 2 * v + 1))
                    nc.vector.reciprocal(recip[:, 2 * (v % 2), :], psum_r[:, 2 * (v % 2), :]).then_inc(recip_ready, 1)
                    return
                job, g = softmax_job(stage, v), JOB[stage] + v
                dve.wait_ge(p_ready, NT * (g + 1))
                if job["window"]:
                    dve.wait_ge(sink_ready, HA * MIX[stage] + v + 1)
                    chain(nc.vector.tensor_tensor(psum_r[:, g % 4, :], psum_r[:, g % 4, :], sink_e[:, g % 4, :], ALU.add))
                nc.vector.reciprocal(recip[:, g % 4, :], psum_r[:, g % 4, :]).then_inc(recip_ready, 1)
                dve.wait_ge(recip_ready, HEAD[stage] + v + 1)
                later_tiles(stage, v).then_inc(pl_ready, 1)

            def later_tiles(stage, n):
                ring = PROBS[kind(stage)]
                for i in range(NT // 2, NT):
                    tile = ring[n % len(ring)][:, off(i):off(i) + keys(softmax_job(stage, n), i)[1]]
                    ins = nc.vector.tensor_scalar(tile, tile, recip[:, n % 4, i:i + 1], None, ALU.mult)
                return ins

            def difference(v):
                m = 2 * (v % 2)
                a, b = PROBS["diff"][m:m + 2]
                dve.wait_ge(p_ready, NT * (JOB["diff"] + 2 * v + 2))
                chain(nc.vector.reciprocal(recip[:, m + 1, :], psum_r[:, m + 1, :]))
                chain(nc.vector.tensor_scalar(recip[:, m + 1, :], recip[:, m + 1, :], nlam[:, 0:1], None, ALU.mult))
                chain(later_tiles("diff", 2 * v))
                dve.wait_ge(first_ready, v + 1)
                for i in range(NT):
                    ins = nc.vector.scalar_tensor_tensor(a[:, off(i):off(i + 1)], b[:, off(i):off(i + 1)],
                                                         recip[:, m + 1, i:i + 1], a[:, off(i):off(i + 1)], ALU.mult, ALU.add)
                ins.then_inc(pn_ready, 1)

            def probs_out(stage, v):
                g = HEAD[stage] + v
                w1, w3 = (turned_width(stage, v, b) for b in TURN_GROUPS[1])
                dve.wait_ge(pt_turned, len(TURN_GROUPS) * g + 2)
                if g:
                    dve.wait_ge(pv_done, g)
                if w1 + w3 == T:
                    nc.vector.tensor_copy(probs_t[:, T:2 * T], TURN[1][:, :]).then_inc(pt_dve, 1)
                else:
                    nc.vector.tensor_copy(probs_t[:, T:T + w1], TURN[1][:, 0:w1])
                    nc.vector.tensor_copy(probs_t[:, 2 * T - P:2 * T], TURN[1][:, T - P:T]).then_inc(pt_dve, 1)

            def head_out(stage, v):
                if stage != "diff" and v % 2:
                    dve.wait_ge(ohi_ready, OUTB[stage] + v // 2 + 1)
                    nc.vector.tensor_tensor(h_lo[:, v // 2, :], OUT[:, :], h_hi[:, v // 2, :].bitcast(f32),
                                            ALU.subtract).then_inc(o_ready, 1)

            def sub_invert(v):
                dve.wait_ge(sub_out, v + 1)
                nc.vector.reciprocal(proj[:, KT + v, :], proj[:, KT + v, :]).then_inc(sub_inv, 1)

            def sub_normalise(v):
                dve.wait_ge(sub_root, v + 1)
                nc.vector.scalar_tensor_tensor(proj[:, 2 * KT + v, :], proj[:, v, :], g_sub, proj[:, KT + v, :],
                                               ALU.mult, ALU.mult).then_inc(sub_norm, 1)

            def sub_low(v):
                dve.wait_ge(ohi_ready, OUTB["diff"] + v + 1)
                nc.vector.tensor_tensor(h_lo[:, v, :], proj[:, 2 * KT + v, :], h_hi[:, v, :].bitcast(f32),
                                        ALU.subtract).then_inc(o_ready, 1)

            def attention(stage):
                n = N_HEADS[stage]
                bias_max(stage, 0)
                bias_max(stage, 1)
                invert_sums(stage, 0)
                if stage == "diff":
                    for v in range(n):
                        difference(v)
                        if v + 1 < n:
                            bias_max(stage, 2 * v + 2)
                            bias_max(stage, 2 * v + 3)
                            invert_sums(stage, v + 1)
                        probs_out(stage, v)
                        if v:
                            sub_invert(v - 1)
                    sub_invert(n - 1)
                    for v in range(n):
                        sub_normalise(v)
                        if v:
                            sub_low(v - 1)
                    sub_low(n - 1)
                    return
                bias_max(stage, 2)
                invert_sums(stage, 1)
                probs_out(stage, 0)
                for v in range(n):
                    if v + 2 < n:
                        invert_sums(stage, v + 2)
                    if v + 3 < n:
                        bias_max(stage, v + 3)
                    if v + 1 < n:
                        probs_out(stage, v + 1)
                    head_out(stage, v)
                    if stage in MIX and v < HA:
                        topk_rounds(stage, EARLY_ROUNDS + LATE * v // HA, EARLY_ROUNDS + LATE * (v + 1) // HA)

            for k in range(1, KT, 2):
                dve.wait_ge(x_turned, k + 1)
                nc.vector.tensor_copy(xres[:, k, :], bank[1][:, :]).then_inc(bank_free[1], 1)
            lo(0)
            lo(1)
            for k in range(KT):
                h_low(stages[0], k)

            def small_values():
                dve.wait_ge(rows_out, 2 + 2 * DEPTH)
                dve.wait_ge(small_in, 16 * N_SMALL)
                chain(nc.vector.tensor_scalar(nsinks[:, :, :], sinks[:, :, :], -1.0, None, ALU.mult))
                chain(nc.vector.tensor_scalar(g_sub, g_sub, 1.0 - LAMBDA_INIT, None, ALU.mult))
                chain(nc.vector.tensor_tensor(lam_t[:, :, :], lam_in[:, 0:4:2, :], lam_in[:, 1:4:2, :], ALU.mult))
                nc.vector.reduce_sum(lam_e[:, :], lam_t[:, :, :], AX.X).then_inc(lam_ready, 1)

            def make_lambda():
                dve.wait_ge(lam_ready, 2)
                chain(nc.vector.tensor_tensor(nlam[:, :], lam_e[:, 1:2], lam_e[:, 0:1], ALU.subtract))
                chain(nc.vector.tensor_scalar(nlam[:, :], nlam[:, :], -LAMBDA_INIT, None, ALU.add))

            for name in stages:
                c = BASE[name]
                if name != "final":
                    lo(c + 2)
                    if name in SQUARED:
                        lo(c + 3)
                invert(name)
                if name != "final" and name not in SQUARED:
                    lo(c + 3)
                if name == "final":
                    for k in range(KT + 1):
                        if k < KT:
                            nc.vector.scalar_tensor_tensor(xres[:, k, :], xres[:, k, :], gain("final_norm", 0, k), rstd[:, :],
                                                           ALU.mult, ALU.mult).then_inc(x_done, 1)
                        if k and name in NEXT:
                            h_low(NEXT[name], k - 1)
                    continue
                if name == stages[0]:
                    small_values()
                if kind(name) == "ffn":
                    gated_ff(name)
                elif kind(name) == "mix":
                    l = MIX[name]
                    for i, cb in enumerate(W_IN_ORDER):
                        cols = slice(0, UNIT[c + i][1])
                        divided(c + i, proj[cols, cb, :], 0, cols)
                        if i >= 2:
                            lo(c + i + 2)
                        if i == 4:
                            dve.wait_ge(idxw_turned, l + 1)
                            chain(nc.vector.tensor_scalar(w_idx[:, 1:NT, :],
                                                          OUT[:, 0:HI * (NT - 1)].rearrange("p (t h) -> p t h", h=HI),
                                                          HI ** -0.5, None, ALU.mult))
                        if i in (4, 5, 6):
                            index_scores(name, i - 3)
                        if i == 9:
                            invert("ckv_" + name)
                            nc.vector.scalar_tensor_tensor(ckv_n[:, :], proj[:, CKV, :], g_ckv[:, l:l + 1], rstd2[:, :],
                                                           ALU.mult, ALU.mult).then_inc(ckvn_ready, 1)
                        if i >= 5:
                            topk_rounds(name, min(3 * (i - 5), EARLY_ROUNDS), min(3 * (i - 4), EARLY_ROUNDS))
                    attention(name)
                    output_gemm(c + 18, "add", name)
                elif kind(name) == "diff":
                    make_lambda()
                    for i in range(3 * KT):
                        divided(c + i, proj[:, i, :])
                        if i >= 2:
                            lo(c + i + 2)
                    attention(name)
                    output_gemm(c + 3 * KT, "set", None)
                elif kind(name) == "fox":
                    z, e, u, cq, ck = (t[FG_ROW:FG_ROW + 16, :] for t in fgate)
                    for i in range(1 + 3 * KT):
                        if i == 0:
                            gates = slice(FG_ROW, FG_ROW + 16)
                            divided(c, z, 0, gates)
                        else:
                            divided(c + i, proj[:, i - 1, :])
                        if i >= 2:
                            lo(c + i + 2)
                        if i == 5:
                            dve.wait_ge(fg_act, 3)
                            nc.vector.tensor_scalar(u, e, 1.0, None, ALU.add).then_inc(fg_one, 1)
                            dve.wait_ge(fg_one, 1)
                            chain(nc.vector.tensor_scalar(ck, u, -1.0, None, ALU.add))
                            chain(nc.vector.tensor_tensor(e, e, ck, ALU.subtract))
                        if i == 7:
                            dve.wait_ge(fg_act, 4)
                            chain(nc.vector.reciprocal(u, u))
                            chain(nc.vector.tensor_tensor(e, e, u, ALU.mult))
                            chain(nc.vector.tensor_tensor(e, e, cq, ALU.add))
                        if i == 9:
                            chain(nc.vector.scalar_tensor_tensor(z, z, 0.0, e, ALU.min, ALU.subtract))
                            chain(nc.vector.tensor_scalar(z, z, 1.0 / SCALE, None, ALU.mult))
                            chain(nc.vector.memset(u, 1.0))
                            chain(nc.vector.tensor_tensor_scan(cq, u, z, 0.0, ALU.mult, ALU.add))
                        if i == 11:
                            high, low, minus_high, minus_low = (t[FG_ROW:FG_ROW + 16, :] for t in fparts)
                            chain(nc.vector.tensor_copy(high, cq))
                            chain(nc.vector.tensor_tensor(low, cq, high.bitcast(f32), ALU.subtract))
                            chain(nc.vector.tensor_scalar(minus_high, high.bitcast(f32), -1.0, None, ALU.mult))
                            nc.vector.tensor_scalar(minus_low, low.bitcast(f32), -1.0, None, ALU.mult).then_inc(fg_ready, 1)
                        if i == 2 * KT - 1:
                            for k in range(KT):
                                h_low("fox_q", k)
                    attention(name)
                    output_gemm(c + 1 + 3 * KT, "set", None)
                elif kind(name) == "conv":
                    conv_ff(name)
                if name in CHAINED:
                    post(name)

        @block.tensor
        def _(pe):
            def gemm(c, x_hi, x_lo, ready, count, j=0, release=False):
                b = c % 2
                nk, cols = UNIT[c]
                pe.wait_ge(lo_ready, c + 1 + 2 * j)
                if c - 2 not in FIRST:
                    pe.wait_ge(bank_free[b], XT_USES + c // 2 + j)
                for k in range(nk):
                    pe.wait_ge(ready, count + k + 1)
                    for n, (w, x) in enumerate(((w_hi, x_hi), (w_hi, x_lo), (w_lo, x_hi))):
                        mm = nc.tensor.matmul(result(c)[0:cols, :], w[b][:, k, 0:cols], x[:, k, :],
                                              start=(k == 0 and n == 0), stop=(k == nk - 1 and n == 2))
                    if release and k < nk - 1:
                        mm.then_inc(h_used, 1)
                mm.then_inc(mm_done, 1)

            def gemm_both(c, count):
                for s in range(2):
                    pe.wait_ge(lo_ready, c + s + 1)
                    pe.wait_ge(bank_free[(c + s) % 2], XT_USES + (c + s) // 2)
                for k in range(KT):
                    pe.wait_ge(h_ready, count + k + 1)
                    for s in range(2):
                        b = (c + s) % 2
                        cols = UNIT[c + s][1]
                        for n, (w, x) in enumerate(((w_hi, h_hi), (w_hi, h_lo), (w_lo, h_hi))):
                            mm = nc.tensor.matmul(result(c + s)[0:cols, :], w[b][:, k, 0:cols], x[:, k, :],
                                                  start=(k == 0 and n == 0), stop=(k == KT - 1 and n == 2))
                        if k == KT - 1:
                            mm.then_inc(mm_done, 1)

            def first_units(name, c, count):
                if name in SQUARED:
                    gemm_both(c, count)
                    stat_of_squares(name, [SQUARES[name][:, k, :] for k in range(KT)])
                else:
                    gemm(c, h_hi, h_lo, h_ready, count)
                    stat_of_sums(name)
                    gemm(c + 1, h_hi, h_lo, h_ready, count)

            def gemm_pairs(c, n, x_hi, x_lo, ready, count, first=0):
                with pe.Fori(first, n // 2) as j:
                    for s in range(2):
                        gemm(c + 2 * first + s, x_hi, x_lo, ready, count, j - first if first else j)

            def stat_free(name):
                if name in ROOT and ROOT[name]:
                    pe.wait_ge(rms_ready, ROOT[name])

            def stat_of_sums(name):
                stat_free(name)
                pe.wait_ge(ssq_ready, POOL_SUM[name] + 1)
                alone = name not in SQ_FIRST
                mm = nc.tensor.matmul(STATB[:, :], ones[:, :], ssq[:, :], start=True, stop=alone)
                if not alone:
                    pe.wait_ge(sq_ready, SQ_FIRST[name] + 1)
                    mm = nc.tensor.matmul(STATB[:, :], ones[:, :], sq[1][:, :], start=False, stop=True)
                mm.then_inc(sum_ready, 1)

            def stat_of_squares(name, blocks):
                stat_free(name)
                for k, b in enumerate(blocks):
                    pe.wait_ge(sq_ready, SQ_FIRST[name] + k + 1)
                    mm = nc.tensor.matmul(STATB[:, :], ones[:, :], b, start=(k == 0), stop=(k == len(blocks) - 1))
                mm.then_inc(sum_ready, 1)

            def turn_values(stage, groups):
                for g, (src, width, rows) in enumerate(groups):
                    if g >= 2:
                        pe.wait_ge(vt_ready, VT_FIRST[stage] + g - 1)
                    for b in range(NT):
                        mm = nc.tensor.transpose(TURN[g % 2][:, width * b:width * (b + 1)], src[:, P * b:P * (b + 1)],
                                                 ident[rows, rows])
                    mm.then_inc(vt_turned, 1)
                pe.wait_ge(vt_ready, VT_FIRST[stage] + len(groups))

            def scores(stage, n):
                job, g = softmax_job(stage, n), JOB[stage] + n
                for i in range(NT):
                    first, w = keys(job, i)
                    if g:
                        pe.wait_ge(s_biased, NT * (g - 1) + i + 1)
                    mm = nc.tensor.matmul(SCORES[i][:, 0:w], job["q"][:, P * i:P * (i + 1)], job["k"][:, first:first + w],
                                          start=True, stop="decay" not in job)
                    if "decay" in job:
                        row, col = 32 * (job["decay"] % 4), job["decay"] // 4
                        mm = nc.tensor.matmul(SCORES[i][:, 0:w], decay_q[row:row + 4, col, P * i:P * (i + 1)],
                                              decay_k[row:row + 4, col, first:first + w], start=False, stop=True,
                                              tile_position=(row, 0))
                    mm.then_inc(s_ready, 1)

            def sub_sums(v):
                pe.wait_ge(o_sq, v + 1)
                nc.tensor.matmul(OUT[:, :], mean_p[:, :], proj[:, KT + v, :], start=True, stop=True).then_inc(sub_sum, 1)

            def turn(stage, v):
                g = HEAD[stage] + v
                n = 2 * v if stage == "diff" else v
                job = softmax_job(stage, n)
                ring = PROBS[kind(stage)]
                src = ring[n % len(ring)]
                pe.wait_ge(pn_ready, g + 1)
                if stage != "diff":
                    pe.wait_ge(pl_ready, PL_FIRST[stage] + v + 1)
                if g:
                    pe.wait_ge(pt_act, 2 * g)
                    pe.wait_ge(pt_dve, g)
                for bank_t, blocks in zip(TURN, TURN_GROUPS):
                    for b in blocks:
                        last = min(b + 1, NT - 1) if job["window"] else NT - 1
                        for i in range(b, last + 1):
                            col, to = off(i) + P * b - keys(job, i)[0], TURN_AT[b] + P * (i - b)
                            mm = nc.tensor.transpose(bank_t[:, to:to + P], src[:, col:col + P], ident[:, :])
                    mm.then_inc(pt_turned, 1)

            def values(stage, v):
                g = HEAD[stage] + v
                window = softmax_job(stage, 2 * v if stage == "diff" else v)["window"]
                rows = slice(0, P) if stage == "diff" else slice(HD * (v % 2), HD * (v % 2) + HD)
                if stage == "diff":
                    if v:
                        pe.wait_ge(sub_out, v)
                elif v % 2 == 0 and v:
                    pe.wait_ge(o_ready, OUTB[stage] + v // 2)
                pe.wait_ge(pt_act, 2 * g + 2)
                pe.wait_ge(pt_dve, g + 1)
                for b in range(NT):
                    at = SLOT_AT[b]
                    if window:
                        cols = slice(P * b, P * (b + 1))
                        if b:
                            before = SLOT_AT[b - 1] + P
                            nc.tensor.matmul(OUT[rows, cols], head_values(stage, v, b - 1), probs_t[:, before:before + P],
                                             start=True, stop=False)
                        mm = nc.tensor.matmul(OUT[rows, cols], head_values(stage, v, b), probs_t[:, at:at + P],
                                              start=(b == 0), stop=True)
                    else:
                        mm = nc.tensor.matmul(OUT[rows, P * b:T], head_values(stage, v, b), probs_t[:, at:at + T - P * b],
                                              start=(b == 0), stop=(b == NT - 1))
                mm.then_inc(pv_done, 1)

            def attention(stage):
                n = N_HEADS[stage]
                for m in range(2 if stage == "diff" else 3):
                    scores(stage, m)
                if stage == "diff":
                    for v in range(n):
                        if v + 1 < n:
                            scores(stage, 2 * v + 2)
                            scores(stage, 2 * v + 3)
                        if v:
                            sub_sums(v - 1)
                        turn(stage, v)
                        values(stage, v)
                    sub_sums(n - 1)
                    return
                turn(stage, 0)
                for v in range(n):
                    if v + 3 < n:
                        scores(stage, v + 3)
                    if v + 1 < n:
                        turn(stage, v + 1)
                    values(stage, v)

            pe.wait_ge(consts, 1)
            pe.wait_ge(x_in, 16)
            for k in range(KT):
                if k >= 2:
                    pe.wait_ge(bank_free[k % 2], k // 2)
                for t in range(NT):
                    mm = nc.tensor.transpose(bank[k % 2][:, P * t:P * (t + 1)], xtok[:, t, P * k:P * (k + 1)], ident[:, :])
                mm.then_inc(x_turned, 1)
            pe.wait_ge(gains_in, 16 * len(GAINS))
            nc.tensor.transpose(bank[5][:, 0:P], gain_rows[:, :], ident[:, :]).then_inc(gains_turned, 1)

            def channel_rows():
                pe.wait_ge(rows_in, 16 * N_ROWS)
                pe.wait_ge(rows_out, 1)
                nc.tensor.transpose(bank[7][:, 4 * T // 5:4 * T // 5 + DEPTH + 1], few_rows[:, :],
                                    ident[0:DEPTH + 1, 0:DEPTH + 1]).then_inc(rows_turned, 1)
                for i in range(2 * DEPTH):
                    nc.tensor.transpose(bank[7][:, 4 * FB * i:4 * FB * (i + 1)], conv_rows[i][:, :],
                                        ident[0:4 * FB, 0:4 * FB]).then_inc(rows_turned, 1)
                pe.wait_ge(small_in, 16 * N_SMALL)
                for r, (tab, hot, heads) in enumerate(TABLES):
                    if r:
                        pe.wait_ge(tab_row, 2 * r)
                    for a, w in ((0, T), (1, P)):
                        nc.tensor.matmul(bank[5 + a][0:heads, 0:w], tab[:, 0:heads], hot[:, T * a:T * a + w],
                                         start=True, stop=True).then_inc(tab_mm, 1)

            for name in stages:
                c = BASE[name]
                if name == "final":
                    stat_of_sums(name)
                    continue
                h0 = KT * PRE[name]
                if kind(name) in ("ffn", "conv"):
                    for hf in range(HALVES):
                        if hf == 0:
                            first_units(name, c, h0)
                            if name == stages[0]:
                                channel_rows()
                            gemm(c + 2, h_hi, h_lo, h_ready, h0)
                            gemm(c + 3, h_hi, h_lo, h_ready, h0)
                        gemm_pairs(c + 30 * hf, 2 * FH, h_hi, h_lo, h_ready, h0, first=0 if hf else 2)
                        gemm_pairs(c + 30 * hf + 2 * FH, KT, act_hi, act_lo, act_ready, FF[name] + FH * hf)
                elif kind(name) == "mix":
                    l = MIX[name]
                    first_units(name, c, h0)
                    for i in range(2, 8):
                        gemm(c + i, h_hi, h_lo, h_ready, h0)
                        if i == 3:
                            wait_evacuated(pe, c)
                            pe.wait_ge(shifted, 2 * l + 1)
                            for t in range(1, NT):
                                mm = nc.tensor.transpose(OUT[:, HI * (t - 1):HI * t], proj[HD:KI_COLS, KI, P * t:P * (t + 1)],
                                                         ident[HD:KI_COLS, HD:KI_COLS])
                            mm.then_inc(idxw_turned, 1)
                            wait_evacuated(pe, c + 2)
                        if 3 <= i <= 5:
                            t = i - 2
                            w = P * (t + 1)
                            if t > 1:
                                pe.wait_ge(rel_ready, 3 * l + t - 1)
                            for h in range(HI):
                                r = HD * (h % 2)
                                mm = nc.tensor.matmul(DOTS[h][:, 0:w], proj[r:r + HD, QI + h // 2, P * t:P * (t + 1)],
                                                      proj[0:HD, KI, 0:w] if r == 0 else k_idx[HD:P, 0:w],
                                                      start=True, stop=True)
                            mm.then_inc(dots_ready, 1)
                    stat_of_squares("ckv_" + name, [sq[0][:, :]])
                    gemm_pairs(c + 8, 6, h_hi, h_lo, h_ready, h0)
                    pe.wait_ge(ckvn_ready, l + 1)
                    pe.wait_ge(score_ready, 3 * l + 1)
                    nc.tensor.matmul(OUT[:, :], w_kvup[:, l, :], ckv_n[:, :], start=True, stop=True).then_inc(kvup_done, 1)
                    gemm_pairs(c + 14, 4, h_hi, h_lo, h_ready, h0)
                    wait_evacuated(pe, c + 16)
                    wait_evacuated(pe, c + 17)
                    pe.wait_ge(shifted, 2 * l + 2)
                    pe.wait_ge(kv_ready, l + 1)
                    every = slice(0, P)
                    turn_values(name, [(proj[:, VA, :], P, every), (proj[:, VB, :], P, every), (proj[:, VB + 1, :], P, every),
                                       (v_sp_t[HD:P, :], HD, slice(HD, P))])
                    attention(name)
                    gemm_pairs(c + 18, KT - 2, h_hi, h_lo, o_ready, OUTB[name])
                    gemm(c + 16 + KT, h_hi, h_lo, o_ready, OUTB[name])
                    gemm(c + 17 + KT, h_hi, h_lo, o_ready, OUTB[name], release=True)
                elif kind(name) == "diff":
                    first_units(name, c, h0)
                    gemm(c + 2, h_hi, h_lo, h_ready, h0)
                    gemm(c + 3, h_hi, h_lo, h_ready, h0)
                    gemm_pairs(c, 3 * KT, h_hi, h_lo, h_ready, h0, first=2)
                    wait_evacuated(pe, c + 3 * KT - 2)
                    wait_evacuated(pe, c + 3 * KT - 1)
                    turn_values(name, [(proj[:, 2 * KT + g, :], P, slice(0, P)) for g in range(KT)])
                    attention(name)
                    gemm_pairs(c + 3 * KT, KT, h_hi, h_lo, o_ready, OUTB[name])
                elif kind(name) == "fox":
                    first_units(name, c, h0)
                    gemm(c + 2, h_hi, h_lo, h_ready, h0)
                    gemm(c + 3, h_hi, h_lo, h_ready, h0)
                    gemm_pairs(c + 4, 2 * KT - 4, h_hi, h_lo, h_ready, h0)
                    gemm(c + 2 * KT, h_hi, h_lo, h_ready, h0, release=True)
                    gemm_pairs(c + 1 + 2 * KT, KT, h_hi, h_lo, h_ready, KT * PRE["fox_q"])
                    wait_evacuated(pe, c + 3 * KT - 1)
                    wait_evacuated(pe, c + 3 * KT)
                    turn_values(name, [(proj[:, KT + g, :], P, slice(0, P)) for g in range(KT)])
                    pe.wait_ge(decay_in, 16 * 64)
                    attention(name)
                    gemm_pairs(c + 1 + 3 * KT, KT, h_hi, h_lo, o_ready, OUTB[name])
                if name in CHAINED:
                    stat_of_sums("post_" + name)
            for t in range(NT):
                for a in range(2):
                    if t >= 2:
                        pe.wait_ge(y_out, 2 * (t - 2) + a + 1)
                    for k in range(4 * a, 4 * a + 4):
                        wait_x(pe, stages[-1] if stages else None, k)
                        mm = nc.tensor.transpose(bank[3 + 2 * (t % 2) + a][:, P * (k % 4):P * (k % 4 + 1)],
                                                 xres[:, k, P * t:P * (t + 1)], ident[:, :])
                    mm.then_inc(y_turned, 1)


_INS = ["x", "rel_bias_table", "ffn1_norm", "ffn1_w_gate", "ffn1_w_up", "ffn1_w_down", "mix_norm", "w_in", "attn_sinks",
        "kv_norm_c", "w_kv_up_c", "w_out", "ffn2_norm", "ffn2_w_gate", "ffn2_w_up", "ffn2_w_down", "final_norm",
        "rel_bias_2", "a_norm_pre_2", "a_norm_post_2", "a_w_qkv_2", "a_lam_q1_2", "a_lam_k1_2", "a_lam_q2_2",
        "a_lam_k2_2", "a_subln_2", "a_w_o_2", "kv_norm_2", "w_kvf_2", "b_f_2", "b_norm_pre_2", "b_norm_post_2",
        "b_w_q_2", "b_w_o_2", "ffn_norm_pre_2", "ffn_norm_post_2", "ffn_w_in_2", "ffn_conv_w_2", "ffn_conv_b_2",
        "ffn_w_out_2"]


def kernel(**inputs):
    import concourse.bacc as bacc
    from concourse.bass_utils import run_bass_kernel_spmd

    nc = bacc.Bacc("TRN2", target_bir_lowering=False, num_devices=1)
    inputs = dict(inputs, onehot_causal=t5_onehot(T), onehot_window=t5_onehot(WINDOW))
    arrays, aps = {}, {}
    for name in _INS + ["onehot_causal", "onehot_window"]:
        a = np.ascontiguousarray(inputs[name])
        arrays[f"in_{name}_dram"] = a
        aps[name] = nc.dram_tensor(f"in_{name}_dram", a.shape, mybir.dt.from_np(a.dtype), kind="ExternalInput").ap()
    out = nc.dram_tensor("out_0_dram", (1, T, D), mybir.dt.float32, kind="ExternalOutput").ap()
    program(nc, aps, out, ALL_STAGES)
    r = run_bass_kernel_spmd(nc, [arrays], core_ids=[0])
    return r.results[0]["out_0_dram"]
```

```python
import math
from contextlib import ExitStack

import numpy as np
import concourse.bass as bass
from concourse import mybir

T, D, F, P = 512, 1024, 2816, 128
DEPTH, HD = 2, 64
KT, NT = D // P, T // P
FB = F // P
HALVES = 2
FH = FB // HALVES
BUCKETS, MAX_DIST, WINDOW = 32, 128, 128
D_IN, D_KVF = 2244, 2064
HA, HB, HC, HI = 8, 4, 4, 4
TOPK = T // 4
SCALE = HD ** -0.5
RMS_EPS, SUBLN_EPS = 1e-6, 1e-5
MASKED = -1e30
TAKEN = -3e38
NEAR = 2 * P
SPAN = T + P
PACK = P * NT * (NT + 1) // 2
LAMBDA_INIT = 0.8 - 0.6 * math.exp(0.0)

QA, KA, VA, QB, KB, VB, QC, CKV, QI, KI = 0, 4, 5, 6, 8, 10, 12, 14, 15, 17
W_IN_ORDER = [KI, QI, QI + 1, CKV] + list(range(CKV))
KI_COLS = D_IN - KI * P
FG_ROW, FG_COLS = 96, 112

GAINS = ["ffn1_norm", "mix_norm", "ffn2_norm", "final_norm", "a_norm_pre_2", "a_norm_post_2", "kv_norm_2",
         "b_norm_pre_2", "b_norm_post_2", "ffn_norm_pre_2", "ffn_norm_post_2"]
GAIN_ROWS = {"ffn1_norm": 2, "mix_norm": 2, "ffn2_norm": 2, "ffn_norm_pre_2": 2, "ffn_norm_post_2": 2}

ALL_STAGES = ["ffn1_0", "mix_0", "ffn2_0", "ffn1_1", "mix_1", "ffn2_1", "final", "diff", "conv_0", "fox", "conv_1"]


def kind(name):
    return "ffn" if name[:3] == "ffn" else name.split("_")[0]


def off(i):
    return P * i * (i + 1) // 2


TURN_GROUPS = [(0,), (1, 3), (2,)]
TURN_AT = {0: 0, 1: 0, 3: T - P, 2: 0}
SLOT_AT = {0: 0, 1: T, 3: 2 * T - P, 2: 2 * T}


def t5_onehot(window):
    dist = T - 1 - np.arange(SPAN)
    n = np.maximum(dist, 0)
    exact = BUCKETS // 2
    large = exact + (np.log(np.maximum(n, 1) / exact) / math.log(MAX_DIST / exact) * (BUCKETS - exact)).astype(np.int64)
    bucket = np.where(n < exact, n, np.minimum(large, BUCKETS - 1))
    hot = np.zeros((BUCKETS + 1, SPAN), np.float32)
    hot[bucket, np.arange(SPAN)] = 1.0 / SCALE
    hot[BUCKETS] = np.where((dist < 0) | (dist >= window), MASKED / SCALE, 0.0)
    return hot


def program(nc, A, out, stages):
    f32, f32r = mybir.dt.float32, mybir.dt.float32r
    ALU, ACT, AX = mybir.AluOpType, mybir.ActivationFunctionType, mybir.AxisListType
    DS = bass.ds

    UNIT, BASE = [], {}
    UNITS = {
        "ffn": ([(KT, P)] * (2 * FH) + [(FH, P)] * KT) * HALVES,
        "mix": [(KT, KI_COLS)] + [(KT, P)] * 17 + [(KT, P)] * KT,
        "diff": [(KT, P)] * (3 * KT) + [(KT, P)] * KT,
        "conv": ([(KT, P)] * (2 * FH) + [(FH, P)] * KT) * HALVES,
        "fox": [(KT, FG_COLS)] + [(KT, P)] * (3 * KT) + [(KT, P)] * KT,
        "final": [],
    }
    for name in stages:
        BASE[name] = len(UNIT)
        UNIT.extend(UNITS[kind(name)])
    MIX = {n: i for i, n in enumerate(n for n in stages if n[:3] == "mix")}
    N_HEADS = {"mix_0": 16, "mix_1": 16, "diff": 8, "fox": 16}
    XT_USES = KT // 2

    pre_norms = [n for n in stages if n != "final"]
    PRE = {}
    for n in pre_norms:
        PRE[n] = len(PRE)
        if n == "fox":
            PRE["fox_q"] = len(PRE)
    HALF_ROOT, HALF_SQ, half_squares = {}, {}, 0
    STAT, ROOT, POOL_SUM, SQ_FIRST, X_FIRST, NEXT = {}, {}, {}, {}, {}, {}
    squares = half_squares = 0
    HALF_ROOT, HALF_SQ = {}, {}
    for a, b in zip(stages, stages[1:]):
        NEXT[a] = b
    CHAINED = ("diff", "conv_0", "fox", "conv_1")
    SQUARED = ("ffn1_0",) + CHAINED
    HALVED = [b for a, b in NEXT.items() if a in CHAINED]
    for n in stages:
        STAT[n], ROOT[n] = len(STAT), len(ROOT)
        if n in HALVED:
            HALF_ROOT[n], HALF_SQ[n] = len(HALF_ROOT), half_squares
            half_squares += KT
        if n in SQUARED:
            SQ_FIRST[n] = squares
            squares += KT
        else:
            POOL_SUM[n] = len(POOL_SUM)
        if n == "final":
            X_FIRST[n] = KT * len(X_FIRST)
        if n in MIX:
            STAT["ckv_" + n], ROOT["ckv_" + n] = len(STAT), len(ROOT)
            SQ_FIRST["ckv_" + n] = squares
            squares += 1
        if n in CHAINED:
            STAT["post_" + n], ROOT["post_" + n] = len(STAT), len(ROOT)
            POOL_SUM["post_" + n] = len(POOL_SUM)
            SQ_FIRST["post_" + n] = squares
            squares += 2
            HALF_ROOT["post_" + n], HALF_SQ["post_" + n] = len(HALF_ROOT), half_squares
            half_squares += 2
            X_FIRST[n] = KT * len(X_FIRST)
    T_FIRST = {n: KT * i for i, n in enumerate(n for n in stages if n in CHAINED)}
    USED = {n: (KT - 1) * i for i, n in enumerate(n for n in [m for m in stages if m[:4] == "ffn2"] + ["fox_q"])}
    JOB, HEAD, OUTB, VT_FIRST = {}, {}, {}, {}
    jobs = heads = turned = 0
    for n in stages:
        if n in N_HEADS:
            JOB[n], HEAD[n], OUTB[n], VT_FIRST[n] = jobs, heads, KT * len(OUTB), turned
            jobs, heads, turned = jobs + 16, heads + N_HEADS[n], turned + (4 if n in MIX else KT)
    PL_FIRST = {n: 16 * i for i, n in enumerate(n for n in stages if n[:3] in ("mix", "fox"))}
    FF = {n: FB * i for i, n in enumerate(n for n in stages if n[:3] in ("ffn", "con"))}
    CV = {n: FB * i for i, n in enumerate(n for n in stages if n[:4] == "conv")}

    ctx = ExitStack()
    with ctx:
        where = [nc.sbuf_base + (-nc.sbuf_base) % 32]

        def room(size):
            at = where[0]
            where[0] += size + (-size) % 32
            assert where[0] <= nc.sbuf_usable_end, where[0]
            return at

        def put(name, shape, at=None, dt=f32):
            size = 4 * int(np.prod(shape[1:]))
            return nc.alloc_sbuf_tensor_at(name, shape, dt, offset=room(size) if at is None else at)

        def sem(name):
            return ctx.enter_context(nc.semaphore(name))

        xres = put("xres", [P, KT, T])
        h_hi, h_lo = (put(n, [P, KT, T], dt=f32r) for n in ("h_hi", "h_lo"))
        raw = [put(f"w_raw{i}", [P, FH, P]) for i in range(2)]
        w_hi = [put(f"w_hi{i}", [P, FH, P], dt=f32r) for i in range(2)]
        w_lo = [put(f"w_lo{i}", [P, FH, P], dt=f32r) for i in range(2)]

        bias_at = room(4 * (HA * NEAR + (HB + HC) * T))
        bias_win = put("bias_win", [P, HA, NEAR], bias_at)
        bias_far = put("bias_far", [P, HB + HC, T], bias_at + 4 * HA * NEAR)
        bias_diff = put("bias_diff", [P, 8, T], bias_at + 4 * HA * NEAR)
        causal = put("causal", [P, T], bias_at)
        decay_q = put("decay_q", [P, 4, T], bias_at + 4 * T, f32r)
        decay_k = put("decay_k", [P, 4, T], bias_at + 4 * 5 * T, f32r)

        big_at = room(4 * 24 * T)
        act_hi = put("act_hi", [P, FH, T], big_at, f32r)
        act_lo = put("act_lo", [P, FH, T], big_at + 4 * FH * T, f32r)
        proj = put("proj", [P, 24, T], big_at)
        pen_bias = [put(f"pen_bias{i}", [P, PACK], big_at + 4 * (18 * T + i * PACK)) for i in range(2)]

        val_at = room(4 * 8 * T)
        v_win = put("v_win", [P, NT, P], val_at)
        v_blk = put("v_blk", [P, NT, 2 * P], val_at + 4 * T)
        v_sp = put("v_sp", [P, NT, HD], val_at + 4 * 3 * T)
        k_swap = put("k_swap", [P, T], val_at + 4 * 4 * T)
        k_idx = put("k_idx", [P, T], val_at + 4 * 6 * T)
        k_sp = put("k_sp", [P, T], val_at + 4 * 7 * T)
        v_all = put("v_all", [P, NT, D], val_at)
        acc = put("acc", [P, KT, T], val_at)
        xtok, ytok = put("xtok", [P, NT, D], val_at), put("ytok", [P, NT, D], big_at)

        prob_at = room(2 * 4 * PACK)
        score_at = room(4 * PACK)
        pair = [put("probs0", [P, PACK], prob_at), put("probs1", [P, PACK], prob_at + 4 * PACK)]
        third = put("probs2", [P, PACK], score_at)
        in_proj = put("probs2_mix", [P, PACK], big_at + 4 * CKV * T)
        PROBS = {"mix": pair + [in_proj], "fox": pair + [third],
                 "diff": pair + [third, put("probs3", [P, PACK], bias_at)]}
        rel = put("rel", [P, HI, T], prob_at)
        score = put("score", [P, PACK], score_at)
        ckv_n = put("ckv_n", [P, T], prob_at + 4 * HI * T)
        gated = put("gated", [P, T], prob_at)
        gate_r = put("gate_r", [P, T], prob_at + 8 * T)
        tap_g = put("tap_g", [P, T], prob_at + 4 * T)
        tap_v = put("tap_v", [P, T], prob_at + 8 * T)
        prod = put("prod", [P, T], prob_at + 12 * T)
        scaled_g, scaled_v = put("scaled_g", [P, T], prob_at + 16 * T), put("scaled_v", [P, T], score_at)
        norm_t = [put(f"norm_t{i}", [P, T], prob_at + 4 * i * T) for i in range(4)]
        biased_at = room(4 * PACK)
        biased = put("biased", [P, PACK], biased_at)
        sq = [put(f"sq{i}", [P, T], biased_at + 4 * i * T) for i in range(2)]
        sq_last = [sq[1], put("sq_last", [P, T], prob_at + 16 * T)]
        psq = put("psq", [P, T], biased_at)
        fgate = [put(f"fgate{i}", [P, T], prob_at + 4 * i * T) for i in range(5)]
        fparts = [put(f"fparts{i}", [P, T], prob_at + 4 * at * T, f32r) for i, at in enumerate((0, 1, 2, 4))]
        turned_at = room(4 * PACK)
        probs_t = put("probs_t", [P, PACK], turned_at)
        rstd2 = put("rstd2", [P, T], turned_at)
        v_sp_t = put("v_sp_t", [P, T], big_at + 4 * 23 * T)
        ssq, rms, rstd = put("ssq", [P, T]), put("rms", [P, T]), put("rstd", [P, T])

        ident, ones = put("ident", [P, P]), put("ones", [P, P])
        gain_rows, gains = put("gain_rows", [P, P], turned_at), put("gains", [P, P])
        conv_rows = [put(f"conv_rows{i}", [4 * FB, P], turned_at + 4 * P * (1 + i)) for i in range(4)]
        conv = put("conv", [P, DEPTH, 4, 2 * FB])
        onehot = [put(f"onehot{i}", [BUCKETS + 1, SPAN], bias_at + 4 * SPAN * i) for i in range(2)]
        table, table2 = put("table", [BUCKETS + 1, 16]), put("table2", [BUCKETS + 1, 8])
        brow = [put(f"brow{i}", [16, SPAN], bias_at + 4 * SPAN * (2 + i)) for i in range(3)]
        w_kvup = put("w_kvup", [P, DEPTH, P])
        few_rows = put("few_rows", [DEPTH + 1, P], turned_at + 4 * P * 8)
        g_few = put("g_few", [P, DEPTH + 1])
        g_ckv, g_sub = g_few[:, 0:DEPTH], g_few[:, DEPTH:DEPTH + 1]
        sinks, nsinks = put("sinks", [P, DEPTH, HA]), put("nsinks", [P, DEPTH, HA])
        lam_in, lam_t = put("lam_in", [P, 4, HD], turned_at + 4 * P * 5), put("lam_t", [P, 2, HD], turned_at + 4 * P * 7)
        lam_e = put("lam_e", [P, 2])
        nlam = put("nlam", [P, 1])
        spare = put("spare", [P, 1])
        eps_c, sub_eps, mean_p = put("eps_c", [P, 1]), put("sub_eps", [P, 1]), put("mean_p", [P, P])
        nmax, psum_r, recip = (put(n, [P, 4, NT]) for n in ("nmax", "psum_r", "recip"))
        sink_e = put("sink_e", [P, 4, NT])
        top8 = put("top8", [P, 8])
        w_idx = put("w_idx", [P, NT, HI])
        bf_col = put("bf_col", [P, 1])
        brow_d = [nc.dram_tensor(f"bias_rows{i}", [8, P, SPAN], f32, kind="Internal") for i in range(3)]

        bank = [ctx.enter_context(nc.psum_tensor(f"bank{i}", [P, T], f32)) for i in range(8)]
        FIRST = {BASE[n] + i: bank[3 + 2 * (i // 2) + (BASE[n] + i) % 2]
                 for n in stages if n != "final" for i in range(4 if kind(n) == "conv" else 2)}

        def result(c):
            return FIRST.get(c, bank[c % 2])

        STATB, OUT = bank[2], bank[7]
        HALF = [slice(0, T // 2), slice(T // 2, T)]
        STAT_HALF = [STATB[:, HALF[0]], OUT[:, HALF[1]]]
        EARLY_HALF = [bank[3], bank[4]]
        SCORES = [bank[0], bank[1], bank[3], bank[4]]
        DOTS = [bank[3], bank[4], bank[5], bank[6]]
        TURN = [bank[5], bank[6], bank[2]]

        raw_full = [sem("raw_full0"), sem("raw_full1")]
        hi_ready, lo_ready = sem("hi_ready"), sem("lo_ready")
        mm_done = sem("mm_done")
        bank_free = [sem("bank_free0"), sem("bank_free1")]
        consts, x_in, x_turned = sem("consts"), sem("x_in"), sem("x_turned")
        gains_in, rows_in, gains_turned, rows_turned, rows_out = (
            sem("gains_in"), sem("rows_in"), sem("gains_turned"), sem("rows_turned"), sem("rows_out"))
        small_in = sem("small_in")
        tab_mm, tab_row, tab_dram, tab_back = sem("tab_mm"), sem("tab_row"), sem("tab_dram"), sem("tab_back")
        ssq_ready, pool_step = sem("ssq_ready"), sem("pool_step")
        sq_ready, h_used = sem("sq_ready"), sem("h_used")
        sum_ready, rms_ready, rstd_ready = sem("sum_ready"), sem("rms_ready"), sem("rstd_ready")
        t_ready, hhi_ready, h_ready = sem("t_ready"), sem("hhi_ready"), sem("h_ready")
        x_done = sem("x_done")
        half_done, half_taken = sem("half_done"), sem("half_taken")
        sq_first, sum_first, rms_first, rstd_first = sem("sq_first"), sem("sum_first"), sem("rms_first"), sem("rstd_first")
        t_first, x_first, hhi_first, h_first = sem("t_first"), sem("x_first"), sem("hhi_first"), sem("h_first")
        silu_ready, gate_ready, prod_ready = sem("silu_ready"), sem("gate_ready"), sem("prod_ready")
        acthi_ready, act_ready = sem("acthi_ready"), sem("act_ready")
        gelu_ready, tap_ready, conv_step, conv_done = sem("gelu_ready"), sem("tap_ready"), sem("conv_step"), sem("conv_done")
        shifted = sem("shifted")
        idxw_turned, dots_ready, rel_ready, score_ready = (sem("idxw_turned"), sem("dots_ready"), sem("rel_ready"),
                                                           sem("score_ready"))
        score_masked, pen_ready, penb_ready = sem("score_masked"), sem("pen_ready"), sem("penb_ready")
        ckvn_ready, kvup_done, kv_ready = sem("ckvn_ready"), sem("kvup_done"), sem("kv_ready")
        vt_turned, vt_ready = sem("vt_turned"), sem("vt_ready")
        s_ready, s_biased, p_ready, sink_ready = sem("s_ready"), sem("s_biased"), sem("p_ready"), sem("sink_ready")
        sinkin_ready = sem("sinkin_ready")
        pn_ready, pt_turned = sem("pn_ready"), sem("pt_turned")
        pt_even, pt_odd, pv_done = sem("pt_even"), sem("pt_odd"), sem("pv_done")
        ohi_ready, o_ready, o_sq = sem("ohi_ready"), sem("o_ready"), sem("o_sq")
        recip_ready, first_ready, pl_ready = sem("recip_ready"), sem("first_ready"), sem("pl_ready")
        sub_sum, sub_out, sub_inv = sem("sub_sum"), sem("sub_out"), sem("sub_inv")
        sub_root, sub_norm = sem("sub_root"), sem("sub_norm")
        lam_ready, fg_one, fg_ready, decay_in = sem("lam_ready"), sem("fg_one"), sem("fg_ready"), sem("decay_in")
        fg_act = sem("fg_act")
        y_turned, y_out, stored = sem("y_turned"), sem("y_out"), sem("stored")
        dve_step = sem("dve_step")

        def wait_evacuated(eng, c, j=0):
            eng.wait_ge(bank_free[c % 2], XT_USES + c // 2 + 1 + j)

        assert T // 256 == 2

        def softmax_job(stage, n):
            if stage.startswith("mix"):
                if n < HA:
                    h, lo = n, HD * (n % 2)
                    keys_of = proj[:, KA, :] if h // (HA // 2) == h % 2 else k_swap
                    return dict(q=proj[lo:lo + HD, QA + h // 2, :], k=keys_of[lo:lo + HD, :], window=True,
                                bias=lambda i, h=h: bias_win[:, h, NEAR - (P if i == 0 else NEAR):NEAR])
                if n < HA + HB:
                    h = n - HA
                    lo = HD * (h % 2)
                    return dict(q=proj[lo:lo + HD, QB + h // 2, :], k=proj[lo:lo + HD, KB + h // 2, :], window=False,
                                bias=lambda i, h=h: bias_far[:, h, T - P * (i + 1):T])
                h = n - HA - HB
                lo = HD * (h % 2)
                return dict(q=proj[lo:lo + HD, QC + h // 2, :], k=k_sp[lo:lo + HD, :], window=False, sparse=h,
                            bias=lambda i, h=h: (bias_far[:, HB + h, T - P:T] if i == 0 else
                                                 pen_bias[h % 2][:, off(i):off(i + 1)]))
            if stage == "diff":
                h, lo = n // 2, HD * (n % 2)
                return dict(q=proj[lo:lo + HD, h, :], k=proj[lo:lo + HD, KT + h, :], window=False,
                            bias=lambda i, h=h: bias_diff[:, h, T - P * (i + 1):T])
            lo = HD * (n % 2)
            return dict(q=proj[lo:lo + HD, 2 * KT + n // 2, :], k=proj[lo:lo + HD, n // 2, :], window=False, decay=n,
                        bias=lambda i: causal[:, T - P * (i + 1):T])

        def keys(job, i):
            first = P * max(0, i - 1) if job["window"] else 0
            return first, P * (i + 1) - first

        def head_values(stage, v, b):
            if stage.startswith("mix"):
                if v < HA:
                    g = v // (HA // 2)
                    return v_win[:, b, HD * g:HD * (g + 1)]
                if v < HA + HB:
                    return v_blk[:, b, HD * (v - HA):HD * (v - HA + 1)]
                return v_sp[:, b, :]
            w = P if stage == "diff" else HD
            return v_all[:, b, w * v:w * (v + 1)]

        def act_turns(stage, v):
            return stage == "diff" or stage in MIX and v < HA

        def turned_width(stage, v, b):
            if stage in MIX and v < HA:
                return min(NEAR, T - P * b)
            return T - P * b

        gain_at, at = {}, 0
        for g in GAINS:
            for l in range(GAIN_ROWS.get(g, 1)):
                gain_at[g, l] = at
                at += KT

        def gain(name, l, k):
            return gains[:, gain_at[name, l] + k:gain_at[name, l] + k + 1]

        PRE_GAIN = {"ffn1_0": ("ffn1_norm", 0), "mix_0": ("mix_norm", 0), "ffn2_0": ("ffn2_norm", 0),
                    "ffn1_1": ("ffn1_norm", 1), "mix_1": ("mix_norm", 1), "ffn2_1": ("ffn2_norm", 1),
                    "final": ("final_norm", 0), "diff": ("a_norm_pre_2", 0), "conv_0": ("ffn_norm_pre_2", 0),
                    "fox": ("kv_norm_2", 0), "fox_q": ("b_norm_pre_2", 0), "conv_1": ("ffn_norm_pre_2", 1)}
        POST_GAIN = {"diff": ("a_norm_post_2", 0), "conv_0": ("ffn_norm_post_2", 0), "fox": ("b_norm_post_2", 0),
                     "conv_1": ("ffn_norm_post_2", 1)}
        N_ROWS = 2 + 3 * DEPTH
        N_SMALL = 11
        TABLES = [(table, onehot[1], HA), (table, onehot[0], 16), (table2, onehot[0], 8)]
        out_units = {n: BASE[n] + len(UNITS[kind(n)]) - KT for n in stages}

        BEFORE = {b: a for a, b in NEXT.items()} | {stages[0]: None}
        FOLLOW = {a: b for a, b in NEXT.items() if b not in CHAINED and b != "final"}
        LAST_USE = {n: (BASE["fox"] + 2 * KT if n == "fox_q" else out_units[BEFORE[n]] + KT - 1)
                    for n in USED if n != "fox_q" or "fox" in BASE}
        SQUARES = {n: (proj if n == "ffn1_0" else acc) for n in SQUARED}
        CONV_FF = {n: sum(FB for m in stages[:i] if kind(m) == "conv") for i, n in enumerate(stages)}

        def wait_x(eng, stage, k):
            if stage is None:
                eng.wait_ge(bank_free[k % 2], k // 2 + 1)
            elif stage in X_FIRST:
                eng.wait_ge(x_done, X_FIRST[stage] + k + 1)
            else:
                wait_evacuated(eng, out_units[stage] + k)

        FEW_AT = 4 * FB * 2 * DEPTH
        POOL_LOW = range(10, 18)

        block = ctx.enter_context(nc.Block())

        @block.sync
        def _(sp):
            def load(c, src, j=None):
                nk, cols = UNIT[c]
                if c >= 2:
                    sp.wait_ge(lo_ready, c - 1 if j is None else c - 1 + 2 * j)
                elif j is not None:
                    sp.wait_ge(lo_ready, c + 1 + 2 * (j - 1))
                sp.dma_start(raw[c % 2][:, 0:nk, 0:cols], src).then_inc(raw_full[c % 2], 16)

            def kview(w, l):
                return w[l].rearrange("(k p) n -> p k n", p=P)

            def ff(name, up_a, up_b, down):
                for hf in range(HALVES):
                    c = BASE[name] + 30 * hf
                    first = hf * FH * P
                    with sp.Fori(1 if c == 0 else 0, FH) as j:
                        for s, w in enumerate((up_a, up_b)):
                            load(c + s, w[:, :, DS(first + P * j, P)], j)
                    c += 2 * FH
                    with sp.Fori(0, KT // 2) as j:
                        for s in range(2):
                            load(c + s, down[:, hf * FH:(hf + 1) * FH, DS(2 * P * j + P * s, P)], j)

            def columns(c, w, n):
                with sp.Fori(0, n // 2) as j:
                    for s in range(2):
                        load(c + s, w[:, :, DS(P * s + 2 * P * j, P)], j)

            sp.dma_start(xtok[:, :, :], A["x"][0].rearrange("(t p) d -> p t d", p=P)).then_inc(x_in, 16)
            load(0, kview(A["ffn1_w_gate"], 0)[:, :, 0:P])
            load(1, kview(A["ffn1_w_up"], 0)[:, :, 0:P])
            for n, g in enumerate(GAINS):
                rows = GAIN_ROWS.get(g, 1) * KT
                src = A[g].rearrange("l (k p) -> (l k) p", p=P) if len(A[g].shape) == 2 else \
                    A[g].rearrange("(k p) -> k p", p=P)
                sp.dma_start(gain_rows[gain_at[g, 0]:gain_at[g, 0] + rows, :], src).then_inc(gains_in, 16)
            sp.dma_start(few_rows[0:DEPTH, :], A["kv_norm_c"]).then_inc(rows_in, 16)
            sp.dma_start(few_rows[DEPTH:DEPTH + 1, :], A["a_subln_2"]).then_inc(rows_in, 16)
            for l in range(DEPTH):
                taps = A["ffn_conv_w_2"][l].rearrange("c (j p) -> (c j) p", p=P)
                sp.dma_start(conv_rows[2 * l][0:4 * FB, :], taps[0:4 * FB, :]).then_inc(rows_in, 16)
                sp.dma_start(conv_rows[2 * l + 1][0:2 * FB, :], taps[4 * FB:6 * FB, :]).then_inc(rows_in, 16)
                sp.dma_start(conv_rows[2 * l + 1][2 * FB:4 * FB, :],
                              A["ffn_conv_b_2"][l].rearrange("(j p) -> j p", p=P)).then_inc(rows_in, 16)
            sp.dma_start(table[0:BUCKETS, :], A["rel_bias_table"]).then_inc(small_in, 16)
            sp.dma_start(table2[0:BUCKETS, :], A["rel_bias_2"]).then_inc(small_in, 16)
            sp.dma_start(onehot[0][:, :], A["onehot_causal"]).then_inc(small_in, 16)
            sp.dma_start(onehot[1][:, :], A["onehot_window"]).then_inc(small_in, 16)
            sp.dma_start(w_kvup[:, :, :], A["w_kv_up_c"].rearrange("l p n -> p l n")).then_inc(small_in, 16)
            sp.dma_start(sinks[:, :, :].rearrange("p l h -> p (l h)"),
                          A["attn_sinks"].rearrange("l h -> (l h)").partition_broadcast(P)).then_inc(small_in, 16)
            sp.dma_start(bf_col[FG_ROW:FG_ROW + 16, :],
                          A["b_f_2"].rearrange("(h a) -> h a", a=1)).then_inc(small_in, 16)
            for n, w in enumerate(("a_lam_q1_2", "a_lam_k1_2", "a_lam_q2_2", "a_lam_k2_2")):
                sp.dma_start(lam_in[:, n, :],
                              A[w].rearrange("l d -> (l d)").partition_broadcast(P)).then_inc(small_in, 16)

            for name in stages:
                l = int(name[-1]) if name[-1] in "01" else 0
                c = BASE[name]
                if kind(name) == "ffn":
                    w = name[:4]
                    ff(name, kview(A[w + "_w_gate"], l), kview(A[w + "_w_up"], l), kview(A[w + "_w_down"], l))
                elif kind(name) == "mix":
                    w = kview(A["w_in"], l)
                    for i, cb in enumerate(W_IN_ORDER[:4]):
                        load(c + i, w[:, :, P * cb:P * cb + UNIT[c + i][1]])
                    columns(c + 4, w, 14)
                    columns(c + 18, kview(A["w_out"], l), KT)
                elif kind(name) == "diff":
                    columns(c, kview(A["a_w_qkv_2"], 0), 3 * KT)
                    columns(c + 3 * KT, kview(A["a_w_o_2"], 0), KT)
                elif kind(name) == "fox":
                    w = A["w_kvf_2"].rearrange("(k p) n -> p k n", p=P)
                    load(c, w[:, :, D_KVF - FG_COLS:D_KVF])
                    columns(c + 1, w, 2 * KT)
                    columns(c + 1 + 2 * KT, kview(A["b_w_q_2"], 0), KT)
                    columns(c + 1 + 3 * KT, kview(A["b_w_o_2"], 0), KT)
                elif kind(name) == "conv":
                    w = kview(A["ffn_w_in_2"], l)
                    ff(name, w[:, :, 0:F], w[:, :, F:2 * F], kview(A["ffn_w_out_2"], l))
            for t in range(NT):
                sp.wait_ge(y_out, 2 * t + 2)
                sp.dma_start(out[0, P * t:P * (t + 1), :], ytok[:, t, :]).then_inc(stored, 16)
            sp.wait_ge(stored, 16 * NT)

        @block.gpsimd
        def _(pool):
            steps = [0]

            def chain(ins):
                steps[0] += 1
                ins.then_inc(pool_step, 1)
                pool.wait_ge(pool_step, steps[0])

            chain(nc.gpsimd.memset(ident[:, :], 0.0))
            chain(nc.gpsimd.affine_select(out=ident[:, :], in_=ident[:, :], compare_op=ALU.not_equal, fill=1.0,
                                          base=0, pattern=[[-1, P]], channel_multiplier=1))
            chain(nc.gpsimd.memset(ones[:, :], 1.0))
            chain(nc.gpsimd.memset(table[BUCKETS:BUCKETS + 1, :], 1.0))
            chain(nc.gpsimd.memset(table2[BUCKETS:BUCKETS + 1, :], 1.0))
            chain(nc.gpsimd.memset(eps_c[:, :], RMS_EPS))
            chain(nc.gpsimd.memset(sub_eps[:, :], SUBLN_EPS))
            nc.gpsimd.memset(mean_p[:, :], 1.0 / P).then_inc(consts, 1)

            def sum_squares(wait_block, src, n=KT):
                for k in range(n):
                    wait_block(k)
                    if k == 0:
                        chain(nc.gpsimd.tensor_tensor(ssq[:, :], src[:, k, :], src[:, k, :], ALU.mult))
                        continue
                    chain(nc.gpsimd.tensor_tensor(psq[:, :], src[:, k, :], src[:, k, :], ALU.mult))
                    add = nc.gpsimd.tensor_tensor(ssq[:, :], ssq[:, :], psq[:, :], ALU.add)
                    if k < n - 1:
                        chain(add)
                    else:
                        add.then_inc(ssq_ready, 1)

            def store_bias_rows():
                for r, (_, _, heads) in enumerate(TABLES):
                    pool.wait_ge(tab_row, 2 * r + 2)
                    rows = brow[r][heads - 8:heads, :].unsqueeze(1).broadcast_to((8, P, SPAN))
                    pool.dma_start(brow_d[r].ap(), rows).then_inc(tab_dram, 16)

            def spread_bias(dst, r, width):
                src = bass.AP(brow_d[r].ap().tensor, T - 1 - (width - P), [[SPAN - 1, P], [P * SPAN, 8], [1, width]])
                pool.dma_start(dst, src).then_inc(tab_back, 16)

            def normalise(stage, v):
                n = 2 * v if stage == "diff" else v
                job, g = softmax_job(stage, n), JOB[stage] + n
                ring = PROBS[kind(stage)]
                buf = ring[n % len(ring)]
                pool.wait_ge(recip_ready, HEAD[stage] + v + 1)
                for i in range(NT // 2):
                    tile = buf[:, off(i):off(i) + keys(job, i)[1]]
                    ins = nc.gpsimd.tensor_scalar(tile, tile, recip[:, g % 4, i:i + 1], None, ALU.mult)
                ins.then_inc(first_ready if stage == "diff" else pn_ready, 1)

            def select(h):
                if h == 0:
                    pool.wait_ge(pen_ready, 3 * (MIX[name] + 1))
                    pool.wait_ge(tab_back, 32)
                if h >= 2:
                    pool.wait_ge(s_biased, NT * (JOB[name] + HA + HB + h - 1))
                for i in range(1, NT):
                    nc.gpsimd.tensor_tensor(pen_bias[h % 2][:, off(i):off(i + 1)], bias_far[:, HB + h, T - P * (i + 1):T],
                                            score[:, off(i):off(i + 1)], ALU.add).then_inc(penb_ready, 1)

            store_bias_rows()
            before = None
            for name in stages:
                if name in POOL_SUM:
                    sum_squares(lambda k: wait_x(pool, before, k), xres)
                if name in MIX:
                    if MIX[name] == 0:
                        pool.wait_ge(tab_dram, 16 * len(TABLES))
                        spread_bias(bias_win[:, :, :], 0, NEAR)
                        spread_bias(bias_far[:, :, :], 1, T)
                    for i in range(1, NT):
                        pool.wait_ge(score_ready, 3 * MIX[name] + i)
                        own = score[:, off(i) + P * i:off(i + 1)]
                        nc.gpsimd.affine_select(out=own, in_=own, compare_op=ALU.is_ge, fill=MASKED, base=0,
                                                pattern=[[-1, P]], channel_multiplier=1).then_inc(score_masked, 1)
                    for i in POOL_LOW:
                        c = BASE[name] + i
                        pool.wait_ge(lo_ready, c)
                        pool.wait_ge(hi_ready, c + 1)
                        nc.gpsimd.tensor_tensor(w_lo[c % 2][:, 0:KT, :], raw[c % 2][:, 0:KT, :],
                                                w_hi[c % 2][:, 0:KT, :].bitcast(f32), ALU.subtract).then_inc(lo_ready, 1)
                    for v in range(N_HEADS[name]):
                        normalise(name, v)
                        if v in (9, 10, 12, 13):
                            select((9, 10, 12, 13).index(v))
                if name == "diff":
                    pool.wait_ge(tab_dram, 16 * len(TABLES))
                    if MIX:
                        pool.wait_ge(s_biased, NT * JOB[name])
                    spread_bias(bias_diff[:, :, :], 2, T)
                    for v in range(KT):
                        normalise(name, v)
                if name == "fox":
                    pool.wait_ge(o_ready, OUTB["fox"])
                    chain(nc.gpsimd.memset(causal[:, :], 0.0))
                    chain(nc.gpsimd.affine_select(out=causal[:, :], in_=causal[:, :], compare_op=ALU.is_ge,
                                                  fill=MASKED / SCALE, base=T - P, pattern=[[-1, T]],
                                                  channel_multiplier=1))
                    chain(nc.gpsimd.memset(decay_q[:, :, :].bitcast(f32), 1.0))
                    chain(nc.gpsimd.memset(decay_k[:, :, :].bitcast(f32), 1.0))
                    pool.wait_ge(fg_ready, 1)
                    for h in range(16):
                        row, col = 32 * (h % 4), h // 4
                        for n, part in enumerate(fparts):
                            to, r = (decay_q, row + n) if n < 2 else (decay_k, row + n)
                            pool.dma_start(to[r:r + 1, col, :],
                                           part[FG_ROW + h:FG_ROW + h + 1, :]).then_inc(decay_in, 16)
                    for v in range(N_HEADS[name]):
                        normalise(name, v)
                if name in CHAINED:
                    sum_squares(lambda k: wait_evacuated(pool, out_units[name] + k), acc, KT - 2)
                    for half, tok in enumerate(HALF):
                        for k in range(KT):
                            if half == 0:
                                pool.wait_ge(t_first, T_FIRST[name] + k + 1)
                            else:
                                pool.wait_ge(t_ready, T_FIRST[name] + k + 1)
                            nc.gpsimd.tensor_tensor(xres[:, k, tok], xres[:, k, tok], norm_t[k % 4][:, tok],
                                                    ALU.add).then_inc(x_done if half else x_first, 1)
                before = name

        @block.scalar
        def _(act):
            def hi(c, j=0, also=None):
                if c >= len(UNIT):
                    return
                nk, cols = UNIT[c]
                if also is not None:
                    act.wait_ge(*also)
                if c >= 2:
                    act.wait_ge(mm_done, c - 1 + 2 * j)
                act.wait_ge(raw_full[c % 2], 16 * (c // 2 + 1) + 16 * j)
                nc.scalar.activation(w_hi[c % 2][:, 0:nk, 0:cols], raw[c % 2][:, 0:nk, 0:cols],
                                     ACT.Copy).then_inc(hi_ready, 1)

            def root(name, n):
                nc.scalar.activation(spare[:, :], eps_c[:, :], ACT.Sqrt)
                if ROOT[name]:
                    act.wait_ge(rstd_ready, ROOT[name])
                act.wait_ge(sum_ready, STAT[name] + 1)
                nc.scalar.activation(rms[:, :], STATB[:, :], ACT.Sqrt, bias=eps_c[:, 0:1],
                                     scale=1.0 / n).then_inc(rms_ready, 1)

            def h_high(name, k):
                g, l = PRE_GAIN[name]
                if name != "fox_q":
                    wait_x(act, BEFORE[name], k)
                if name in USED:
                    if k < KT - 1:
                        act.wait_ge(h_used, USED[name] + k + 1)
                    else:
                        act.wait_ge(mm_done, LAST_USE[name] + 1)
                nc.scalar.activation(h_hi[:, k, :], xres[:, k, :], ACT.Copy, scale=gain(g, l, k)).then_inc(hhi_ready, 1)

            def half_input(name, k, half):
                g, l = PRE_GAIN[name]
                tok = HALF[half]
                if half == 0:
                    act.wait_ge(x_first, T_FIRST[BEFORE[name]] + k + 1)
                else:
                    wait_x(act, BEFORE[name], k)
                nc.scalar.activation(h_hi[:, k, tok], xres[:, k, tok], ACT.Copy,
                                     scale=gain(g, l, k)).then_inc(hhi_ready if half else hhi_first, 1)
                nc.scalar.activation(SQUARES[name][:, k, tok], xres[:, k, tok],
                                     ACT.Square).then_inc(sq_ready if half else sq_first, 1)

            def half_square(name, half, b):
                if half == 0:
                    act.wait_ge(half_taken, T_FIRST[name] // KT * 2 + b + 1)
                else:
                    wait_evacuated(act, out_units[name] + KT - 2 + b)
                nc.scalar.activation(sq_last[b][:, HALF[half]], acc[:, KT - 2 + b, HALF[half]],
                                     ACT.Square).then_inc(sq_ready if half else sq_first, 1)

            def half_root(event, n, half):
                if half == 0:
                    act.wait_ge(rstd_ready, ROOT[event])
                    act.wait_ge(sum_first, HALF_ROOT[event] + 1)
                else:
                    act.wait_ge(sum_ready, STAT[event] + 1)
                nc.scalar.activation(rms[:, HALF[half]], STAT_HALF[half], ACT.Sqrt, bias=eps_c[:, 0:1],
                                     scale=1.0 / n).then_inc(rms_ready if half else rms_first, 1)

            def finish(name):
                c = out_units[name] + KT
                nc.scalar.activation(spare[:, :], eps_c[:, :], ACT.Sqrt)
                half_square(name, 0, 0)
                half_square(name, 0, 1)
                hi(c)
                half_root("post_" + name, D, 0)
                half_square(name, 1, 0)
                hi(c + 1)
                half_square(name, 1, 1)
                following = NEXT.get(name)
                if following is None:
                    half_root("post_" + name, D, 1)
                    return
                for half in range(2):
                    for k in range(KT):
                        half_input(following, k, half)
                        if half == 0 and k == 2:
                            half_root("post_" + name, D, 1)
                        if half == 1 and k == 4:
                            half_root(following, D, 0)

            def squared_input(name):
                for k in range(KT):
                    h_high(name, k)
                    nc.scalar.activation(SQUARES[name][:, k, :], xres[:, k, :], ACT.Square).then_inc(sq_ready, 1)

            def act_high(jj):
                nc.scalar.activation(act_hi[:, DS(jj, 1), :], prod[:, :].rearrange("p (o n) -> p o n", o=1),
                                     ACT.Copy).then_inc(acthi_ready, 1)

            def down_parts(c, name, halves=False):
                with act.Fori(0, KT // 2 - 1) as j:
                    hi(c + 2, j)
                    hi(c + 3, j)
                if halves:
                    return
                hi(c + KT)
                follow = FOLLOW.get(name)
                if follow:
                    for k in range(KT - 1):
                        h_high(follow, k)
                hi(c + KT + 1)
                if follow:
                    h_high(follow, KT - 1)

            def gated_ff(name):
                for hf in range(HALVES):
                    c = BASE[name] + 30 * hf


                    def pair(j):
                        at, jj = (c + 2 * j, 0) if isinstance(j, int) else (c + 2, j - 1)
                        product = (bank_free[(c + 1) % 2], XT_USES + (c + 1) // 2 + 1 + j)
                        act.wait_ge(bank_free[c % 2], XT_USES + c // 2 + 1 + j)
                        nc.scalar.activation(gated[:, :], scaled_g[:, :], ACT.Silu).then_inc(silu_ready, 1)
                        if at in FIRST:
                            act.wait_ge(*product)
                        else:
                            hi(at + 2, jj)
                            hi(at + 3, jj, also=product)
                        act_high(j)

                    if hf == 0:
                        pair(0)
                    with act.Fori(1 - hf, FH - 1) as j:
                        pair(j)
                    pair(FH - 1)
                    down_parts(c + 2 * FH, name if hf else None)

            def conv_ff(name):
                l = int(name[-1])

                def tap(dst, src, ch):
                    nc.scalar.activation(dst[:, :], src[:, :], ACT.Identity, bias=conv[:, l, 3, DS(ch, 1)],
                                         scale=conv[:, l, 2, DS(ch, 1)]).then_inc(tap_ready, 1)

                for hf in range(HALVES):
                    c = BASE[name] + 30 * hf
                    cv = CV[name] + FH * hf

                    lead = 2 if hf == 0 else 1

                    def pair(j, first=False):
                        at, jj = (c + 2 * j, 0) if isinstance(j, int) else (c + 2 * lead, j - lead)
                        if not first:
                            act.wait_ge(prod_ready, cv + j)
                        made_g = (bank_free[c % 2], XT_USES + c // 2 + 1 + j)
                        made_v = (bank_free[(c + 1) % 2], XT_USES + (c + 1) // 2 + 1 + j)
                        early = at in FIRST
                        if early:
                            act.wait_ge(*made_g)
                        else:
                            hi(at + 2, jj, also=made_g)
                        if not first:
                            act_high(j - 1)
                        tap(tap_g, scaled_g, hf * FH + j)
                        if early and first:
                            hi(at + 4)
                        if early:
                            act.wait_ge(*made_v)
                        else:
                            hi(at + 3, jj, also=made_v)
                        tap(tap_v, scaled_v, FB + hf * FH + j)
                        act.wait_ge(conv_done, 2 * cv + 1 + 2 * j)
                        nc.scalar.activation(gated[:, :], tap_g[:, :], ACT.Gelu_apprx_tanh).then_inc(gelu_ready, 1)
                        if early and first:
                            hi(at + 5)

                    for j in range(lead):
                        pair(j, first=(j == 0))
                    with act.Fori(lead, FH - 1) as j:
                        pair(j)
                    pair(FH - 1)
                    act.wait_ge(prod_ready, cv + FH)
                    act_high(FH - 1)
                    down_parts(c + 2 * FH, None, halves=hf == 1)

            def turn_values(stage, groups):
                for g, dst in enumerate(groups):
                    act.wait_ge(vt_turned, VT_FIRST[stage] + g + 1)
                    w = dst.shape[2]
                    nc.scalar.activation(dst, TURN[g % 2][:, 0:NT * w].rearrange("p (b w) -> p b w", w=w),
                                         ACT.Copy).then_inc(vt_ready, 1)

            def exps(stage, n):
                job, g = softmax_job(stage, n), JOB[stage] + n
                ring = PROBS[kind(stage)]
                if n >= len(ring):
                    used = (n - len(ring)) // (2 if stage == "diff" else 1)
                    act.wait_ge(pt_turned, len(TURN_GROUPS) * (HEAD[stage] + used + 1))
                for i in range(NT):
                    w = keys(job, i)[1]
                    act.wait_ge(s_biased, NT * g + i + 1)
                    nc.scalar.activation(ring[n % len(ring)][:, off(i):off(i) + w], biased[:, off(i):off(i) + w], ACT.Exp,
                                         bias=nmax[:, g % 4, i:i + 1], scale=-1.0,
                                         accum_out=psum_r[:, g % 4, i:i + 1]).then_inc(p_ready, 1)
                if job["window"]:
                    act.wait_ge(sinkin_ready, HA * MIX[stage] + n + 1)
                    nc.scalar.activation(sink_e[:, g % 4, :], sink_e[:, g % 4, :], ACT.Exp).then_inc(sink_ready, 1)

            def probs_out(stage, v):
                g = HEAD[stage] + v
                for n, group in enumerate(TURN_GROUPS):
                    if n == 1 and not act_turns(stage, v):
                        continue
                    b = group[0]
                    w = turned_width(stage, v, b)
                    act.wait_ge(pt_turned, len(TURN_GROUPS) * g + n + 1)
                    if g:
                        act.wait_ge(pv_done, g)
                    if n == 1:
                        if stage == "diff":
                            nc.scalar.activation(probs_t[:, T:2 * T], TURN[1][:, :], ACT.Copy).then_inc(pt_odd, 1)
                            continue
                        nc.scalar.activation(probs_t[:, T:T + w], TURN[1][:, 0:w], ACT.Copy)
                        nc.scalar.activation(probs_t[:, 2 * T - P:2 * T], TURN[1][:, T - P:T], ACT.Copy).then_inc(pt_odd, 1)
                        continue
                    nc.scalar.activation(probs_t[:, SLOT_AT[b]:SLOT_AT[b] + w], TURN[n][:, 0:w],
                                         ACT.Copy).then_inc(pt_even, 1)

            def head_out(stage, v):
                g = HEAD[stage] + v
                if stage == "diff":
                    act.wait_ge(pv_done, g + 1)
                    nc.scalar.activation(proj[:, v, :], OUT[:, :], ACT.Copy)
                    nc.scalar.activation(proj[:, KT + v, :], OUT[:, :], ACT.Square).then_inc(o_sq, 1)
                elif v % 2:
                    act.wait_ge(pv_done, g + 1)
                    nc.scalar.activation(h_hi[:, v // 2, :], OUT[:, :], ACT.Copy).then_inc(ohi_ready, 1)

            def sub_mean(v):
                act.wait_ge(sub_sum, v + 1)
                nc.scalar.activation(proj[:, KT + v, :], OUT[:, :], ACT.Identity, bias=sub_eps[:, 0:1],
                                     scale=1.0).then_inc(sub_out, 1)

            def sub_sqrt(v):
                act.wait_ge(sub_inv, v + 1)
                nc.scalar.activation(proj[:, KT + v, :], proj[:, KT + v, :], ACT.Sqrt).then_inc(sub_root, 1)

            def sub_high(v):
                act.wait_ge(sub_norm, v + 1)
                nc.scalar.activation(h_hi[:, v, :], proj[:, 2 * KT + v, :], ACT.Copy).then_inc(ohi_ready, 1)

            def attention(stage):
                n = N_HEADS[stage]
                for m in range(2 if stage == "diff" else 3):
                    exps(stage, m)
                if stage == "diff":
                    for v in range(n):
                        if v + 1 < n:
                            exps(stage, 2 * v + 2)
                            exps(stage, 2 * v + 3)
                        if v:
                            sub_mean(v - 1)
                        probs_out(stage, v)
                        if v == n - 1:
                            for u in range(n - 2):
                                sub_sqrt(u)
                        head_out(stage, v)
                    sub_mean(n - 1)
                    sub_sqrt(n - 2)
                    for u in range(n - 1):
                        sub_high(u)
                    sub_sqrt(n - 1)
                    sub_high(n - 1)
                    return
                probs_out(stage, 0)
                for v in range(n):
                    if v + 3 < n:
                        exps(stage, v + 3)
                    if v + 1 < n:
                        probs_out(stage, v + 1)
                    head_out(stage, v)

            for k in range(0, KT, 2):
                act.wait_ge(x_turned, k + 1)
                nc.scalar.activation(xres[:, k, :], bank[0][:, :], ACT.Copy).then_inc(bank_free[0], 1)
            act.wait_ge(gains_turned, 1)
            nc.scalar.activation(gains[:, :], bank[5][:, 0:P], ACT.Copy).then_inc(rows_out, 1)
            act.wait_ge(rows_out, 1)
            hi(0)
            hi(1)
            squared_input(stages[0])

            def channel_rows():
                act.wait_ge(rows_turned, 1 + 2 * DEPTH)
                nc.scalar.activation(g_few[:, :], bank[7][:, FEW_AT:FEW_AT + DEPTH + 1], ACT.Copy).then_inc(rows_out, 1)
                for i in range(2 * DEPTH):
                    nc.scalar.activation(conv[:, i // 2, 2 * (i % 2):2 * (i % 2) + 2, :],
                                         bank[7][:, 4 * FB * i:4 * FB * (i + 1)].rearrange("p (c j) -> p c j", c=2),
                                         ACT.Copy).then_inc(rows_out, 1)
                for r, (_, _, heads) in enumerate(TABLES):
                    for a, w in ((0, T), (1, P)):
                        act.wait_ge(tab_mm, 2 * r + a + 1)
                        nc.scalar.activation(brow[r][0:heads, T * a:T * a + w], bank[5 + a][0:heads, 0:w],
                                             ACT.Copy).then_inc(tab_row, 1)
                act.wait_ge(lam_ready, 1)
                nc.scalar.activation(lam_e[:, :], lam_e[:, :], ACT.Exp).then_inc(lam_ready, 1)

            for name in stages:
                c = BASE[name]
                if name in CHAINED and name not in HALVED:
                    squared_input(name)
                if name == "final":
                    root(name, D)
                    continue
                hi(c + 2)
                if name in SQUARED:
                    hi(c + 3)
                if name in HALVED:
                    half_root(name, D, 1)
                else:
                    root(name, D)
                if name not in SQUARED:
                    hi(c + 3)
                if name == stages[0]:
                    channel_rows()
                if kind(name) == "ffn":
                    gated_ff(name)
                elif kind(name) == "mix":
                    l = MIX[name]
                    for i, cb in enumerate(W_IN_ORDER):
                        if i >= 2:
                            hi(c + i + 2)
                        if cb in (KI, KA):
                            wait_evacuated(act, c + i)
                            if cb == KA:
                                nc.scalar.activation(k_swap[0:HD, :], proj[HD:P, KA, :], ACT.Copy)
                            nc.scalar.activation((k_idx if cb == KI else k_swap)[HD:P, :], proj[0:HD, cb, :],
                                                 ACT.Copy).then_inc(shifted, 1)
                        if cb == CKV:
                            wait_evacuated(act, c + i)
                            nc.scalar.activation(sq[0][:, :], proj[:, CKV, :], ACT.Square).then_inc(sq_ready, 1)
                        if i in (3, 4, 5):
                            t = i - 2
                            w = P * (t + 1)
                            act.wait_ge(dots_ready, 3 * l + t)
                            if t > 1:
                                act.wait_ge(score_ready, 3 * l + t - 1)
                            for h in range(HI):
                                ins = nc.scalar.activation(rel[:, h, 0:w], DOTS[h][:, 0:w], ACT.Relu, scale=SCALE)
                            ins.then_inc(rel_ready, 1)
                        if i == 8:
                            root("ckv_" + name, P)
                        if i == 14:
                            act.wait_ge(kvup_done, l + 1)
                            nc.scalar.activation(k_sp[0:HD, :], OUT[0:HD, :], ACT.Copy)
                            nc.scalar.activation(k_sp[HD:P, :], OUT[0:HD, :], ACT.Copy)
                            nc.scalar.activation(v_sp_t[HD:P, :], OUT[HD:P, :], ACT.Copy).then_inc(kv_ready, 1)
                    turn_values(name, [v_win[:, :, :], v_blk[:, :, 0:P], v_blk[:, :, P:2 * P], v_sp[:, :, :]])
                    attention(name)
                    down_parts(c + 18, name)
                elif kind(name) == "diff":
                    for i in range(2, 3 * KT):
                        hi(c + i + 2)
                    turn_values(name, [v_all[:, :, P * g:P * (g + 1)] for g in range(KT)])
                    attention(name)
                    down_parts(c + 3 * KT, None, halves=True)
                elif kind(name) == "fox":
                    z, e, u, cq, ck = (t[FG_ROW:FG_ROW + 16, :] for t in fgate)
                    for i in range(1 + 3 * KT):
                        if i >= 2:
                            hi(c + i + 2)
                        if i == 4:
                            wait_evacuated(act, c)
                            nc.scalar.activation(z, z, ACT.Identity, bias=bf_col[FG_ROW:FG_ROW + 16, :],
                                                 scale=1.0).then_inc(fg_act, 1)
                            act.wait_ge(fg_act, 1)
                            nc.scalar.activation(e, z, ACT.Abs).then_inc(fg_act, 1)
                            act.wait_ge(fg_act, 2)
                            nc.scalar.activation(e, e, ACT.Exp, scale=-1.0).then_inc(fg_act, 1)
                        if i == 6:
                            act.wait_ge(fg_one, 1)
                            nc.scalar.activation(cq, u, ACT.Ln).then_inc(fg_act, 1)
                        if i == 2 * KT - 1:
                            for k in range(KT):
                                h_high("fox_q", k)
                    turn_values(name, [v_all[:, :, P * g:P * (g + 1)] for g in range(KT)])
                    attention(name)
                    down_parts(c + 1 + 3 * KT, None, halves=True)
                elif kind(name) == "conv":
                    conv_ff(name)
                if name in CHAINED:
                    finish(name)
            for t in range(NT):
                for a in range(2):
                    act.wait_ge(y_turned, 2 * t + a + 1)
                    nc.scalar.activation(ytok[:, t, T * a:T * (a + 1)], bank[3 + 2 * (t % 2) + a][:, :],
                                         ACT.Copy).then_inc(y_out, 1)

        @block.vector
        def _(dve):
            steps = [0]

            def mark(ins):
                steps[0] += 1
                ins.then_inc(dve_step, 1)
                return steps[0]

            def chain(ins):
                dve.wait_ge(dve_step, mark(ins))

            def lo(c, j=0):
                if c >= len(UNIT):
                    return
                nk, cols = UNIT[c]
                dve.wait_ge(hi_ready, c + 1 + 2 * j)
                nc.vector.tensor_tensor(w_lo[c % 2][:, 0:nk, 0:cols], raw[c % 2][:, 0:nk, 0:cols],
                                        w_hi[c % 2][:, 0:nk, 0:cols].bitcast(f32), ALU.subtract).then_inc(lo_ready, 1)

            def invert(name):
                dve.wait_ge(rms_ready, ROOT[name] + 1)
                dst = rstd if name in BASE else rstd2
                nc.vector.reciprocal(dst[:, :], rms[:, :]).then_inc(rstd_ready, 1)
                dve.wait_ge(rstd_ready, ROOT[name] + 1)

            def h_low(name, k):
                g, l = PRE_GAIN[name]
                dve.wait_ge(hhi_ready, KT * PRE[name] + k + 1)
                nc.vector.scalar_tensor_tensor(h_lo[:, k, :], xres[:, k, :], gain(g, l, k), h_hi[:, k, :].bitcast(f32),
                                               ALU.mult, ALU.subtract).then_inc(h_ready, 1)

            def half_low(name, k, half):
                g, l = PRE_GAIN[name]
                tok = HALF[half]
                if half == 0:
                    dve.wait_ge(hhi_first, T_FIRST[BEFORE[name]] + k + 1)
                else:
                    dve.wait_ge(hhi_ready, KT * PRE[name] + k + 1)
                nc.vector.scalar_tensor_tensor(h_lo[:, k, tok], xres[:, k, tok], gain(g, l, k), h_hi[:, k, tok].bitcast(f32),
                                               ALU.mult, ALU.subtract).then_inc(h_ready if half else h_first, 1)

            def half_take(name, how, half, b):
                c = out_units[name] + KT - 2 + b
                at = acc[:, KT - 2 + b, HALF[half]]
                if half == 0:
                    dve.wait_ge(half_done, T_FIRST[name] // KT * 2 + b + 1)
                    got = EARLY_HALF[b][:, HALF[0]]
                else:
                    dve.wait_ge(mm_done, c + 1)
                    got = bank[c % 2][:, HALF[1]]
                if how == "set":
                    ins = nc.vector.tensor_scalar(at, got, 1.0, None, ALU.mult)
                else:
                    ins = nc.vector.tensor_tensor(at, got, at, ALU.add)
                ins.then_inc(bank_free[c % 2] if half else half_taken, 1)

            def half_invert(event, half):
                dst = (rstd if event in BASE else rstd2)[:, HALF[half]]
                if half == 0:
                    dve.wait_ge(rms_first, HALF_ROOT[event] + 1)
                    nc.vector.reciprocal(dst, rms[:, HALF[0]]).then_inc(rstd_first, 1)
                    dve.wait_ge(rstd_first, HALF_ROOT[event] + 1)
                else:
                    dve.wait_ge(rms_ready, ROOT[event] + 1)
                    nc.vector.reciprocal(dst, rms[:, HALF[1]]).then_inc(rstd_ready, 1)
                    dve.wait_ge(rstd_ready, ROOT[event] + 1)

            def post(name, how):
                g, l = POST_GAIN[name]
                c = out_units[name] + KT
                half_take(name, how, 0, 0)
                half_take(name, how, 0, 1)
                half_take(name, how, 1, 0)
                lo(c)
                half_invert("post_" + name, 0)
                lag = 2
                for half, tok in enumerate(HALF):
                    for k in range(KT + lag):
                        if k < KT:
                            if k >= 4 and half == 0:
                                dve.wait_ge(x_first, T_FIRST[name] + k - 3)
                            elif k >= 4:
                                dve.wait_ge(x_done, X_FIRST[name] + k - 3)
                            nc.vector.scalar_tensor_tensor(norm_t[k % 4][:, tok], acc[:, k, tok], gain(g, l, k), rstd2[:, tok],
                                                           ALU.mult, ALU.mult).then_inc(t_ready if half else t_first, 1)
                        if half == 0 and k == 1:
                            half_take(name, how, 1, 1)
                            lo(c + 1)
                        if k >= lag and name in NEXT:
                            half_low(NEXT[name], k - lag, half)
                        if half == 0 and k == 5:
                            half_invert("post_" + name, 1)
                if name in NEXT:
                    half_invert(NEXT[name], 0)

            def divided(c, dst, j=0, rows=slice(0, P)):
                dve.wait_ge(mm_done, c + 1 + 2 * j)
                nc.vector.tensor_tensor(dst, result(c)[rows, :], rstd[rows, :], ALU.mult).then_inc(bank_free[c % 2], 1)

            def act_low(count, jj):
                dve.wait_ge(acthi_ready, count)
                nc.vector.tensor_tensor(act_lo[:, DS(jj, 1), :], prod[:, :].rearrange("p (o n) -> p o n", o=1),
                                        act_hi[:, DS(jj, 1), :].bitcast(f32), ALU.subtract).then_inc(act_ready, 1)

            def output_gemm(c, how, name, halves=False):
                def take(c, n, j=0):
                    b = c % 2
                    got = bank[b][:, :].rearrange("p (o n) -> p o n", o=1)
                    dve.wait_ge(mm_done, c + 1 + 2 * j)
                    if how == "half":
                        ins = nc.vector.scalar_tensor_tensor(xres[:, DS(n, 1), :], got, 0.5, xres[:, DS(n, 1), :],
                                                             ALU.mult, ALU.add)
                    elif how == "add":
                        ins = nc.vector.tensor_tensor(xres[:, DS(n, 1), :], got, xres[:, DS(n, 1), :], ALU.add)
                    elif how == "set":
                        ins = nc.vector.tensor_scalar(acc[:, DS(n, 1), :], got, 1.0, None, ALU.mult)
                    else:
                        ins = nc.vector.tensor_tensor(acc[:, DS(n, 1), :], got, acc[:, DS(n, 1), :], ALU.add)
                    ins.then_inc(bank_free[b], 1)

                with dve.Fori(0, KT // 2 - 1) as j:
                    for s in range(2):
                        take(c + s, 2 * j + s, j)
                        lo(c + 2 + s, j)
                if halves:
                    return
                follow = FOLLOW.get(name)
                take(c + KT - 2, KT - 2)
                lo(c + KT)
                if follow:
                    for k in range(KT - 1):
                        h_low(follow, k)
                take(c + KT - 1, KT - 1)
                if follow:
                    h_low(follow, KT - 1)
                lo(c + KT + 1)

            def gated_ff(name):
                for hf in range(HALVES):
                    c = BASE[name] + 30 * hf
                    a0 = FF[name] + FH * hf

                    def pair(j):
                        at, jj = (c + 2 * j, 0) if isinstance(j, int) else (c + 2, j - 1)
                        divided(at, scaled_g[:, :], jj)
                        if at not in FIRST:
                            lo(at + 2, jj)
                        dve.wait_ge(silu_ready, a0 - CONV_FF[name] + 1 + j)
                        nc.vector.tensor_tensor(gate_r[:, :], gated[:, :], rstd[:, :], ALU.mult).then_inc(gate_ready, 1)
                        dve.wait_ge(gate_ready, a0 - CONV_FF[name] + 1 + j)
                        dve.wait_ge(mm_done, c + 2 + 2 * j)
                        nc.vector.tensor_tensor(prod[:, :], gate_r[:, :], result(at + 1)[:, :],
                                                ALU.mult).then_inc(bank_free[(c + 1) % 2], 1)
                        if at not in FIRST:
                            lo(at + 3, jj)
                        act_low(a0 + 1 + j, j)

                    if hf == 0:
                        pair(0)
                    with dve.Fori(1 - hf, FH - 1) as j:
                        pair(j)
                    pair(FH - 1)
                    output_gemm(c + 2 * FH, "half", name if hf else None)

            def conv_ff(name):
                l = int(name[-1])
                for hf in range(HALVES):
                    c = BASE[name] + 30 * hf
                    a0, cv = FF[name] + FH * hf, CV[name] + FH * hf

                    def taps(dst, src, ch, count):
                        dve.wait_ge(tap_ready, count)
                        nc.vector.scalar_tensor_tensor(dst[:, 1:T], src[:, 0:T - 1], conv[:, l, 1, DS(ch, 1)],
                                                       dst[:, 1:T], ALU.mult, ALU.add).then_inc(conv_step, 1)
                        dve.wait_ge(conv_step, count)
                        nc.vector.scalar_tensor_tensor(dst[:, 2:T], src[:, 0:T - 2], conv[:, l, 0, DS(ch, 1)],
                                                       dst[:, 2:T], ALU.mult, ALU.add).then_inc(conv_done, 1)

                    lead = 2 if hf == 0 else 1

                    def pair(j, first=False):
                        at, jj = (c + 2 * j, 0) if isinstance(j, int) else (c + 2 * lead, j - lead)
                        early = at in FIRST
                        if not first:
                            dve.wait_ge(prod_ready, cv + j)
                        divided(at, scaled_g[:, :], jj)
                        if not early:
                            lo(at + 2, jj)
                        elif not first:
                            lo(at + 3)
                        if not first:
                            act_low(a0 + j, j - 1)
                        taps(tap_g, scaled_g, hf * FH + j, 2 * cv + 1 + 2 * j)
                        if early and first:
                            lo(at + 4)
                        divided(at + 1, scaled_v[:, :], jj)
                        if not early:
                            lo(at + 3, jj)
                        taps(tap_v, scaled_v, FB + hf * FH + j, 2 * cv + 2 + 2 * j)
                        dve.wait_ge(conv_done, 2 * cv + 2 + 2 * j)
                        if not first:
                            dve.wait_ge(act_ready, a0 + j)
                        dve.wait_ge(gelu_ready, cv + 1 + j)
                        nc.vector.tensor_tensor(prod[:, :], gated[:, :], tap_v[:, :], ALU.mult).then_inc(prod_ready, 1)

                    for j in range(lead):
                        pair(j, first=(j == 0))
                    with dve.Fori(lead, FH - 1) as j:
                        pair(j)
                    pair(FH - 1)
                    act_low(a0 + FH, FH - 1)
                    output_gemm(c + 2 * FH, "set" if hf == 0 else "sum", None, halves=hf == 1)

            def index_scores(name, t):
                l, w = MIX[name], P * (t + 1)
                dst = score[:, off(t):off(t + 1)]
                dve.wait_ge(rel_ready, 3 * l + t)
                chain(nc.vector.tensor_scalar(dst, rel[:, 0, 0:w], w_idx[:, t, 0:1], None, ALU.mult))
                for h in range(1, HI):
                    ins = nc.vector.scalar_tensor_tensor(dst, rel[:, h, 0:w], w_idx[:, t, h:h + 1], dst, ALU.mult, ALU.add)
                    if h < HI - 1:
                        chain(ins)
                ins.then_inc(score_ready, 1)

            EARLY_ROUNDS = 40
            LATE = 3 * (TOPK // 8) - EARLY_ROUNDS

            def topk_rounds(name, first, last):
                per = TOPK // 8
                for n in range(first, last):
                    t, r = 1 + n // per, n % per
                    tile = score[:, off(t):off(t + 1)]
                    if r == 0:
                        dve.wait_ge(score_masked, 3 * MIX[name] + t)
                    chain(nc.vector.max(top8[:, :], tile))
                    chain(nc.vector.match_replace(tile, top8[:, :], tile, TAKEN))
                    if r == per - 1:
                        nc.vector.tensor_scalar(tile, tile, TAKEN / 2, MASKED / SCALE, ALU.is_gt,
                                                ALU.mult).then_inc(pen_ready, 1)

            def bias_max(stage, n):
                job, g = softmax_job(stage, n), JOB[stage] + n
                if n == 0 and stage in MIX:
                    dve.wait_ge(tab_back, 32)
                if n == 0 and stage == "diff":
                    dve.wait_ge(tab_back, 16 * (3 if MIX else 1))
                for i in range(NT):
                    w = keys(job, i)[1]
                    if "sparse" in job and i:
                        dve.wait_ge(penb_ready, 12 * MIX[stage] + 3 * job["sparse"] + i)
                    if g:
                        dve.wait_ge(p_ready, NT * (g - 1) + i + 1)
                    dve.wait_ge(s_ready, NT * g + i + 1)
                    floor = nsinks[:, MIX[stage], n:n + 1] if job["window"] else -TAKEN
                    nc.vector.tensor_tensor_reduce(biased[:, off(i):off(i) + w], SCORES[i][:, 0:w], job["bias"](i), -SCALE,
                                                   floor, ALU.add, ALU.min, nmax[:, g % 4, i:i + 1]).then_inc(s_biased, 1)
                if job["window"]:
                    dve.wait_ge(s_biased, NT * (g + 1))
                    nc.vector.tensor_scalar(sink_e[:, g % 4, :], nmax[:, g % 4, :], sinks[:, MIX[stage], n:n + 1], None,
                                            ALU.add).then_inc(sinkin_ready, 1)

            def invert_sums(stage, v):
                if stage == "diff":
                    dve.wait_ge(p_ready, NT * (JOB[stage] + 2 * v + 1))
                    nc.vector.reciprocal(recip[:, 2 * (v % 2), :], psum_r[:, 2 * (v % 2), :]).then_inc(recip_ready, 1)
                    return
                job, g = softmax_job(stage, v), JOB[stage] + v
                dve.wait_ge(p_ready, NT * (g + 1))
                if job["window"]:
                    dve.wait_ge(sink_ready, HA * MIX[stage] + v + 1)
                    chain(nc.vector.tensor_tensor(psum_r[:, g % 4, :], psum_r[:, g % 4, :], sink_e[:, g % 4, :], ALU.add))
                nc.vector.reciprocal(recip[:, g % 4, :], psum_r[:, g % 4, :]).then_inc(recip_ready, 1)
                dve.wait_ge(recip_ready, HEAD[stage] + v + 1)
                later_tiles(stage, v).then_inc(pl_ready, 1)

            def later_tiles(stage, n):
                ring = PROBS[kind(stage)]
                for i in range(NT // 2, NT):
                    tile = ring[n % len(ring)][:, off(i):off(i) + keys(softmax_job(stage, n), i)[1]]
                    ins = nc.vector.tensor_scalar(tile, tile, recip[:, n % 4, i:i + 1], None, ALU.mult)
                return ins

            def difference(v):
                m = 2 * (v % 2)
                a, b = PROBS["diff"][m:m + 2]
                dve.wait_ge(p_ready, NT * (JOB["diff"] + 2 * v + 2))
                chain(nc.vector.reciprocal(recip[:, m + 1, :], psum_r[:, m + 1, :]))
                chain(nc.vector.tensor_scalar(recip[:, m + 1, :], recip[:, m + 1, :], nlam[:, 0:1], None, ALU.mult))
                chain(later_tiles("diff", 2 * v))
                dve.wait_ge(first_ready, v + 1)
                for i in range(NT):
                    ins = nc.vector.scalar_tensor_tensor(a[:, off(i):off(i + 1)], b[:, off(i):off(i + 1)],
                                                         recip[:, m + 1, i:i + 1], a[:, off(i):off(i + 1)], ALU.mult, ALU.add)
                ins.then_inc(pn_ready, 1)

            def probs_out(stage, v):
                if act_turns(stage, v):
                    return
                g = HEAD[stage] + v
                w1, w3 = (turned_width(stage, v, b) for b in TURN_GROUPS[1])
                dve.wait_ge(pt_turned, len(TURN_GROUPS) * g + 2)
                if g:
                    dve.wait_ge(pv_done, g)
                assert w1 + w3 == T
                nc.vector.tensor_copy(probs_t[:, T:2 * T], TURN[1][:, :]).then_inc(pt_odd, 1)

            def head_out(stage, v):
                if stage != "diff" and v % 2:
                    dve.wait_ge(ohi_ready, OUTB[stage] + v // 2 + 1)
                    nc.vector.tensor_tensor(h_lo[:, v // 2, :], OUT[:, :], h_hi[:, v // 2, :].bitcast(f32),
                                            ALU.subtract).then_inc(o_ready, 1)

            def sub_invert(v):
                dve.wait_ge(sub_out, v + 1)
                nc.vector.reciprocal(proj[:, KT + v, :], proj[:, KT + v, :]).then_inc(sub_inv, 1)

            def sub_normalise(v):
                dve.wait_ge(sub_root, v + 1)
                nc.vector.scalar_tensor_tensor(proj[:, 2 * KT + v, :], proj[:, v, :], g_sub, proj[:, KT + v, :],
                                               ALU.mult, ALU.mult).then_inc(sub_norm, 1)

            def sub_low(v):
                dve.wait_ge(ohi_ready, OUTB["diff"] + v + 1)
                nc.vector.tensor_tensor(h_lo[:, v, :], proj[:, 2 * KT + v, :], h_hi[:, v, :].bitcast(f32),
                                        ALU.subtract).then_inc(o_ready, 1)

            def attention(stage):
                n = N_HEADS[stage]
                bias_max(stage, 0)
                bias_max(stage, 1)
                invert_sums(stage, 0)
                if stage == "diff":
                    for v in range(n):
                        difference(v)
                        if v + 1 < n:
                            bias_max(stage, 2 * v + 2)
                            bias_max(stage, 2 * v + 3)
                            invert_sums(stage, v + 1)
                        probs_out(stage, v)
                        if v:
                            sub_invert(v - 1)
                    for u in range(n - 2):
                        sub_normalise(u)
                    sub_invert(n - 1)
                    sub_normalise(n - 2)
                    for u in range(n - 1):
                        sub_low(u)
                    sub_normalise(n - 1)
                    sub_low(n - 1)
                    return
                bias_max(stage, 2)
                invert_sums(stage, 1)
                probs_out(stage, 0)
                for v in range(n):
                    if v + 2 < n:
                        invert_sums(stage, v + 2)
                    if v + 3 < n:
                        bias_max(stage, v + 3)
                    if v + 1 < n:
                        probs_out(stage, v + 1)
                    head_out(stage, v)
                    if stage in MIX and v < HA:
                        topk_rounds(stage, EARLY_ROUNDS + LATE * v // HA, EARLY_ROUNDS + LATE * (v + 1) // HA)

            for k in range(1, KT, 2):
                dve.wait_ge(x_turned, k + 1)
                nc.vector.tensor_copy(xres[:, k, :], bank[1][:, :]).then_inc(bank_free[1], 1)
            lo(0)
            lo(1)
            for k in range(KT):
                h_low(stages[0], k)

            def small_values():
                dve.wait_ge(rows_out, 2 + 2 * DEPTH)
                dve.wait_ge(small_in, 16 * N_SMALL)
                chain(nc.vector.tensor_scalar(nsinks[:, :, :], sinks[:, :, :], -1.0, None, ALU.mult))
                chain(nc.vector.tensor_scalar(g_sub, g_sub, 1.0 - LAMBDA_INIT, None, ALU.mult))
                chain(nc.vector.tensor_tensor(lam_t[:, :, :], lam_in[:, 0:4:2, :], lam_in[:, 1:4:2, :], ALU.mult))
                nc.vector.reduce_sum(lam_e[:, :], lam_t[:, :, :], AX.X).then_inc(lam_ready, 1)

            def make_lambda():
                dve.wait_ge(lam_ready, 2)
                chain(nc.vector.tensor_tensor(nlam[:, :], lam_e[:, 1:2], lam_e[:, 0:1], ALU.subtract))
                chain(nc.vector.tensor_scalar(nlam[:, :], nlam[:, :], -LAMBDA_INIT, None, ALU.add))

            for name in stages:
                c = BASE[name]
                if name != "final":
                    lo(c + 2)
                    if name in SQUARED:
                        lo(c + 3)
                if name in HALVED:
                    half_invert(name, 1)
                else:
                    invert(name)
                if name != "final" and name not in SQUARED:
                    lo(c + 3)
                if name == "final":
                    for k in range(KT + 1):
                        if k < KT:
                            nc.vector.scalar_tensor_tensor(xres[:, k, :], xres[:, k, :], gain("final_norm", 0, k), rstd[:, :],
                                                           ALU.mult, ALU.mult).then_inc(x_done, 1)
                        if k and name in NEXT:
                            h_low(NEXT[name], k - 1)
                    continue
                if name == stages[0]:
                    small_values()
                if kind(name) == "ffn":
                    gated_ff(name)
                elif kind(name) == "mix":
                    l = MIX[name]
                    for i, cb in enumerate(W_IN_ORDER):
                        cols = slice(0, UNIT[c + i][1])
                        divided(c + i, proj[cols, cb, :], 0, cols)
                        if i >= 2 and i + 2 not in POOL_LOW:
                            if i + 1 in POOL_LOW:
                                dve.wait_ge(lo_ready, c + i + 2)
                            lo(c + i + 2)
                        if i == 4:
                            dve.wait_ge(idxw_turned, l + 1)
                            chain(nc.vector.tensor_scalar(w_idx[:, 1:NT, :],
                                                          OUT[:, 0:HI * (NT - 1)].rearrange("p (t h) -> p t h", h=HI),
                                                          HI ** -0.5, None, ALU.mult))
                        if i in (4, 5, 6):
                            index_scores(name, i - 3)
                        if i == 9:
                            invert("ckv_" + name)
                            nc.vector.scalar_tensor_tensor(ckv_n[:, :], proj[:, CKV, :], g_ckv[:, l:l + 1], rstd2[:, :],
                                                           ALU.mult, ALU.mult).then_inc(ckvn_ready, 1)
                        if 5 <= i < 17:
                            topk_rounds(name, EARLY_ROUNDS * (i - 5) // 12, EARLY_ROUNDS * (i - 4) // 12)
                    attention(name)
                    output_gemm(c + 18, "add", name)
                elif kind(name) == "diff":
                    make_lambda()
                    for i in range(3 * KT):
                        divided(c + i, proj[:, i, :])
                        if i >= 2:
                            lo(c + i + 2)
                    attention(name)
                    output_gemm(c + 3 * KT, "set", None, halves=True)
                elif kind(name) == "fox":
                    z, e, u, cq, ck = (t[FG_ROW:FG_ROW + 16, :] for t in fgate)
                    for i in range(1 + 3 * KT):
                        if i == 0:
                            gates = slice(FG_ROW, FG_ROW + 16)
                            divided(c, z, 0, gates)
                        else:
                            divided(c + i, proj[:, i - 1, :])
                        if i >= 2:
                            lo(c + i + 2)
                        if i == 5:
                            dve.wait_ge(fg_act, 3)
                            nc.vector.tensor_scalar(u, e, 1.0, None, ALU.add).then_inc(fg_one, 1)
                            dve.wait_ge(fg_one, 1)
                            chain(nc.vector.tensor_scalar(ck, u, -1.0, None, ALU.add))
                            chain(nc.vector.tensor_tensor(e, e, ck, ALU.subtract))
                        if i == 7:
                            dve.wait_ge(fg_act, 4)
                            chain(nc.vector.reciprocal(u, u))
                            chain(nc.vector.tensor_tensor(e, e, u, ALU.mult))
                            chain(nc.vector.tensor_tensor(e, e, cq, ALU.add))
                        if i == 9:
                            chain(nc.vector.scalar_tensor_tensor(z, z, 0.0, e, ALU.min, ALU.subtract))
                            chain(nc.vector.tensor_scalar(z, z, 1.0 / SCALE, None, ALU.mult))
                            chain(nc.vector.memset(u, 1.0))
                            chain(nc.vector.tensor_tensor_scan(cq, u, z, 0.0, ALU.mult, ALU.add))
                        if i == 11:
                            high, low, minus_high, minus_low = (t[FG_ROW:FG_ROW + 16, :] for t in fparts)
                            chain(nc.vector.tensor_copy(high, cq))
                            chain(nc.vector.tensor_tensor(low, cq, high.bitcast(f32), ALU.subtract))
                            chain(nc.vector.tensor_scalar(minus_high, high.bitcast(f32), -1.0, None, ALU.mult))
                            nc.vector.tensor_scalar(minus_low, low.bitcast(f32), -1.0, None, ALU.mult).then_inc(fg_ready, 1)
                        if i == 2 * KT - 1:
                            for k in range(KT):
                                h_low("fox_q", k)
                    attention(name)
                    output_gemm(c + 1 + 3 * KT, "set", None, halves=True)
                elif kind(name) == "conv":
                    conv_ff(name)
                if name in CHAINED:
                    post(name, "sum" if kind(name) == "conv" else "set")

        @block.tensor
        def _(pe):
            def gemm(c, x_hi, x_lo, ready, count, j=0, release=False):
                b = c % 2
                nk, cols = UNIT[c]
                pe.wait_ge(lo_ready, c + 1 + 2 * j)
                if c - 2 not in FIRST:
                    pe.wait_ge(bank_free[b], XT_USES + c // 2 + j)
                for k in range(nk):
                    pe.wait_ge(ready, count + k + 1)
                    for n, (w, x) in enumerate(((w_hi, x_hi), (w_hi, x_lo), (w_lo, x_hi))):
                        mm = nc.tensor.matmul(result(c)[0:cols, :], w[b][:, k, 0:cols], x[:, k, :],
                                              start=(k == 0 and n == 0), stop=(k == nk - 1 and n == 2))
                    if release and k < nk - 1:
                        mm.then_inc(h_used, 1)
                mm.then_inc(mm_done, 1)

            def gemm_both(c, count):
                for s in range(2):
                    pe.wait_ge(lo_ready, c + s + 1)
                    pe.wait_ge(bank_free[(c + s) % 2], XT_USES + (c + s) // 2)
                for k in range(KT):
                    pe.wait_ge(h_ready, count + k + 1)
                    for s in range(2):
                        b = (c + s) % 2
                        cols = UNIT[c + s][1]
                        for n, (w, x) in enumerate(((w_hi, h_hi), (w_hi, h_lo), (w_lo, h_hi))):
                            mm = nc.tensor.matmul(result(c + s)[0:cols, :], w[b][:, k, 0:cols], x[:, k, :],
                                                  start=(k == 0 and n == 0), stop=(k == KT - 1 and n == 2))
                        if k == KT - 1:
                            mm.then_inc(mm_done, 1)

            def gemm_two(c, x_hi, x_lo, ready, count):
                nk = UNIT[c][0]
                for s, blocks in ((0, range(nk - 1)), (1, range(nk // 2)), (0, [nk - 1]), (1, range(nk // 2, nk))):
                    u = c + s
                    if blocks[0] == 0:
                        pe.wait_ge(lo_ready, u + 1)
                        pe.wait_ge(bank_free[u % 2], XT_USES + u // 2)
                    for k in blocks:
                        pe.wait_ge(ready, count + k + 1)
                        for n, (w, x) in enumerate(((w_hi, x_hi), (w_hi, x_lo), (w_lo, x_hi))):
                            mm = nc.tensor.matmul(result(u)[:, :], w[u % 2][:, k, :], x[:, k, :],
                                                  start=(k == 0 and n == 0), stop=(k == nk - 1 and n == 2))
                    if blocks[-1] == nk - 1:
                        mm.then_inc(mm_done, 1)

            def gemm_halves(name, c, count):
                before = BEFORE[name]
                for s in range(2):
                    pe.wait_ge(lo_ready, c + s + 1)
                pe.wait_ge(half_taken, T_FIRST[before] // KT * 2 + 2)
                for half, tok in enumerate(HALF):
                    for k in range(KT):
                        if half == 0:
                            pe.wait_ge(h_first, T_FIRST[before] + k + 1)
                        else:
                            pe.wait_ge(h_ready, count + k + 1)
                        for s in range(2):
                            b = (c + s) % 2
                            cols = UNIT[c + s][1]
                            for n, (w, x) in enumerate(((w_hi, h_hi), (w_hi, h_lo), (w_lo, h_hi))):
                                mm = nc.tensor.matmul(result(c + s)[0:cols, tok], w[b][:, k, 0:cols], x[:, k, tok],
                                                      start=(k == 0 and n == 0), stop=(k == KT - 1 and n == 2))
                            if half and k == KT - 1:
                                mm.then_inc(mm_done, 1)
                    half_stat(name, half, [SQUARES[name][:, k, tok] for k in range(KT)])

            def half_stat(event, half, blocks):
                if half == 0:
                    stat_free(event)
                summed = event in POOL_SUM
                if summed:
                    if half == 0:
                        pe.wait_ge(ssq_ready, POOL_SUM[event] + 1)
                    nc.tensor.matmul(STAT_HALF[half], ones[:, :], ssq[:, HALF[half]], start=True, stop=False)
                for k, b in enumerate(blocks):
                    if half == 0:
                        pe.wait_ge(sq_first, HALF_SQ[event] + k + 1)
                    else:
                        pe.wait_ge(sq_ready, SQ_FIRST[event] + k + 1)
                    mm = nc.tensor.matmul(STAT_HALF[half], ones[:, :], b, start=(k == 0 and not summed),
                                          stop=(k == len(blocks) - 1))
                mm.then_inc(sum_ready if half else sum_first, 1)

            def finish(name, x_hi, x_lo, ready, count):
                c = out_units[name]
                nk = UNIT[c][0]
                if kind(name) in ("conv", "diff"):
                    gemm_two(c, x_hi, x_lo, ready, count)
                    gemm_pairs(c, KT - 2, x_hi, x_lo, ready, count, first=1)
                else:
                    gemm_pairs(c, KT - 2, x_hi, x_lo, ready, count)
                for half, tok in enumerate(HALF):
                    for s in range(2):
                        u = c + KT - 2 + s
                        if half == 0:
                            pe.wait_ge(lo_ready, u + 1)
                        else:
                            pe.wait_ge(bank_free[u % 2], XT_USES + u // 2)
                        dst = bank[u % 2][:, tok] if half else EARLY_HALF[s][:, tok]
                        for k in range(nk):
                            pe.wait_ge(ready, count + k + 1)
                            for n, (w, x) in enumerate(((w_hi, x_hi), (w_hi, x_lo), (w_lo, x_hi))):
                                mm = nc.tensor.matmul(dst, w[u % 2][:, k, :], x[:, k, tok],
                                                      start=(k == 0 and n == 0), stop=(k == nk - 1 and n == 2))
                        mm.then_inc(mm_done if half else half_done, 1)
                        if (half, s) == (1, 0):
                            half_stat("post_" + name, 0, [b[:, HALF[0]] for b in sq_last])
                half_stat("post_" + name, 1, [b[:, HALF[1]] for b in sq_last])

            def first_units(name, c, count):
                if name in SQUARED:
                    if name in HALVED:
                        gemm_halves(name, c, count)
                    else:
                        gemm_both(c, count)
                        stat_of_squares(name, [SQUARES[name][:, k, :] for k in range(KT)])
                else:
                    gemm(c, h_hi, h_lo, h_ready, count)
                    stat_of_sums(name)
                    gemm(c + 1, h_hi, h_lo, h_ready, count)

            def gemm_pairs(c, n, x_hi, x_lo, ready, count, first=0):
                with pe.Fori(first, n // 2) as j:
                    for s in range(2):
                        gemm(c + 2 * first + s, x_hi, x_lo, ready, count, j - first if first else j)

            def stat_free(name):
                if name in ROOT and ROOT[name]:
                    pe.wait_ge(rms_ready, ROOT[name])

            def stat_of_sums(name):
                stat_free(name)
                pe.wait_ge(ssq_ready, POOL_SUM[name] + 1)
                nc.tensor.matmul(STATB[:, :], ones[:, :], ssq[:, :], start=True, stop=True).then_inc(sum_ready, 1)

            def stat_of_squares(name, blocks):
                stat_free(name)
                for k, b in enumerate(blocks):
                    pe.wait_ge(sq_ready, SQ_FIRST[name] + k + 1)
                    mm = nc.tensor.matmul(STATB[:, :], ones[:, :], b, start=(k == 0), stop=(k == len(blocks) - 1))
                mm.then_inc(sum_ready, 1)

            def turn_values(stage, groups):
                for g, (src, width, rows) in enumerate(groups):
                    if g >= 2:
                        pe.wait_ge(vt_ready, VT_FIRST[stage] + g - 1)
                    for b in range(NT):
                        mm = nc.tensor.transpose(TURN[g % 2][:, width * b:width * (b + 1)], src[:, P * b:P * (b + 1)],
                                                 ident[rows, rows])
                    mm.then_inc(vt_turned, 1)
                pe.wait_ge(vt_ready, VT_FIRST[stage] + len(groups))

            def scores(stage, n):
                job, g = softmax_job(stage, n), JOB[stage] + n
                for i in range(NT):
                    first, w = keys(job, i)
                    if g:
                        pe.wait_ge(s_biased, NT * (g - 1) + i + 1)
                    mm = nc.tensor.matmul(SCORES[i][:, 0:w], job["q"][:, P * i:P * (i + 1)], job["k"][:, first:first + w],
                                          start=True, stop="decay" not in job)
                    if "decay" in job:
                        row, col = 32 * (job["decay"] % 4), job["decay"] // 4
                        mm = nc.tensor.matmul(SCORES[i][:, 0:w], decay_q[row:row + 4, col, P * i:P * (i + 1)],
                                              decay_k[row:row + 4, col, first:first + w], start=False, stop=True,
                                              tile_position=(row, 0))
                    mm.then_inc(s_ready, 1)

            def sub_sums(v):
                pe.wait_ge(o_sq, v + 1)
                nc.tensor.matmul(OUT[:, :], mean_p[:, :], proj[:, KT + v, :], start=True, stop=True).then_inc(sub_sum, 1)

            def turn(stage, v):
                g = HEAD[stage] + v
                n = 2 * v if stage == "diff" else v
                job = softmax_job(stage, n)
                ring = PROBS[kind(stage)]
                src = ring[n % len(ring)]
                pe.wait_ge(pn_ready, g + 1)
                if stage != "diff":
                    pe.wait_ge(pl_ready, PL_FIRST[stage] + v + 1)
                if g:
                    pe.wait_ge(pt_even, 2 * g)
                    pe.wait_ge(pt_odd, g)
                for bank_t, blocks in zip(TURN, TURN_GROUPS):
                    for b in blocks:
                        last = min(b + 1, NT - 1) if job["window"] else NT - 1
                        for i in range(b, last + 1):
                            col, to = off(i) + P * b - keys(job, i)[0], TURN_AT[b] + P * (i - b)
                            mm = nc.tensor.transpose(bank_t[:, to:to + P], src[:, col:col + P], ident[:, :])
                    mm.then_inc(pt_turned, 1)

            def values(stage, v):
                g = HEAD[stage] + v
                window = softmax_job(stage, 2 * v if stage == "diff" else v)["window"]
                rows = slice(0, P) if stage == "diff" else slice(HD * (v % 2), HD * (v % 2) + HD)
                if stage == "diff":
                    if v:
                        pe.wait_ge(sub_out, v)
                elif v % 2 == 0 and v:
                    pe.wait_ge(o_ready, OUTB[stage] + v // 2)
                pe.wait_ge(pt_even, 2 * g + 2)
                pe.wait_ge(pt_odd, g + 1)
                for b in range(NT):
                    at = SLOT_AT[b]
                    if window:
                        cols = slice(P * b, P * (b + 1))
                        if b:
                            before = SLOT_AT[b - 1] + P
                            nc.tensor.matmul(OUT[rows, cols], head_values(stage, v, b - 1), probs_t[:, before:before + P],
                                             start=True, stop=False)
                        mm = nc.tensor.matmul(OUT[rows, cols], head_values(stage, v, b), probs_t[:, at:at + P],
                                              start=(b == 0), stop=True)
                    else:
                        mm = nc.tensor.matmul(OUT[rows, P * b:T], head_values(stage, v, b), probs_t[:, at:at + T - P * b],
                                              start=(b == 0), stop=(b == NT - 1))
                mm.then_inc(pv_done, 1)

            def attention(stage):
                n = N_HEADS[stage]
                for m in range(2 if stage == "diff" else 3):
                    scores(stage, m)
                if stage == "diff":
                    for v in range(n):
                        if v + 1 < n:
                            scores(stage, 2 * v + 2)
                            scores(stage, 2 * v + 3)
                        if v:
                            sub_sums(v - 1)
                        turn(stage, v)
                        values(stage, v)
                    sub_sums(n - 1)
                    return
                turn(stage, 0)
                for v in range(n):
                    if v + 3 < n:
                        scores(stage, v + 3)
                    if v + 1 < n:
                        turn(stage, v + 1)
                    values(stage, v)

            pe.wait_ge(consts, 1)
            pe.wait_ge(x_in, 16)
            for k in range(KT):
                if k >= 2:
                    pe.wait_ge(bank_free[k % 2], k // 2)
                for t in range(NT):
                    mm = nc.tensor.transpose(bank[k % 2][:, P * t:P * (t + 1)], xtok[:, t, P * k:P * (k + 1)], ident[:, :])
                mm.then_inc(x_turned, 1)
            pe.wait_ge(gains_in, 16 * len(GAINS))
            nc.tensor.transpose(bank[5][:, 0:P], gain_rows[:, :], ident[:, :]).then_inc(gains_turned, 1)

            def channel_rows():
                pe.wait_ge(rows_in, 16 * N_ROWS)
                pe.wait_ge(rows_out, 1)
                nc.tensor.transpose(bank[7][:, FEW_AT:FEW_AT + DEPTH + 1], few_rows[:, :],
                                    ident[0:DEPTH + 1, 0:DEPTH + 1]).then_inc(rows_turned, 1)
                for i in range(2 * DEPTH):
                    nc.tensor.transpose(bank[7][:, 4 * FB * i:4 * FB * (i + 1)], conv_rows[i][:, :],
                                        ident[0:4 * FB, 0:4 * FB]).then_inc(rows_turned, 1)
                pe.wait_ge(small_in, 16 * N_SMALL)
                for r, (tab, hot, heads) in enumerate(TABLES):
                    if r:
                        pe.wait_ge(tab_row, 2 * r)
                    for a, w in ((0, T), (1, P)):
                        nc.tensor.matmul(bank[5 + a][0:heads, 0:w], tab[:, 0:heads], hot[:, T * a:T * a + w],
                                         start=True, stop=True).then_inc(tab_mm, 1)

            for name in stages:
                c = BASE[name]
                if name == "final":
                    stat_of_sums(name)
                    continue
                h0 = KT * PRE[name]
                if kind(name) in ("ffn", "conv"):
                    for hf in range(HALVES):
                        if hf == 0:
                            first_units(name, c, h0)
                            if name == stages[0]:
                                channel_rows()
                            gemm(c + 2, h_hi, h_lo, h_ready, h0)
                            gemm(c + 3, h_hi, h_lo, h_ready, h0)
                            if kind(name) == "conv":
                                gemm(c + 4, h_hi, h_lo, h_ready, h0)
                                gemm(c + 5, h_hi, h_lo, h_ready, h0)
                        first = 0 if hf else 3 if kind(name) == "conv" else 2
                        gemm_pairs(c + 30 * hf, 2 * FH, h_hi, h_lo, h_ready, h0, first=first)
                        if hf and name in CHAINED:
                            finish(name, act_hi, act_lo, act_ready, FF[name] + FH * hf)
                        elif kind(name) == "conv":
                            gemm_two(c + 2 * FH, act_hi, act_lo, act_ready, FF[name] + FH * hf)
                            gemm_pairs(c + 2 * FH, KT, act_hi, act_lo, act_ready, FF[name] + FH * hf, first=1)
                        else:
                            gemm_pairs(c + 30 * hf + 2 * FH, KT, act_hi, act_lo, act_ready, FF[name] + FH * hf)
                elif kind(name) == "mix":
                    l = MIX[name]
                    first_units(name, c, h0)
                    for i in range(2, 8):
                        gemm(c + i, h_hi, h_lo, h_ready, h0)
                        if i == 3:
                            wait_evacuated(pe, c)
                            pe.wait_ge(shifted, 2 * l + 1)
                            for t in range(1, NT):
                                mm = nc.tensor.transpose(OUT[:, HI * (t - 1):HI * t], proj[HD:KI_COLS, KI, P * t:P * (t + 1)],
                                                         ident[HD:KI_COLS, HD:KI_COLS])
                            mm.then_inc(idxw_turned, 1)
                            wait_evacuated(pe, c + 2)
                        if 3 <= i <= 5:
                            t = i - 2
                            w = P * (t + 1)
                            if t > 1:
                                pe.wait_ge(rel_ready, 3 * l + t - 1)
                            for h in range(HI):
                                r = HD * (h % 2)
                                mm = nc.tensor.matmul(DOTS[h][:, 0:w], proj[r:r + HD, QI + h // 2, P * t:P * (t + 1)],
                                                      proj[0:HD, KI, 0:w] if r == 0 else k_idx[HD:P, 0:w],
                                                      start=True, stop=True)
                            mm.then_inc(dots_ready, 1)
                    stat_of_squares("ckv_" + name, [sq[0][:, :]])
                    gemm_pairs(c + 8, 6, h_hi, h_lo, h_ready, h0)
                    pe.wait_ge(ckvn_ready, l + 1)
                    pe.wait_ge(score_ready, 3 * l + 1)
                    nc.tensor.matmul(OUT[:, :], w_kvup[:, l, :], ckv_n[:, :], start=True, stop=True).then_inc(kvup_done, 1)
                    gemm_pairs(c + 14, 4, h_hi, h_lo, h_ready, h0)
                    wait_evacuated(pe, c + 16)
                    wait_evacuated(pe, c + 17)
                    pe.wait_ge(shifted, 2 * l + 2)
                    pe.wait_ge(kv_ready, l + 1)
                    every = slice(0, P)
                    turn_values(name, [(proj[:, VA, :], P, every), (proj[:, VB, :], P, every), (proj[:, VB + 1, :], P, every),
                                       (v_sp_t[HD:P, :], HD, slice(HD, P))])
                    attention(name)
                    gemm_pairs(c + 18, KT - 2, h_hi, h_lo, o_ready, OUTB[name])
                    gemm(c + 16 + KT, h_hi, h_lo, o_ready, OUTB[name])
                    gemm(c + 17 + KT, h_hi, h_lo, o_ready, OUTB[name], release=True)
                elif kind(name) == "diff":
                    first_units(name, c, h0)
                    gemm(c + 2, h_hi, h_lo, h_ready, h0)
                    gemm(c + 3, h_hi, h_lo, h_ready, h0)
                    gemm_pairs(c, 3 * KT, h_hi, h_lo, h_ready, h0, first=2)
                    wait_evacuated(pe, c + 3 * KT - 2)
                    wait_evacuated(pe, c + 3 * KT - 1)
                    turn_values(name, [(proj[:, 2 * KT + g, :], P, slice(0, P)) for g in range(KT)])
                    attention(name)
                    finish(name, h_hi, h_lo, o_ready, OUTB[name])
                elif kind(name) == "fox":
                    first_units(name, c, h0)
                    gemm(c + 2, h_hi, h_lo, h_ready, h0)
                    gemm(c + 3, h_hi, h_lo, h_ready, h0)
                    gemm_pairs(c + 4, 2 * KT - 4, h_hi, h_lo, h_ready, h0)
                    gemm(c + 2 * KT, h_hi, h_lo, h_ready, h0, release=True)
                    gemm_pairs(c + 1 + 2 * KT, KT, h_hi, h_lo, h_ready, KT * PRE["fox_q"])
                    wait_evacuated(pe, c + 3 * KT - 1)
                    wait_evacuated(pe, c + 3 * KT)
                    turn_values(name, [(proj[:, KT + g, :], P, slice(0, P)) for g in range(KT)])
                    pe.wait_ge(decay_in, 16 * 64)
                    attention(name)
                    finish(name, h_hi, h_lo, o_ready, OUTB[name])
            for t in range(NT):
                for a in range(2):
                    if t >= 2:
                        pe.wait_ge(y_out, 2 * (t - 2) + a + 1)
                    for k in range(4 * a, 4 * a + 4):
                        if stages[-1] in CHAINED and t < NT // 2:
                            pe.wait_ge(x_first, T_FIRST[stages[-1]] + k + 1)
                        else:
                            wait_x(pe, stages[-1], k)
                        mm = nc.tensor.transpose(bank[3 + 2 * (t % 2) + a][:, P * (k % 4):P * (k % 4 + 1)],
                                                 xres[:, k, P * t:P * (t + 1)], ident[:, :])
                    mm.then_inc(y_turned, 1)


_INS = ["x", "rel_bias_table", "ffn1_norm", "ffn1_w_gate", "ffn1_w_up", "ffn1_w_down", "mix_norm", "w_in", "attn_sinks",
        "kv_norm_c", "w_kv_up_c", "w_out", "ffn2_norm", "ffn2_w_gate", "ffn2_w_up", "ffn2_w_down", "final_norm",
        "rel_bias_2", "a_norm_pre_2", "a_norm_post_2", "a_w_qkv_2", "a_lam_q1_2", "a_lam_k1_2", "a_lam_q2_2",
        "a_lam_k2_2", "a_subln_2", "a_w_o_2", "kv_norm_2", "w_kvf_2", "b_f_2", "b_norm_pre_2", "b_norm_post_2",
        "b_w_q_2", "b_w_o_2", "ffn_norm_pre_2", "ffn_norm_post_2", "ffn_w_in_2", "ffn_conv_w_2", "ffn_conv_b_2",
        "ffn_w_out_2"]


def kernel(**inputs):
    import concourse.bacc as bacc
    from concourse.bass_utils import run_bass_kernel_spmd

    nc = bacc.Bacc("TRN2", target_bir_lowering=False, num_devices=1)
    inputs = dict(inputs, onehot_causal=t5_onehot(T), onehot_window=t5_onehot(WINDOW))
    arrays, aps = {}, {}
    for name in _INS + ["onehot_causal", "onehot_window"]:
        a = np.ascontiguousarray(inputs[name])
        arrays[f"in_{name}_dram"] = a
        aps[name] = nc.dram_tensor(f"in_{name}_dram", a.shape, mybir.dt.from_np(a.dtype), kind="ExternalInput").ap()
    out = nc.dram_tensor("out_0_dram", (1, T, D), mybir.dt.float32, kind="ExternalOutput").ap()
    program(nc, aps, out, ALL_STAGES)
    r = run_bass_kernel_spmd(nc, [arrays], core_ids=[0])
    return r.results[0]["out_0_dram"]
```
